# Optimizing a Trainium2 kernel written in Bass

```python
import jax, jax.numpy as jnp
from jax import lax
import numpy as np
import math

D_MODEL = 1024
BATCH = 1
SEQ = 256
DEPTH = 1

HEAD_DIM = 64
RWKV_HEADS = D_MODEL // HEAD_DIM
RWKV_WIDTH = RWKV_HEADS * HEAD_DIM
DECAY_LORA = 64
AAA_LORA = 64
GATE_LORA = 160
RWKV_COLS = 3 * RWKV_WIDTH + DECAY_LORA + AAA_LORA + GATE_LORA
GN_EPS = 64e-5
ATTN_PAIRS = ((128, 1), (512, 4), (2048, 16))
ATTN_GROUPS = 3
ATTN_HEADS_PER_GROUP = 4
ATTN_HEADS = ATTN_GROUPS * ATTN_HEADS_PER_GROUP
ATTN_WIDTH = ATTN_HEADS * HEAD_DIM
N_BRANCHES = 2
IN_COLS = RWKV_COLS + 3 * ATTN_WIDTH + N_BRANCHES * D_MODEL
D_FF = 2816
RMS_EPS = 1e-6
NEG_INF = -1e30


def _split_last(t, sizes):
    out, start = [], 0
    for n in sizes:
        out.append(t[..., start:start + n])
        start += n
    return out

def rms_norm(x, g):
    xf = x.astype(jnp.float32)
    y = xf * lax.rsqrt(jnp.mean(xf * xf, axis=-1, keepdims=True) + RMS_EPS)
    return y.astype(x.dtype) * g

def swiglu(h, w_in, w_out):
    gate, up = _split_last(h @ w_in, (D_FF, D_FF))
    return (jax.nn.silu(gate) * up) @ w_out

def token_shift(p, mu):
    prev = jnp.pad(p, ((0, 0), (1, 0), (0, 0)))[:, :-1]
    return p + (prev - p) * mu

def wkv7_scan(r, w, k, v, a, b):
    B, S, H, N = r.shape
    to_time = lambda t: jnp.moveaxis(t, 1, 0)

    def step(state, inp):
        r_t, w_t, k_t, v_t, a_t, b_t = inp
        sa = jnp.einsum('bhvk,bhk->bhv', state, a_t)
        state = (state * w_t[:, :, None, :] + sa[..., None] * b_t[:, :, None, :]
                 + v_t[..., None] * k_t[:, :, None, :])
        return state, jnp.einsum('bhvk,bhk->bhv', state, r_t)

    state0 = jnp.zeros((B, H, N, N), jnp.float32)
    _, out = lax.scan(step, state0, (to_time(r), to_time(w), to_time(k),
                                      to_time(v), to_time(a), to_time(b)))
    return jnp.moveaxis(out, 0, 1)

def rwkv7_time_mix(p, mu, w0, w2, a0, a2, g2, k_k, k_a, r_k, ln_w, ln_b):
    B, S, _ = p.shape
    H, N = RWKV_HEADS, HEAD_DIM
    p = token_shift(p.astype(jnp.float32), mu)
    r, k, v, wd, ad, gd = _split_last(
        p, (RWKV_WIDTH, RWKV_WIDTH, RWKV_WIDTH, DECAY_LORA, AAA_LORA, GATE_LORA))
    w = -jax.nn.softplus(-(w0 + jnp.tanh(wd) @ w2)) - 0.5
    decay = jnp.exp(-jnp.exp(w))
    a = jax.nn.sigmoid(a0 + ad @ a2)
    g = jax.nn.sigmoid(gd) @ g2
    heads = lambda t: t.reshape(B, S, H, N)
    kk = heads(k * k_k)
    kk = kk / jnp.maximum(jnp.sqrt(jnp.sum(kk * kk, axis=-1, keepdims=True)), 1e-12)
    k = k * (1.0 + (a - 1.0) * k_a)
    rh, kh, vh, ah = heads(r), heads(k), heads(v), heads(a)
    wkv = wkv7_scan(rh, heads(decay), kh, vh, -kk, kk * ah)
    mean = jnp.mean(wkv, axis=-1, keepdims=True)
    var = jnp.mean(jnp.square(wkv - mean), axis=-1, keepdims=True)
    y = ((wkv - mean) * lax.rsqrt(var + GN_EPS)).reshape(B, S, RWKV_WIDTH) * ln_w + ln_b
    bonus = jnp.sum(rh * kh * r_k, axis=-1, keepdims=True) * vh
    return (y + bonus.reshape(B, S, RWKV_WIDTH)) * g

def dilated_group_attention(q, k, v, window, dilation):
    B, S, Hg, E = q.shape
    span = window // dilation
    blk = span
    sub = S // dilation
    nb = -(-sub // blk)
    pad = nb * blk - sub

    def to_sub(t):
        t = t.reshape(B, sub, dilation, Hg, E).transpose(0, 2, 1, 3, 4)
        t = jnp.pad(t, ((0, 0), (0, 0), (0, pad), (0, 0), (0, 0)))
        return t.reshape(B, dilation, nb, blk, Hg, E)

    def with_prev(t):
        tp = jnp.pad(t, ((0, 0), (0, 0), (1, 0), (0, 0), (0, 0), (0, 0)))
        return jnp.concatenate([tp[:, :, :-1], tp[:, :, 1:]], axis=3)

    qb = to_sub(q)
    kw, vw = with_prev(to_sub(k)), with_prev(to_sub(v))
    s = jnp.einsum('bdnqhe,bdnkhe->bdnhqk', qb, kw)
    qi = jnp.arange(blk)[:, None]
    kj = jnp.arange(2 * blk)[None, :]
    dist = qi + blk - kj
    bidx = jnp.arange(nb)[:, None, None]
    valid = (dist >= 0) & (dist <= span) & (bidx * blk + kj - blk >= 0)
    s = jnp.where(valid[None, None, :, None], s, NEG_INF)
    m = jnp.max(s, axis=-1, keepdims=True)
    pexp = jnp.exp(s - m)
    den = jnp.sum(pexp, axis=-1, keepdims=True)
    o = jnp.einsum('bdnhqk,bdnkhe->bdnqhe', pexp / den, vw)
    lse = (m + jnp.log(den))[..., 0].transpose(0, 1, 2, 4, 3)
    o = o.reshape(B, dilation, nb * blk, Hg, E)[:, :, :sub]
    o = o.transpose(0, 2, 1, 3, 4).reshape(B, S, Hg, E)
    lse = lse.reshape(B, dilation, nb * blk, Hg)[:, :, :sub]
    lse = lse.transpose(0, 2, 1, 3).reshape(B, S, Hg)
    return o, lse

def dilated_attention(pq, pk, pv, q_gain, k_gain):
    B, S, _ = pq.shape
    heads = lambda t: t.astype(jnp.float32).reshape(B, S, ATTN_HEADS, HEAD_DIM)
    q = rms_norm(heads(pq), q_gain) * (HEAD_DIM ** -0.5)
    k = rms_norm(heads(pk), k_gain)
    v = heads(pv)
    outs, lses = [], []
    for gi, (window, dilation) in enumerate(ATTN_PAIRS):
        sl = slice(gi * ATTN_HEADS_PER_GROUP, (gi + 1) * ATTN_HEADS_PER_GROUP)
        o, lse = dilated_group_attention(q[:, :, sl], k[:, :, sl], v[:, :, sl], window, dilation)
        outs.append(o)
        lses.append(lse)
    o = jnp.stack(outs, axis=2)
    alpha = jax.nn.softmax(jnp.stack(lses, axis=2), axis=2)
    return (o * alpha[..., None]).reshape(B, S, ATTN_WIDTH)

def first_inputs(seed: int = 0) -> dict:
    key = jax.random.key(seed)
    ks = jax.random.split(key, 27)
    f32 = jnp.float32
    L, D = DEPTH, D_MODEL

    def nrm(k, shape, scale):
        return scale * jax.random.normal(k, shape, f32)

    def gain(k, shape):
        return 1.0 + 0.1 * jax.random.normal(k, shape, f32)

    return {
        'x': jax.random.normal(ks[0], (BATCH, SEQ, D), f32),
        'ffn1_norm': gain(ks[1], (L, D)),
        'ffn1_w_in': nrm(ks[2], (L, D, 2 * D_FF), D ** -0.5),
        'ffn1_w_out': nrm(ks[3], (L, D_FF, D), D_FF ** -0.5),
        'mix_norm': gain(ks[4], (L, D)),
        'w_in': nrm(ks[5], (L, D, IN_COLS), D ** -0.5),
        'b_gate': nrm(ks[6], (L, N_BRANCHES * D), 0.1),
        'rwkv_mu': jax.random.uniform(ks[7], (L, RWKV_COLS), f32),
        'rwkv_w0': jax.random.uniform(ks[8], (L, RWKV_WIDTH), f32, -6.0, 0.0),
        'rwkv_w2': nrm(ks[9], (L, DECAY_LORA, RWKV_WIDTH), 0.1 * DECAY_LORA ** -0.5),
        'rwkv_a0': nrm(ks[10], (L, RWKV_WIDTH), 0.1),
        'rwkv_a2': nrm(ks[11], (L, AAA_LORA, RWKV_WIDTH), AAA_LORA ** -0.5),
        'rwkv_g2': nrm(ks[12], (L, GATE_LORA, RWKV_WIDTH), GATE_LORA ** -0.5),
        'rwkv_k_k': gain(ks[13], (L, RWKV_WIDTH)),
        'rwkv_k_a': gain(ks[14], (L, RWKV_WIDTH)),
        'rwkv_r_k': nrm(ks[15], (L, RWKV_HEADS, HEAD_DIM), 0.1),
        'rwkv_ln_w': gain(ks[16], (L, RWKV_WIDTH)),
        'rwkv_ln_b': nrm(ks[17], (L, RWKV_WIDTH), 0.01),
        'attn_q_norm': gain(ks[18], (L, HEAD_DIM)),
        'attn_k_norm': gain(ks[19], (L, HEAD_DIM)),
        'w_proj_rwkv': nrm(ks[20], (L, RWKV_WIDTH, D), RWKV_WIDTH ** -0.5),
        'w_proj_attn': nrm(ks[21], (L, ATTN_WIDTH, D), ATTN_WIDTH ** -0.5),
        'w_out': nrm(ks[22], (L, D, D), D ** -0.5),
        'ffn2_norm': gain(ks[23], (L, D)),
        'ffn2_w_in': nrm(ks[24], (L, D, 2 * D_FF), D ** -0.5),
        'ffn2_w_out': nrm(ks[25], (L, D_FF, D), D_FF ** -0.5),
    }

def first_block(x, ffn1_norm, ffn1_w_in, ffn1_w_out, mix_norm, w_in, b_gate, rwkv_mu,
              rwkv_w0, rwkv_w2, rwkv_a0, rwkv_a2, rwkv_g2, rwkv_k_k, rwkv_k_a, rwkv_r_k,
              rwkv_ln_w, rwkv_ln_b, attn_q_norm, attn_k_norm, w_proj_rwkv, w_proj_attn,
              w_out, ffn2_norm, ffn2_w_in, ffn2_w_out):
    for l in range(DEPTH):
        x = x + 0.5 * swiglu(rms_norm(x, ffn1_norm[l]), ffn1_w_in[l], ffn1_w_out[l])
        h = rms_norm(x, mix_norm[l])
        p_rwkv, p_q, p_k, p_v, p_gate = _split_last(
            h @ w_in[l], (RWKV_COLS, ATTN_WIDTH, ATTN_WIDTH, ATTN_WIDTH, N_BRANCHES * D_MODEL))
        y_a = rwkv7_time_mix(p_rwkv, rwkv_mu[l], rwkv_w0[l], rwkv_w2[l], rwkv_a0[l],
                             rwkv_a2[l], rwkv_g2[l], rwkv_k_k[l], rwkv_k_a[l], rwkv_r_k[l],
                             rwkv_ln_w[l], rwkv_ln_b[l]).astype(x.dtype)
        y_b = dilated_attention(p_q, p_k, p_v, attn_q_norm[l], attn_k_norm[l]).astype(x.dtype)
        g_a, g_b = _split_last(jax.nn.sigmoid(p_gate + b_gate[l]), (D_MODEL, D_MODEL))
        merged = g_a * (y_a @ w_proj_rwkv[l]) + g_b * (y_b @ w_proj_attn[l])
        x = x + merged @ w_out[l]
        x = x + 0.5 * swiglu(rms_norm(x, ffn2_norm[l]), ffn2_w_in[l], ffn2_w_out[l])
    return x


DEPTH_2 = 2

CTX_LEN = 256
GRID_W = 64
NORM_EPS = 1e-6

ML_HEADS = 4
ML_DK = 256
ML_DV = 256
ML_W = ML_HEADS * ML_DV
ML_CHUNK = 128

DA_HEADS = 8
DA_DH = 64
DA_DV = 2 * DA_DH
DA_QK_W = DA_HEADS * 2 * DA_DH
DA_V_W = DA_HEADS * DA_DV
Q_BLOCK = 128
ROPE_BASE = 10000.0

FN_GROUPS = 4
FN_GC = 256
FN_W = FN_GROUPS * FN_GC

N_BRANCH = 3
D_FF_2 = -(-8 * D_MODEL // (3 * 256)) * 256

IN_SPLITS = (ML_DK * ML_HEADS, ML_DK * ML_HEADS, ML_W, ML_W, 4 * ML_HEADS,
             DA_QK_W, DA_QK_W, DA_V_W, FN_W, N_BRANCH * D_MODEL)
D_IN = sum(IN_SPLITS)


def _rmsnorm(x, g):
    xf = x.astype(jnp.float32)
    y = xf * lax.rsqrt(jnp.mean(xf * xf, axis=-1, keepdims=True) + NORM_EPS)
    return (y * g.astype(jnp.float32)).astype(x.dtype)

def _modulate(h, shift, scale):
    return h * (1 + scale) + shift

def _split_cols(u):
    idx, acc = [], 0
    for s in IN_SPLITS[:-1]:
        acc += s
        idx.append(acc)
    return jnp.split(u, idx, axis=-1)

def _axial_rope(rows):
    n_freq = DA_DH // 4
    inv = ROPE_BASE ** (-jnp.arange(n_freq, dtype=jnp.float32) / n_freq)
    r = jnp.repeat(jnp.arange(rows, dtype=jnp.float32), GRID_W)
    col = jnp.tile(jnp.arange(GRID_W, dtype=jnp.float32), rows)
    ang = jnp.concatenate([r[:, None] * inv, col[:, None] * inv], axis=-1)
    return jnp.cos(ang), jnp.sin(ang)

def _rope(x, cos, sin):
    shp = (cos.shape[0],) + (1,) * (x.ndim - 3) + (cos.shape[1],)
    c = cos.reshape(shp).astype(x.dtype)
    s = sin.reshape(shp).astype(x.dtype)
    x1, x2 = jnp.split(x, 2, axis=-1)
    return jnp.concatenate([x1 * c - x2 * s, x1 * s + x2 * c], axis=-1)

def _mlstm_scan(q, k, v, i_pre, f_pre, state):
    B, T, H, DK = q.shape
    DV = v.shape[-1]
    L = ML_CHUNK
    NC = T // L

    def chunks(a):
        a = a.astype(jnp.float32).reshape((B, NC, L, H) + a.shape[3:])
        return jnp.moveaxis(jnp.moveaxis(a, 1, 0), 3, 2)

    tri = jnp.tril(jnp.ones((L, L), dtype=bool))

    def step(carry, xs):
        C, n, m = carry
        qc, kc, vc, ic, fc = xs
        b = jnp.cumsum(jax.nn.log_sigmoid(fc), axis=-1)
        dmat = jnp.where(tri, b[..., :, None] - b[..., None, :] + ic[..., None, :], -jnp.inf)
        inter = b + m[..., None]
        m_t = jnp.maximum(inter, jnp.max(dmat, axis=-1))
        a = jnp.exp(dmat - m_t[..., None]) * jnp.einsum('bhtd,bhsd->bhts', qc, kc)
        sc = jnp.exp(inter - m_t)
        num = sc[..., None] * jnp.einsum('bhtd,bhde->bhte', qc, C) + jnp.einsum('bhts,bhse->bhte', a, vc)
        den = sc * jnp.einsum('bhtd,bhd->bht', qc, n) + jnp.sum(a, axis=-1)
        h = num / jnp.maximum(jnp.abs(den), jnp.exp(-m_t))[..., None]
        b_end = b[..., -1]
        g_s = b_end[..., None] - b + ic
        m_new = jnp.maximum(b_end + m, jnp.max(g_s, axis=-1))
        decay = jnp.exp(b_end + m - m_new)
        kw = kc * jnp.exp(g_s - m_new[..., None])[..., None]
        C_new = decay[..., None, None] * C + jnp.einsum('bhsd,bhse->bhde', kw, vc)
        n_new = decay[..., None] * n + jnp.sum(kw, axis=2)
        return (C_new, n_new, m_new), h

    final, hs = lax.scan(step, state, (chunks(q), chunks(k), chunks(v), chunks(i_pre), chunks(f_pre)))
    h = jnp.transpose(hs, (1, 0, 3, 2, 4)).reshape(B, T, H, DV)
    return h, final

def _mlstm_branch(ul, uc, gate_b, head_g):
    def prep(u):
        B, T, _ = u[0].shape
        q = u[0].reshape(B, T, ML_HEADS, ML_DK)
        k = u[1].reshape(B, T, ML_HEADS, ML_DK) * (ML_DK ** -0.5)
        v = u[2].reshape(B, T, ML_HEADS, ML_DV)
        i_f, f_f, i_b, f_b = jnp.split(u[4] + gate_b, 4, axis=-1)
        return q, k, v, i_f, f_f, i_b, f_b

    flip = lambda a: jnp.flip(a, axis=1)
    ql, kl, vl, ifl, ffl, ibl, fbl = prep(ul)
    qc, kc, vc, ifc, ffc, ibc, fbc = prep(uc)
    B = ql.shape[0]
    zero = (jnp.zeros((B, ML_HEADS, ML_DK, ML_DV), jnp.float32),
            jnp.zeros((B, ML_HEADS, ML_DK), jnp.float32),
            jnp.zeros((B, ML_HEADS), jnp.float32))
    hcf, st_f = _mlstm_scan(qc, kc, vc, ifc, ffc, zero)
    hlf, _ = _mlstm_scan(ql, kl, vl, ifl, ffl, st_f)
    hcb, st_b = _mlstm_scan(flip(qc), flip(kc), flip(vc), flip(ibc), flip(fbc), zero)
    hlb, _ = _mlstm_scan(flip(ql), flip(kl), flip(vl), flip(ibl), flip(fbl), st_b)

    def out(hf, hb, u):
        B, T = hf.shape[:2]
        h = _rmsnorm(hf + hb, head_g.reshape(ML_HEADS, ML_DV)).reshape(B, T, ML_W)
        return h.astype(u[3].dtype) * jax.nn.sigmoid(u[3])

    return out(hlf, flip(hlb), ul), out(hcf, flip(hcb), uc)

def _diff_attn_core(q, k, v, lam):
    s = jnp.einsum('bqhmd,bkhmd->bhmqk', q, k).astype(jnp.float32) * (DA_DH ** -0.5)
    p = jax.nn.softmax(s, axis=-1)
    a = p[:, :, 0] - lam * p[:, :, 1]
    return jnp.einsum('bhqk,bkhe->bqhe', a.astype(v.dtype), v)

def _diff_attn_branch(ul, uc, lam_qk, head_g, cos, sin, lam_init, need_ctx):
    def qkv(u):
        B, T, _ = u[5].shape
        return (u[5].reshape(B, T, DA_HEADS, 2, DA_DH),
                u[6].reshape(B, T, DA_HEADS, 2, DA_DH),
                u[7].reshape(B, T, DA_HEADS, DA_DV))

    lq = lam_qk.astype(jnp.float32)
    lam = jnp.exp(jnp.sum(lq[0] * lq[1])) - jnp.exp(jnp.sum(lq[2] * lq[3])) + lam_init
    ql, kl, vl = qkv(ul)
    qc, kc, vc = qkv(uc)
    ql, kl = _rope(ql, cos, sin), _rope(kl, cos, sin)
    k_all = jnp.concatenate([kl, kc], axis=1)
    v_all = jnp.concatenate([vl, vc], axis=1)
    B, T = ql.shape[:2]
    nb = T // Q_BLOCK
    qb = jnp.moveaxis(ql.reshape(B, nb, Q_BLOCK, DA_HEADS, 2, DA_DH), 1, 0)
    ob = lax.map(lambda qq: _diff_attn_core(qq, k_all, v_all, lam), qb)
    ol = jnp.moveaxis(ob, 0, 1).reshape(B, T, DA_HEADS, DA_DV)

    def post(o):
        Bo, To = o.shape[:2]
        return (_rmsnorm(o, head_g.reshape(DA_HEADS, DA_DV)) * (1.0 - lam_init)).reshape(Bo, To, DA_V_W)

    oc = post(_diff_attn_core(qc, kc, vc, lam)) if need_ctx else None
    return post(ol), oc

def _fourier(u):
    B, T, _ = u.shape
    z = u.astype(jnp.float32).reshape(B, T, FN_GROUPS, FN_GC)
    y = jnp.fft.fftn(z, axes=(1, 3), norm='ortho').real
    return y.reshape(B, T, FN_W).astype(u.dtype)

def _merge(ym, yd, yf, g_pre, w_br_ml, w_br_da, w_br_fn, w_out):
    gm, gd, gf = jnp.split(jax.nn.sigmoid(g_pre), N_BRANCH, axis=-1)
    y = gm * (ym @ w_br_ml) + gd * (yd @ w_br_da) + gf * (yf @ w_br_fn)
    return y @ w_out

def _mixer(hl, hc, w_in, ml_gate_b, ml_head_g, da_lam, da_head_g, w_br_ml, w_br_da, w_br_fn, w_out,
           cos, sin, lam_init, need_ctx):
    ul = _split_cols(hl @ w_in)
    uc = _split_cols(hc @ w_in)
    ml_l, ml_c = _mlstm_branch(ul, uc, ml_gate_b, ml_head_g)
    da_l, da_c = _diff_attn_branch(ul, uc, da_lam, da_head_g, cos, sin, lam_init, need_ctx)
    yl = _merge(ml_l, da_l, _fourier(ul[8]), ul[9], w_br_ml, w_br_da, w_br_fn, w_out)
    yc = _merge(ml_c, da_c, _fourier(uc[8]), uc[9], w_br_ml, w_br_da, w_br_fn, w_out) if need_ctx else None
    return yl, yc

def _swiglu(h, w_in, w_out):
    a, b = jnp.split(h @ w_in, 2, axis=-1)
    return (jax.nn.silu(a) * b) @ w_out

def second_inputs(seed: int = 0) -> dict:
    key = jax.random.key(seed)
    ks = jax.random.split(key, 20)
    f32 = jnp.float32
    D = D_MODEL

    def nrm(k, shape, s):
        return jax.random.normal(k, shape, f32) * s

    f_mask = jnp.array([0.0, 1.0, 0.0, 1.0], f32)[None, :, None]
    f_bias = jnp.linspace(3.0, 6.0, ML_HEADS, dtype=f32)[None, None, :]
    ml_gate_b = (nrm(ks[8], (DEPTH_2, 4, ML_HEADS), 0.1) + f_mask * f_bias).reshape(DEPTH_2, 4 * ML_HEADS)
    return {
        'x': nrm(ks[0], (BATCH, SEQ, D), 1.0),
        'c': nrm(ks[1], (BATCH, D), 1.0),
        'ctx': nrm(ks[2], (BATCH, CTX_LEN, D), 1.0),
        'c_ctx': nrm(ks[3], (D,), 1.0),
        'w_ada': nrm(ks[4], (DEPTH_2, D, 6 * D), 0.5 * D ** -0.5),
        'b_ada': nrm(ks[5], (DEPTH_2, 6 * D), 0.02),
        'norm_g': 1.0 + nrm(ks[6], (DEPTH_2, 2, D), 0.02),
        'w_in': nrm(ks[7], (DEPTH_2, D, D_IN), D ** -0.5),
        'ml_gate_b': ml_gate_b,
        'ml_head_g': 1.0 + nrm(ks[9], (DEPTH_2, ML_W), 0.02),
        'da_lam': nrm(ks[10], (DEPTH_2, 4, DA_DH), 0.1),
        'da_head_g': 1.0 + nrm(ks[11], (DEPTH_2, DA_V_W), 0.02),
        'w_br_ml': nrm(ks[12], (DEPTH_2, ML_W, D), ML_W ** -0.5),
        'w_br_da': nrm(ks[13], (DEPTH_2, DA_V_W, D), DA_V_W ** -0.5),
        'w_br_fn': nrm(ks[14], (DEPTH_2, FN_W, D), FN_W ** -0.5),
        'w_out': nrm(ks[15], (DEPTH_2, D, D), D ** -0.5),
        'w_ffn_in': nrm(ks[16], (DEPTH_2, D, 2 * D_FF_2), D ** -0.5),
        'w_ffn_out': nrm(ks[17], (DEPTH_2, D_FF_2, D), D_FF_2 ** -0.5),
        'final_g': 1.0 + nrm(ks[18], (D,), 0.02),
    }

def second_block(x, c, ctx, c_ctx, w_ada, b_ada, norm_g, w_in, ml_gate_b, ml_head_g, da_lam, da_head_g,
              w_br_ml, w_br_da, w_br_fn, w_out, w_ffn_in, w_ffn_out, final_g):
    T = x.shape[1]
    ROWS = T // GRID_W
    cos, sin = _axial_rope(ROWS)
    s_lat = jax.nn.silu(c)
    s_ctx = jax.nn.silu(c_ctx)
    xl, xc = x, ctx
    for l in range(DEPTH_2):
        need_ctx = l < DEPTH_2 - 1
        lam_init = 0.8 - 0.6 * math.exp(-0.3 * l)
        ml = jnp.split((s_lat @ w_ada[l] + b_ada[l])[:, None, :], 6, axis=-1)
        mc = jnp.split((s_ctx @ w_ada[l] + b_ada[l])[None, None, :], 6, axis=-1)
        hl = _modulate(_rmsnorm(xl, norm_g[l, 0]), ml[0], ml[1])
        hc = _modulate(_rmsnorm(xc, norm_g[l, 0]), mc[0], mc[1])
        yl, yc = _mixer(hl, hc, w_in[l], ml_gate_b[l], ml_head_g[l], da_lam[l], da_head_g[l],
                        w_br_ml[l], w_br_da[l], w_br_fn[l], w_out[l], cos, sin, lam_init, need_ctx)
        xl = xl + ml[2] * yl
        xl = xl + ml[5] * _swiglu(_modulate(_rmsnorm(xl, norm_g[l, 1]), ml[3], ml[4]), w_ffn_in[l], w_ffn_out[l])
        if need_ctx:
            xc = xc + mc[2] * yc
            xc = xc + mc[5] * _swiglu(_modulate(_rmsnorm(xc, norm_g[l, 1]), mc[3], mc[4]), w_ffn_in[l], w_ffn_out[l])
    return _rmsnorm(xl, final_g)


def setup_inputs(seed=0):
    out = dict(first_inputs(seed))
    for name, value in second_inputs(seed + 1).items():
        if name != "x":
            out[name + "_2"] = value
    return out


def reference(
    x, ffn1_norm, ffn1_w_in, ffn1_w_out, mix_norm, w_in, b_gate, rwkv_mu, rwkv_w0, rwkv_w2,
    rwkv_a0, rwkv_a2, rwkv_g2, rwkv_k_k, rwkv_k_a, rwkv_r_k, rwkv_ln_w, rwkv_ln_b, attn_q_norm,
    attn_k_norm, w_proj_rwkv, w_proj_attn, w_out, ffn2_norm, ffn2_w_in, ffn2_w_out, c_2, ctx_2,
    c_ctx_2, w_ada_2, b_ada_2, norm_g_2, w_in_2, ml_gate_b_2, ml_head_g_2, da_lam_2,
    da_head_g_2, w_br_ml_2, w_br_da_2, w_br_fn_2, w_out_2, w_ffn_in_2, w_ffn_out_2, final_g_2,
):
    x = first_block(
        x, ffn1_norm, ffn1_w_in, ffn1_w_out, mix_norm, w_in, b_gate, rwkv_mu, rwkv_w0, rwkv_w2,
        rwkv_a0, rwkv_a2, rwkv_g2, rwkv_k_k, rwkv_k_a, rwkv_r_k, rwkv_ln_w, rwkv_ln_b,
        attn_q_norm, attn_k_norm, w_proj_rwkv, w_proj_attn, w_out, ffn2_norm, ffn2_w_in,
        ffn2_w_out,
    )
    return second_block(
        x, c_2, ctx_2, c_ctx_2, w_ada_2, b_ada_2, norm_g_2, w_in_2, ml_gate_b_2, ml_head_g_2,
        da_lam_2, da_head_g_2, w_br_ml_2, w_br_da_2, w_br_fn_2, w_out_2, w_ffn_in_2,
        w_ffn_out_2, final_g_2,
    )


_drawn_inputs = setup_inputs


def setup_inputs(seed=0):
    import zlib

    import numpy as np

    out = dict(_drawn_inputs(seed))
    spreads = {}
    factors = {'b_gate': 4.469,
     'rwkv_w2': 8.0,
     'rwkv_a0': 5.036,
     'rwkv_k_k': 2.939,
     'rwkv_ln_b': 8.0,
     'attn_q_norm': 8.0,
     'attn_k_norm': 8.0,
     'norm_g_2': 5.396,
     'ml_head_g_2': 8.0,
     'da_lam_2': 3.852,
     'da_head_g_2': 8.0,
     'final_g_2': 2.789}
    for name, (base, spread) in spreads.items():
        noise = np.random.default_rng([zlib.crc32(name.encode()), seed]).standard_normal(out[name].shape)
        drawn = base * np.exp(spread * noise) if base else spread * noise
        out[name] = __import__('jax').numpy.asarray(drawn.astype(out[name].dtype))
    for name, factor in factors.items():
        out[name] = (out[name] * factor).astype(out[name].dtype)
    return out
```

```python
import math
from contextlib import ExitStack

import concourse.bass as bass
from concourse import mybir

F32 = mybir.dt.float32
ALU = mybir.AluOpType
ACT = mybir.ActivationFunctionType
AX = mybir.AxisListType

P = 128
D = 1024
KT = D // P
T = 256
FF = 2816
FT = FF // P
SLOTS = 3
SLAB = 32 * P
DOWN = FT * P
CHUNK = 16
NCH = T // CHUNK
LAM_INIT = [0.8 - 0.6 * math.exp(-0.3 * layer) for layer in range(2)]
EPS = 1e-6
GN_EPS = 64e-5



def stage_list():
    out = []

    def add(name, slabs, done, act, dve, down=False):
        out.append((name, slabs, DOWN if down else SLAB, done, act, dve))

    def ffn(name):
        add(name + "_up", FT // 2, 4, 0, 2)
        add(name + "_down", KT, 1, 0, 1, down=True)

    def merge(name):
        for half in range(2):
            add(f"{name}_gate{half}", 1, 4, 4, 0)
            add(f"{name}_proj{half}", 1, 4, 0, 4)

    ffn("ffn1")
    for n in ("r", "k", "v"):
        add("rwkv_" + n, 2, 4, 4, 0)
    add("rwkv_lora_in", 1, 3, 3, 0)
    add("rwkv_lora_out", 1, 24, 24, 0)
    merge("rwkv")
    add("dil_qk", 3, 4, 4, 0)
    add("dil_v", 2, 2, 0, 2)
    merge("dil")
    add("mix_out", 2, 4, 0, 4)
    ffn("ffn2")
    for la in range(2):
        p = f"l{la}_"
        add(p + "ada", 12, 4, 0, 4)
        for n in ("q", "k", "v"):
            add(p + "ml_" + n, 2, 4, 4, 0)
        add(p + "ml_o", 2, 4, 4, 0)
        merge(p + "ml")
        for n in ("q", "k", "v"):
            add(p + "da_" + n, 2, 4, 4, 0)
        merge(p + "da")
        add(p + "fn", 2, 4 if la == 0 else 2, 4 if la == 0 else 2, 0)
        merge(p + "fn")
        add(p + "out", 2, 4, 0, 4)
        ffn(p + "ffn")
    return out


class Stage:

    def __init__(self, name, slabs, words, done, act, dve, slab0, wide0, down0, done0, act0, dve0):
        self.name, self.slabs, self.words, self.done, self.act, self.dve = name, slabs, words, done, act, dve
        self.slab0, self.wide0, self.down0 = slab0, wide0, down0
        self.done0, self.act0, self.dve0 = done0, act0, dve0
        self.done_end = done0 + slabs * done
        self.act_end = act0 + slabs * act
        self.dve_end = dve0 + slabs * dve

    def slot(self, j):
        return (self.slab0 + j) % SLOTS

    def landed(self, j, i):
        return ((self.slab0 + j) // SLOTS + 1 + i) * 16


def make_stages():
    st, order = {}, []
    slab = wide = down = done = act = dve = 0
    for name, n, words, d, a, v in stage_list():
        s = Stage(name, n, words, d, a, v, slab, wide, down, done, act, dve)
        st[name] = s
        order.append(s)
        slab += n
        wide += n if words == SLAB else 0
        down += n if words == DOWN else 0
        done, act, dve = s.done_end, s.act_end, s.dve_end
    return st, order


ST, ORDER = make_stages()
N_WIDE = sum(s.slabs for s in ORDER if s.words == SLAB)
N_DOWN = sum(s.slabs for s in ORDER if s.words == DOWN)


def over_slabs(eng, n, body, peel):
    for j in range(min(peel, n)):
        body(j, 0)
    full = max(n - peel, 0) // SLOTS
    if full > 1:
        with eng.Fori(0, full) as i:
            for j in range(SLOTS):
                body(peel + j, i)
    elif full == 1:
        for j in range(SLOTS):
            body(peel + j, 0)
    for j in range(peel + full * SLOTS, n):
        body(j, 0)


class Tally:

    def __init__(self, eng, sems, own):
        self.eng, self.sems, self.own = eng, sems, own
        self.n, self.i, self.per, self.start = {}, None, {}, {}

    def at(self, name):
        v = self.n.get(name, 0)
        if self.i is None:
            return v
        assert name in self.per, name
        return v + self.i * self.per[name]

    def wait(self, name, k=1):
        self.n[name] = self.n.get(name, 0) + k
        self.eng.wait_ge(self.sems[name], self.at(name))

    def step(self, ins):
        ins.then_inc(self.sems[self.own], 1)
        self.wait(self.own)

    def out(self, ins, name):
        ins.then_inc(self.sems[name], 1)
        self.wait(name)

    def skip(self, name, k=1):
        self.n[name] = self.n.get(name, 0) + k

    def loop(self, i, per):
        self.i, self.per, self.start = i, per, dict(self.n)

    def end(self, iters):
        for name, per in self.per.items():
            assert self.n.get(name, 0) - self.start.get(name, 0) == per, (name, per, self.n.get(name, 0), self.start.get(name, 0))
            self.n[name] = self.start.get(name, 0) + per * iters
        for name in self.n:
            assert name in self.per or self.n[name] == self.start.get(name, 0), name
        self.i = None


PCOL = {}


def param_columns():
    n = 0
    spec = [("ffn1_norm", 8), ("mix_norm", 8), ("b_gate", 16), ("mu", 27), ("w0", 8), ("a0", 8), ("k_k", 8), ("k_a", 8),
            ("r_k", 8), ("ln_w", 8), ("ln_b", 8), ("q_norm", 1), ("k_norm", 1), ("ffn2_norm", 8), ("final_g", 8),
            ("c", 16)]
    for la in range(2):
        spec += [(f"l{la}_b_ada", 48), (f"l{la}_norm_g", 16), (f"l{la}_ml_g", 8), (f"l{la}_da_g", 8),
                 (f"l{la}_gate_b", 1), (f"l{la}_lam", 4), (f"l{la}_gate_w", 128)]
    for name, k in spec:
        PCOL[name] = (n, k)
        n += k
    return n


NPAR = param_columns()
CC = {"ident": 0, "ones": 128, "pair": 256}
C_COMMON = 384
C1 = {"gram": 0, "ark": 512, "head": 640, "reset": 1152, "dil": 1408}
C1_N = 1408 + 1536
C2 = {"ml": 0, "dft_t": 4096, "dft_c": 5120, "cos": 6144, "sin": 6400, "perm": 6656}
C2_N = 6784


def program(nc, x_in, ctx_in, wide_in, down_in, par_in, const_in, const1_in, const2_in, out, dbg=None):
    with ExitStack() as ctx:
        sem_names = [
            "landed0", "landed1", "landed2", "loads", "block2_free", "consts2", "out_done",
            "tile_done", "act_out", "dve_out", "silu_ready",
            "act_steps", "dve_steps",
            "squares_ready", "sums_ready", "means_ready", "roots_ready", "h_ready", "x_ready",
            "shift_staged", "shift_done", "lora_ready", "rwkv_in_ready", "rwkv_mid",
            "pe_for_act", "pe_for_dve", "act_for_pe", "act_for_dve", "dve_for_pe", "dve_for_act",
            "chunk_staged", "tok_psum", "tok_ready", "gram_psum", "gram_ready", "pow_psum", "pow_ready",
            "scan_psum", "u_ready", "o_psum", "s_ready", "chunk_free",
            "scores", "probs_in", "probs", "pt_psum", "pt_ready", "pv_psum", "pv_out", "weights_out",
        ]
        S = {n: ctx.enter_context(nc.semaphore(n)) for n in sem_names}

        def sb(name, n):
            return ctx.enter_context(nc.sbuf_tensor(name, [P, n], F32))

        ring = sb("weights", SLOTS * SLAB)
        par = sb("params", NPAR)
        com = sb("common", C_COMMON)
        C = sb("masks", C2_N)
        X = sb("x_T", KT * 2 * T)
        H = sb("h_T", KT * 2 * T)
        G = sb("merged_T", KT * 2 * T)
        A = sb("arena", 20480)
        small = sb("small", 400)
        bank = [ctx.enter_context(nc.psum_tensor(f"bank{b}", [P, 512], F32)) for b in range(8)]

        ident, ones, pair = com[:, 0:128], com[:, 128:256], com[:, 256:384]

        def pc(name, k=0, n=1):
            base = PCOL[name][0]
            return par[:, base + k:base + k + n]

        def tiles(buf, base, n, width):
            return buf[:, base:base + n * width].rearrange("p (k t) -> p k t", k=n)

        def bc(ap, dim, n):
            shape = list(ap.shape)
            shape.insert(dim, n)
            return ap.unsqueeze(dim).to_broadcast(shape)

        X1, H1, G1 = tiles(X, 0, KT, T), tiles(H, 0, KT, T), tiles(G, 0, KT, T)
        X2, H2, G2 = tiles(X, 0, KT, 2 * T), tiles(H, 0, KT, 2 * T), tiles(G, 0, KT, 2 * T)
        HALF = KT * T

        def wtile(st, j, q, n=P):
            base = st.slot(j) * SLAB + q * P
            return ring[:, base:base + n]

        def slot(k):
            return A[:, k * HALF:(k + 1) * HALF]

        def slot3(k):
            return slot(k).rearrange("p (k t) -> p k t", k=KT)

        sR, sA, sB, sK, sBH, sKH, sV, sL, sAA, sG = range(10)
        dec = small[:, 0:128]
        ada = small[:, 128:224]
        gs = small[:, 224:256]
        lam = small[:, 256:260]
        stat = small[:, 260:400]

        def used_by(slab):
            for st in ORDER:
                if slab < st.slab0 + st.slabs:
                    return st.done0 + (slab - st.slab0 + 1) * st.done
            raise AssertionError

        def ml_keys(d, q):
            if q < 2:
                own = list(range(0, q + 1)) if d == 0 else list(range(q, 2))
                return own + [2, 3]
            return list(range(2, q + 1)) if d == 0 else list(range(q, 4))

        def token_outputs_back(t, transpose, base, qtiles, nf):
            y = tiles(A, base, 4, D)
            t.wait("dve_for_pe")
            for k in range(nf):
                if k >= 4:
                    t.wait("dve_for_pe")
                for q in range(qtiles):
                    last = transpose(bank[4 + k % 4][:, q * P:(q + 1) * P], y[:, q, k * P:(k + 1) * P])
                last.then_inc(S["pe_for_dve"], 1)
            t.wait("dve_for_pe", 4)

        ROWS_X = A[:, 16400:16912]
        ROWS_L = A[:, 16912:17424]
        ROWS_B = A[:, 17424:17936]
        ROWS_GI = A[:, 17936:18448]
        ROWS_NCM = A[:, 18448:18960]
        ROWS_EM = A[:, 18960:19472]
        ROWS_1 = A[:, 19472:19984]
        ML_COLS = A[:, 19984:20048].rearrange("p (n c d h) -> p n c d h", n=2, c=4, d=2)
        small_c = small[:, 0:16].rearrange("p (k s) -> p k s", k=KT)
        lam_in = small[:, 16:18]
        Y_ML = 12304

        def rows_gi_em(n):
            return (ROWS_GI, ROWS_EM)[n]

        ROWS0 = 16400

        def G_SQ(la):
            return A[:, 0:4096]

        block = ctx.enter_context(nc.Block())

        @block.sync
        def _(sp):
            sp.dma_start(X1, x_in).then_inc(S["loads"], 16)
            sp.dma_start(par[:, :], par_in).then_inc(S["loads"], 16)
            sp.dma_start(com[:, :], const_in).then_inc(S["loads"], 16)
            sp.dma_start(C[:, 0:C1_N], const1_in).then_inc(S["loads"], 16)
            for n, st in enumerate(ORDER):
                if st.name == "l0_ada":
                    sp.wait_ge(S["block2_free"], 1)
                    sp.dma_start(C[:, :], const2_in).then_inc(S["consts2"], 16)
                    sp.dma_start(H2[:, :, T:], ctx_in).then_inc(S["consts2"], 16)

                def load(j, i, st=st):
                    if st.slab0 + j >= SLOTS:
                        sp.wait_ge(S["tile_done"], used_by(st.slab0 + j - SLOTS) + i * SLOTS * st.done)
                    src = (wide_in, st.wide0) if st.words == SLAB else (down_in, st.down0)
                    base = st.slot(j) * SLAB
                    k = src[1] + j + i * SLOTS
                    view = src[0][bass.ds(k, 1)].rearrange("a p n -> (a p) n")
                    sp.dma_start(ring[:, base:base + st.words], view).then_inc(S[f"landed{st.slot(j)}"], 16)

                over_slabs(sp, st.slabs, load, SLOTS)

        @block.tensor
        def _(pe):
            t = Tally(pe, S, None)
            mm = nc.tensor.matmul

            def matmul(out, lhsT, rhs, start=True, stop=True):
                return mm(out, lhsT, rhs, start=start, stop=stop, skip_group_check=True)

            def transpose(out, in_):
                return matmul(out, in_, ident[0:in_.shape[0], 0:in_.shape[0]])

            def enter(st):
                if st.act0:
                    pe.wait_ge(S["act_out"], st.act0)
                if st.dve0:
                    pe.wait_ge(S["dve_out"], st.dve0)

            def arrived(st, j, i=0):
                pe.wait_ge(S[f"landed{st.slot(j)}"], st.landed(j, i))

            def project(st, rhs, n, kt=KT, drains=None):
                enter(st)

                def body(j, i):
                    arrived(st, j, i)
                    for c in range(4):
                        if j >= 1:
                            name, pos = drains[c]
                            per = st.act if name == "act_out" else st.dve
                            base = st.act0 if name == "act_out" else st.dve0
                            pe.wait_ge(S[name], base + per * (j - 1) + pos + 1 + i * (SLOTS * per))
                        for k in range(kt):
                            last = matmul(bank[c][:, 0:n], wtile(st, j, c * kt + k), rhs(k), start=k == 0, stop=k == kt - 1)
                        last.then_inc(S["tile_done"], 1)

                over_slabs(pe, st.slabs, body, 1)

            by_act = [("act_out", c) for c in range(4)]
            by_dve = [("dve_out", c) for c in range(4)]
            by_pairs = [("dve_out", c % 2) for c in range(4)]

            def project_tokens(st, lhs, n_tok, width, groups=4):
                enter(st)
                for j in range(st.slabs):
                    arrived(st, j)
                    for q in range(n_tok):
                        if j >= 1:
                            name = "act_out" if st.act else "dve_out"
                            base, per = (st.act0, st.act) if st.act else (st.dve0, st.dve)
                            pe.wait_ge(S[name], base + per * (j - 1) + q + 1)
                        for k in range(KT):
                            last = matmul(bank[q][:, 0:width], lhs(k, q), wtile(st, j, 0, KT * width)[:, k * width:(k + 1) * width],
                                          start=k == 0, stop=k == KT - 1)
                        last.then_inc(S["tile_done"], 1)

            def norm_sums(width):
                t.wait("squares_ready")
                sq = tiles(A, 0, KT, width)
                for k in range(KT):
                    last = matmul(bank[4][:, 0:width], ones, sq[:, k], start=k == 0, stop=k == KT - 1)
                last.then_inc(S["sums_ready"], 1)
                t.wait("h_ready")

            def ffn(name, h, width):
                project(ST[name + "_up"], lambda k: h[:, k, 0:width], width, drains=by_pairs)
                st = ST[name + "_down"]
                hid = tiles(A, 0, FT, width)
                enter(st)

                def body(j, i):
                    arrived(st, j, i)
                    b = j % SLOTS
                    if j >= SLOTS:
                        pe.wait_ge(S["dve_out"], st.dve0 + j - SLOTS + 1 + i * SLOTS)
                    for k in range(FT):
                        last = matmul(bank[b][:, 0:width], wtile(st, j, k), hid[:, k], start=k == 0, stop=k == FT - 1)
                    last.then_inc(S["tile_done"], 1)

                over_slabs(pe, st.slabs, body, SLOTS)

            def merge(name, h, y, width, kt=KT):
                for half in range(2):
                    project(ST[f"{name}_gate{half}"], lambda k: h[:, k, 0:width], width, drains=by_act)
                    if half == 0:
                        t.wait("dve_for_pe")
                    project(ST[f"{name}_proj{half}"], lambda k: y[:, k, 0:width], width, kt=kt, drains=by_dve)

            pe.wait_ge(S["loads"], 64)
            norm_sums(T)
            ffn("ffn1", H1, T)
            norm_sums(T)
            for n in ("r", "k", "v"):
                project(ST["rwkv_" + n], lambda k: H1[:, k], T, drains=by_act)
            st = ST["rwkv_lora_in"]
            enter(st)
            arrived(st, 0)
            for c in range(3):
                for k in range(KT):
                    last = matmul(bank[c][:, 0:T], wtile(st, 0, c * KT + k), H1[:, k], start=k == 0, stop=k == KT - 1)
                last.then_inc(S["tile_done"], 1)
            st = ST["rwkv_lora_out"]
            enter(st)
            arrived(st, 0)
            t.wait("lora_ready")
            lora = tiles(A, sBH * HALF, 3, T)
            for j in range(KT):
                for c in range(3):
                    q = 3 * j + c
                    if q >= 4:
                        pe.wait_ge(S["act_out"], st.act0 + q - 3)
                    cols = ring[:, st.slot(0) * SLAB:st.slot(0) * SLAB + 3 * D].rearrange("p (a n) -> p a n", a=3)[:, :, j * P:(j + 1) * P]
                    dst = bank[q % 4][:, 0:T]
                    if c == 0:
                        last = matmul(dst, cols[0:64, 0], lora[0:64, 0])
                    elif c == 1:
                        last = matmul(dst, cols[64:128, 0], lora[64:128, 0])
                    else:
                        matmul(dst, cols[:, 1], lora[:, 1], stop=False)
                        last = matmul(dst, cols[0:32, 2], lora[0:32, 2], start=False)
                    last.then_inc(S["tile_done"], 1)
            for _ in range(2):
                t.wait("act_for_pe" if _ == 0 else "dve_for_pe")
                src = slot(sKH)
                for b in range(4):
                    last = matmul(bank[4 + b][:, :], pair, src[:, b * 512:(b + 1) * 512])
                last.then_inc(S["pe_for_act" if _ == 0 else "pe_for_dve"], 1)
            stg = X[:, HALF:HALF + 896].rearrange("p (a c) -> p a c", a=7)
            tok = X[:, HALF + 896:HALF + 1408].rearrange("p (a c) -> p a c", a=4)
            gram = H[:, HALF:HALF + 1024].rearrange("p (g a c) -> p g a c", g=2, a=4)
            ark = H[:, HALF + 1024:HALF + 1280].rearrange("p (g c) -> p g c", g=2)
            mt = H[:, HALF + 1280:HALF + 1536].rearrange("p (g c) -> p g c", g=2)
            q8 = H[:, HALF + 1536:HALF + 1792].rearrange("p (g c) -> p g c", g=2)
            p2 = G[:, HALF:HALF + 512].rearrange("p (g a c) -> p g a c", g=2, a=2)
            p4 = G[:, HALF + 512:HALF + 1024].rearrange("p (g a c) -> p g a c", g=2, a=2)
            wn = G[:, HALF + 1024:HALF + 1408].rearrange("p (a c) -> p a c", a=3)
            vb = C[:, C1_N:C1_N + 1024].rearrange("p (g n) -> p g n", g=2)
            ub = C[:, C1_N + 1024:C1_N + 2048].rearrange("p (g n) -> p g n", g=2)
            state = C[:, C1_N + 2048:C1_N + 2560]
            t.wait("rwkv_in_ready")
            with pe.Fori(0, NCH) as i:
                t.loop(i, {"chunk_staged": 1, "tok_ready": 1, "gram_ready": 1, "pow_ready": 7, "u_ready": 1, "s_ready": 1})
                t.wait("chunk_staged")
                for n, a in enumerate((1, 4, 5, 6)):
                    last = transpose(bank[4][:, n * P:(n + 1) * P], stg[:, a])
                last.then_inc(S["tok_psum"], 1)
                for g in range(2):
                    lo = 64 * g
                    rows = slice(lo, lo + 64)
                    matmul(bank[g][:, 0:256], stg[rows, 2], X[rows, HALF:HALF + 256])
                    matmul(bank[g][:, 256:512], stg[rows, 1], X[rows, HALF + 256:HALF + 512])
                    last = matmul(bank[2 + g][:, 0:128], stg[rows, 3], stg[rows, 0])
                last.then_inc(S["gram_psum"], 1)
                t.wait("gram_ready")
                for g in range(2):
                    matmul(bank[5][:, g * 256:g * 256 + 128], gram[:, g, 2], gram[:, g, 1])
                    last = matmul(bank[5][:, g * 256 + 128:g * 256 + 256], gram[:, g, 1], gram[:, g, 2])
                last.then_inc(S["pow_psum"], 1)
                t.wait("pow_ready")
                for g in range(2):
                    last = matmul(bank[6][:, g * P:(g + 1) * P], p2[:, g, 1], mt[:, g])
                last.then_inc(S["pow_psum"], 1)
                for g in range(2):
                    matmul(bank[7][:, g * 256:g * 256 + 128], p2[:, g, 1], p2[:, g, 0])
                    last = matmul(bank[7][:, g * 256 + 128:g * 256 + 256], p2[:, g, 0], p2[:, g, 1])
                last.then_inc(S["pow_psum"], 1)
                t.wait("pow_ready", 2)
                for g in range(2):
                    last = matmul(bank[6][:, g * P:(g + 1) * P], p4[:, g, 1], mt[:, g])
                last.then_inc(S["pow_psum"], 1)
                for g in range(2):
                    last = matmul(bank[5][:, g * P:(g + 1) * P], p4[:, g, 0], p4[:, g, 1])
                last.then_inc(S["pow_psum"], 1)
                t.wait("pow_ready", 2)
                for g in range(2):
                    last = matmul(bank[6][:, g * P:(g + 1) * P], q8[:, g], mt[:, g])
                last.then_inc(S["pow_psum"], 1)
                t.wait("pow_ready")
                t.wait("tok_ready")
                for g in range(2):
                    matmul(bank[7][64 * g:64 * g + 64, 0:P], tok[:, 0, 64 * g:64 * g + 64], mt[:, g])
                for g in range(2):
                    last = matmul(bank[7][:, (1 + g) * P:(2 + g) * P], gram[:, g, 3], mt[:, g])
                last.then_inc(S["pow_psum"], 1)
                t.wait("pow_ready")
                for g in range(2):
                    rows = slice(64 * g, 64 * g + 64)
                    matmul(bank[g][:, :], wn[rows, 0], state[rows, :], stop=False)
                    last = matmul(bank[g][:, :], wn[:, 1 + g], vb[:, g], start=False)
                last.then_inc(S["scan_psum"], 1)
                for g in range(2):
                    rows = slice(64 * g, 64 * g + 64)
                    matmul(bank[2 + g][:, :], stg[rows, 0], state[rows, :], stop=False)
                    matmul(bank[2 + g][:, :], ark[:, g], vb[:, g], start=False, stop=False)
                t.wait("u_ready")
                for g in range(2):
                    rows = slice(64 * g, 64 * g + 64)
                    matmul(bank[4][rows, :], tok[:, 1, rows], ub[:, g], stop=False)
                    matmul(bank[4][rows, :], tok[:, 2, rows], vb[:, g], start=False)
                    last = matmul(bank[2 + g][:, :], gram[:, g, 0], ub[:, g], start=False)
                last.then_inc(S["o_psum"], 1)
                t.wait("s_ready")
            t.end(NCH)
            t.wait("dve_for_pe")
            o_tok = slot(sL).rearrange("p (c f) -> p c f", c=NCH)
            for b in range(4):
                for c in range(4):
                    last = transpose(bank[4 + b][:, c * P:(c + 1) * P], o_tok[:, 4 * b + c])
            last.then_inc(S["pe_for_dve"], 1)
            merge("rwkv", H1, slot3(sR), T)

            qk = tiles(A, 3072, 12, T)
            v1 = tiles(A, 6144, 2, 768)
            project(ST["dil_qk"], lambda k: H1[:, k], T, drains=by_act)
            project_tokens(ST["dil_v"], lambda k, q: H1[:, k, q * P:(q + 1) * P], 2, 384)
            for half in range(2):
                if half == 0:
                    t.wait("act_for_pe")
                else:
                    t.wait("dve_for_pe")
                for b in range(3):
                    src = A[:, 7680 + (3 * half + b) * 512:7680 + (3 * half + b + 1) * 512]
                    last = matmul(bank[4 + b][:, :], pair, src)
                last.then_inc(S["pe_for_dve"], 1)
            t.wait("dve_for_pe")
            y1 = tiles(A, 13824, 2, 768)

            def dil_scores(h):
                if h >= 2:
                    t.wait("probs_in")
                rows = slice(64 * (h % 2), 64 * (h % 2) + 64)
                for q in range(2):
                    last = matmul(bank[h % 2][:, q * T:(q + 1) * T], qk[rows, h // 2, q * P:(q + 1) * P], qk[rows, 6 + h // 2])
                last.then_inc(S["scores"], 1)

            def dil_values(h):
                pr = A[:, 10752 + (h % 2) * 512:10752 + (h % 2) * 512 + 512].rearrange("p (q k) -> p q k", q=2)
                pt = A[:, 11776 + (h % 2) * 512:11776 + (h % 2) * 512 + 512].rearrange("p (q k) -> p q k", q=2)
                t.wait("probs")
                for q in range(2):
                    for k in range(2):
                        last = transpose(bank[4 + h % 2][:, (2 * q + k) * P:(2 * q + k + 1) * P], pr[:, q, k * P:(k + 1) * P])
                last.then_inc(S["pt_psum"], 1)
                t.wait("pt_ready")
                if h >= 2:
                    t.wait("pv_out")
                for q in range(2):
                    for k in range(2):
                        last = matmul(bank[6 + h % 2][:, q * 64:(q + 1) * 64], pt[:, q, k * P:(k + 1) * P], v1[:, k, h * 64:(h + 1) * 64],
                                      start=k == 0, stop=k == 1)
                last.then_inc(S["pv_psum"], 1)

            for h in range(12):
                dil_scores(h)
                if h:
                    dil_values(h - 1)
            dil_values(11)
            t.wait("probs_in", 2)
            t.wait("pv_out", 2)
            t.wait("dve_for_pe")
            for q in range(2):
                for b in range(2):
                    for c in range(3):
                        last = transpose(bank[4 + 2 * q + b][:, c * P:(c + 1) * P], y1[:, q, (3 * b + c) * P:(3 * b + c + 1) * P])
            last.then_inc(S["pe_for_dve"], 1)
            merge("dil", H1, tiles(A, 0, 6, T), T, kt=6)
            pe.wait_ge(S["dve_out"], ST["mix_out"].dve0)
            t.wait("dve_for_pe")
            project(ST["mix_out"], lambda k: G1[:, k], T, drains=by_dve)
            norm_sums(T)
            ffn("ffn2", H1, T)

            pe.wait_ge(S["consts2"], 32)
            for la in range(2):
                nq = 2 * T if la == 0 else T
                p = f"l{la}_"
                qtiles = nq // P
                t.wait("act_for_pe")
                project(ST[p + "ada"], lambda k: small_c[:, k], 2, drains=by_dve)
                t.wait("dve_for_pe")
                matmul(bank[5][:, 0:2], ones[0:64, :], lam_in[0:64, :]).then_inc(S["pe_for_act"], 1)
                norm_sums(2 * T)
                project(ST[p + "ml_q"], lambda k: H2[:, k, 0:nq], nq, drains=by_act)
                project(ST[p + "ml_k"], lambda k: H2[:, k], 2 * T, drains=by_act)
                project_tokens(ST[p + "ml_v"], lambda k, q: H2[:, k, q * P:(q + 1) * P], 4, 512)
                t.wait("dve_for_pe")
                gw = tiles(G, 0, KT, P)
                for k in range(KT):
                    last = matmul(bank[4][:, :], gw[:, k], H2[:, k], start=k == 0, stop=k == KT - 1)
                last.then_inc(S["pe_for_act"], 1)
                t.wait("dve_for_pe")
                for n in range(2):
                    for c in range(4):
                        last = transpose(bank[5 + n][:, c * P:(c + 1) * P], rows_gi_em(n)[:, c * P:(c + 1) * P])
                last.then_inc(S["pe_for_dve"], 1)
                t.wait("dve_for_pe")
                qT, kT = tiles(A, 0, KT, 2 * T), tiles(A, 4096, KT, 2 * T)
                v2 = A[:, 8192:8192 + 4 * 1028].rearrange("p (s n) -> p s n", s=4)
                for h in range(4):
                    if h:
                        t.wait("dve_for_pe")
                    for s in range(4):
                        for kk in range(2):
                            last = matmul(bank[4 + s][:, 0:nq], kT[:, 2 * h + kk, s * P:(s + 1) * P], qT[:, 2 * h + kk, 0:nq],
                                          start=kk == 0, stop=kk == 1)
                    for d in range(2):
                        r = 64 * d + h
                        last = matmul(bank[d][:, 0:nq], ident[:, r:r + 1].to_broadcast([P, P]), ROWS_NCM[:, 0:nq])
                    last.then_inc(S["scores"], 1)
                    for d in range(2):
                        at = G[:, d * 2048:(d + 1) * 2048].rearrange("p (s q) -> p s q", s=4)
                        t.wait("probs")
                        for q in range(qtiles):
                            keys = ml_keys(d, q)
                            if (h, d) != (0, 0) or q >= 2:
                                t.wait("pv_out")
                            for n, s in enumerate(keys):
                                last = matmul(bank[2 + q % 2][:, 0:257], at[:, s, q * P:(q + 1) * P], v2[:, s, h * 257:(h + 1) * 257],
                                              start=n == 0, stop=n == len(keys) - 1)
                            last.then_inc(S["pv_psum"], 1)
                t.wait("pv_out", 2)
                token_outputs_back(t, transpose, 12304, qtiles, 8)
                enter(ST[p + "ml_o"])
                project(ST[p + "ml_o"], lambda k: H2[:, k, 0:nq], nq, drains=by_act)
                merge(p + "ml", H2, tiles(A, 0, KT, 2 * T), nq)
                project(ST[p + "da_q"], lambda k: H2[:, k, 0:nq], nq, drains=by_act)
                project(ST[p + "da_k"], lambda k: H2[:, k], 2 * T, drains=by_act)
                project_tokens(ST[p + "da_v"], lambda k, q: H2[:, k, q * P:(q + 1) * P], 4, 512)
                pe.wait_ge(S["act_out"], ST[p + "da_v"].act_end)
                perm = C[:, C2["perm"]:C2["perm"] + P]
                for n in range(8):
                    src = (qT, kT)[n // 4]
                    if n >= 2:
                        t.wait("dve_for_pe")
                    for c in range(2):
                        last = matmul(bank[4 + n % 2][:, c * T:(c + 1) * T], perm, src[:, 2 * (n % 4) + c, 0:T])
                    last.then_inc(S["pe_for_dve"], 1)
                t.wait("dve_for_pe", 2)
                v3 = tiles(A, 8192, 4, D)
                units = [(h, q) for h in range(8) for q in range(qtiles)]

                def keys_of(q):
                    return (0, 4) if q < 2 else (2, 4)

                def da_scores(n):
                    h, q = units[n]
                    k0, k1 = keys_of(q)
                    if n >= 2:
                        t.wait("probs_in")
                    for m in range(2):
                        rows = slice(64 * m, 64 * m + 64)
                        last = matmul(bank[4 * m + n % 2][:, 0:(k1 - k0) * P], qT[rows, h, q * P:(q + 1) * P], kT[rows, h, k0 * P:k1 * P])
                    last.then_inc(S["scores"], 1)

                def da_values(n):
                    h, q = units[n]
                    k0, k1 = keys_of(q)
                    t.wait("probs")
                    pr = A[:, 16384 + (n % 2) * 1024:16384 + (n % 2) * 1024 + 512]
                    pt = A[:, 18432 + (n % 2) * 512:18432 + (n % 2) * 512 + 512]
                    for k in range(k1 - k0):
                        last = transpose(bank[2 + n % 2][:, k * P:(k + 1) * P], pr[:, k * P:(k + 1) * P])
                    last.then_inc(S["pt_psum"], 1)
                    t.wait("pt_ready")
                    if n >= 2:
                        t.wait("pv_out")
                    for k in range(k1 - k0):
                        last = matmul(bank[6 + n % 2][:, 0:P], pt[:, k * P:(k + 1) * P], v3[:, k0 + k, h * P:(h + 1) * P],
                                      start=k == 0, stop=k == k1 - k0 - 1)
                    last.then_inc(S["pv_psum"], 1)

                for n in range(len(units)):
                    da_scores(n)
                    if n:
                        da_values(n - 1)
                da_values(len(units) - 1)
                t.wait("probs_in", 2)
                t.wait("pv_out", 2)
                token_outputs_back(t, transpose, 12288, qtiles, 8)
                merge(p + "da", H2, tiles(A, 0, KT, 2 * T), nq)
                project_tokens(ST[p + "fn"], lambda k, q: H2[:, k, q * P:(q + 1) * P], qtiles, 512)
                pe.wait_ge(S["act_out"], ST[p + "fn"].act_end)
                z = tiles(A, 4096, 4, D)
                dft_t = tiles(C, C2["dft_t"], 2, 512)
                dft_c = C[:, C2["dft_c"]:C2["dft_c"] + 1024].rearrange("p (f k n) -> p f k n", f=2, k=2)
                zf = A[:, 8192:16384].rearrange("p (k f s t) -> p k f s t", k=KT, f=2, s=2)
                n = 0
                for k in range(KT):
                    for s in range(nq // T):
                        if n >= 4:
                            t.wait("act_for_pe")
                        for tt in range(2):
                            last = matmul(bank[4 + n % 4][:, :], z[:, 2 * s + tt, k * P:(k + 1) * P], dft_t[:, tt], start=tt == 0, stop=tt == 1)
                        last.then_inc(S["pe_for_act"], 1)
                        n += 1
                t.wait("act_for_pe", 4)
                for k in range(KT):
                    grp, half = k // 2, k % 2
                    if k >= 4:
                        t.wait("act_for_pe")
                    for f in range(2):
                        for kk in range(2):
                            last = matmul(bank[4 + k % 4][:, 0:nq], dft_c[:, f, kk, half * P:(half + 1) * P],
                                          zf[:, 2 * grp + kk, f].rearrange("p s t -> p (s t)")[:, 0:nq],
                                          start=f == 0 and kk == 0, stop=f == 1 and kk == 1)
                    last.then_inc(S["pe_for_act"], 1)
                t.wait("act_for_pe", 4)
                merge(p + "fn", H2, tiles(A, 0, KT, 2 * T), nq)
                t.wait("dve_for_pe")
                project(ST[p + "out"], lambda k: G2[:, k, 0:nq], nq, drains=by_dve)
                norm_sums(nq)
                ffn(p + "ffn", H2, nq)
            norm_sums(T)

        @block.scalar
        def _(act):
            t = Tally(act, S, "act_steps")
            af = nc.scalar.activation

            def tiles_of(st, body):
                def one(j, i):
                    for c in range(st.act):
                        act.wait_ge(S["tile_done"], st.done0 + st.done * j + c + 1 + i * (SLOTS * st.done))
                        ins = body(c, j, i)
                        ins.then_inc(S["act_out"], 1)
                        act.wait_ge(S["act_out"], st.act0 + st.act * j + c + 1 + i * (SLOTS * st.act))
                over_slabs(act, st.slabs, one, 0)

            def norm(x, width, first=False):
                if not first:
                    t.wait("x_ready")
                t.out(af(tiles(A, 0, KT, width), x[:, :, 0:width], ACT.Square), "squares_ready")
                t.wait("means_ready")
                t.out(af(A[:, 4096 + width:4096 + 2 * width], A[:, 4096:4096 + width], ACT.Sqrt), "roots_ready")

            silu_count = [0]

            def ffn(name, width):
                st = ST[name + "_up"]
                base = silu_count[0]
                tmp = tiles(A, FT * 2 * T, 2, width)

                def one(j, i):
                    for c in range(2):
                        act.wait_ge(S["tile_done"], st.done0 + 4 * j + c + 1 + i * (4 * SLOTS))
                        if j >= 1:
                            act.wait_ge(S["dve_out"], st.dve0 + 2 * (j - 1) + c + 1 + i * (2 * SLOTS))
                        af(tmp[:, c], bank[c][:, 0:width], ACT.Silu).then_inc(S["silu_ready"], 1)
                over_slabs(act, st.slabs, one, 1)
                silu_count[0] += 2 * st.slabs

            def merge(name, width, bias=None, gates_at=16384):
                gt = tiles(A, gates_at, 4, 2 * T)
                for half in range(2):
                    st = ST[f"{name}_gate{half}"]
                    act.wait_ge(S["dve_out"], st.dve0)
                    tiles_of(st, lambda c, j, i: af(gt[:, c, 0:width], bank[c][:, 0:width], ACT.Sigmoid,
                                                    bias=pc(bias[0], bias[1] + 4 * half + c) if bias else 0.0))

            act.wait_ge(S["loads"], 64)
            norm(X1, T, first=True)
            ffn("ffn1", T)
            norm(X1, T)
            shift = X[:, HALF:HALF + 4 * 257].rearrange("p (b n) -> p b n", b=4)
            t.wait("dve_for_act")
            n = 0
            for name in ("r", "k", "v", "lora_in"):
                st = ST["rwkv_" + name]
                for j in range(st.slabs):
                    for c in range(st.act):
                        act.wait_ge(S["tile_done"], st.done0 + st.done * j + c + 1)
                        if n >= 4:
                            t.wait("shift_done")
                        af(shift[:, n % 4, 1:257], bank[c][:, 0:T], ACT.Copy).then_inc(S["act_out"], 1)
                        n += 1
            t.wait("shift_done", 4)
            lora = tiles(A, sBH * HALF, 3, T)
            t.step(af(lora[0:64, 0], lora[0:64, 0], ACT.Tanh))
            t.step(af(lora[:, 1], lora[:, 1], ACT.Sigmoid))
            t.out(af(lora[0:32, 2], lora[0:32, 2], ACT.Sigmoid), "lora_ready")
            st = ST["rwkv_lora_out"]
            for q in range(24):
                j, c = q // 3, q % 3
                act.wait_ge(S["tile_done"], st.done0 + q + 1)
                src = bank[q % 4][:, 0:T]
                if c == 0:
                    ins = af(slot3(sL)[:, j], src, ACT.Sigmoid, bias=pc("w0", j))
                elif c == 1:
                    ins = af(slot3(sAA)[:, j], src, ACT.Sigmoid, bias=pc("a0", j))
                else:
                    ins = af(slot3(sG)[:, j], src, ACT.Copy)
                ins.then_inc(S["act_out"], 1)
            act.wait_ge(S["act_out"], st.act_end)
            t.wait("dve_for_act")
            t.out(af(slot(sKH), slot(sA), ACT.Square), "act_for_pe")
            t.wait("pe_for_act")
            for b in range(4):
                ins = af(slot(sBH)[:, b * 512:(b + 1) * 512], bank[4 + b][:, :], ACT.Sqrt)
                if b < 3:
                    t.step(ins)
            t.out(ins, "act_for_dve")
            t.wait("dve_for_act")
            t.out(af(slot(sBH), slot(sL), ACT.Exp), "act_for_dve")
            t.wait("dve_for_act")
            t.out(af(slot(sKH), slot(sL), ACT.Exp, scale=-1.0), "act_for_dve")
            t.wait("dve_for_act")
            t.out(af(slot(sL), G[:, HALF:2 * HALF], ACT.Exp), "act_for_dve")
            stg = X[:, HALF:HALF + 896]
            tok = X[:, HALF + 896:HALF + 1408]
            q7 = A[:, 0:7 * HALF].rearrange("p (a t) -> p a t", a=7 * KT)
            t.wait("rwkv_in_ready")
            with act.Fori(0, NCH) as i:
                t.loop(i, {"chunk_free": 1, "chunk_staged": 1, "tok_psum": 1, "tok_ready": 1})
                t.wait("chunk_free")
                t.out(af(stg.rearrange("p (a t) -> p a t", a=7 * KT), q7[:, :, bass.ds(i * CHUNK, CHUNK)], ACT.Copy), "chunk_staged")
                t.wait("tok_psum")
                t.out(af(tok, bank[4][:, :], ACT.Copy), "tok_ready")
            t.end(NCH)
            t.wait("dve_for_act")
            t.out(af(stat[:, 32:64], stat[:, 64:96], ACT.Sqrt), "act_for_dve")
            merge("rwkv", T, bias=("b_gate", 0), gates_at=sA * HALF)
            st = ST["dil_qk"]
            qk = tiles(A, 3072, 12, T)
            act.wait_ge(S["dve_out"], st.dve0)
            for j in range(3):
                for c in range(4):
                    act.wait_ge(S["tile_done"], st.done0 + 4 * j + c + 1)
                    af(qk[:, 4 * j + c], bank[c][:, 0:T], ACT.Copy).then_inc(S["act_out"], 1)
            act.wait_ge(S["act_out"], st.act_end)
            t.out(af(A[:, 7680:10752], A[:, 3072:6144], ACT.Square), "act_for_pe")
            for _ in range(2):
                t.wait("dve_for_act")
                t.out(af(A[:, 15360:16896], A[:, 15360:16896], ACT.Sqrt), "act_for_dve")
            for h in range(12):
                pr = A[:, 10752 + (h % 2) * 512:10752 + (h % 2) * 512 + 512].rearrange("p (q k) -> p q k", q=2)
                t.wait("weights_out")
                for q in range(2):
                    ins = af(pr[:, q], pr[:, q], ACT.Exp, bias=stat[:, 24 + 2 * h + q:25 + 2 * h + q],
                             accum_out=stat[:, 48 + 2 * h + q:49 + 2 * h + q])
                    if q == 0:
                        t.step(ins)
                t.out(ins, "probs")
            t.out(af(stat[:, 0:24], stat[:, 48:72], ACT.Ln), "act_for_dve")
            t.wait("dve_for_act")
            t.out(af(stat[:, 0:24], stat[:, 0:24], ACT.Exp), "act_for_dve")
            merge("dil", T, bias=("b_gate", 8))
            norm(X1, T)
            ffn("ffn2", T)

            for la in range(2):
                nq = 2 * T if la == 0 else T
                qtiles = nq // P
                p = f"l{la}_"
                if la == 0:
                    act.wait_ge(S["dve_out"], ST[p + "ada"].dve0)
                t.out(af(small[:, 0:16], pc("c", 0, 16), ACT.Silu), "act_for_pe")
                t.wait("pe_for_act")
                t.out(af(lam[:, 0:2], bank[5][:, 0:2], ACT.Exp), "act_for_dve")
                norm(X2, 2 * T)
                qT, kT = tiles(A, 0, KT, 2 * T), tiles(A, 4096, KT, 2 * T)
                t.wait("dve_for_act")
                tiles_of(ST[p + "ml_q"], lambda c, j, i: af(qT[:, 4 * j + c, 0:nq], bank[c][:, 0:nq], ACT.Copy))
                tiles_of(ST[p + "ml_k"], lambda c, j, i: af(kT[:, 4 * j + c], bank[c][:, :], ACT.Copy, scale=1.0 / 16))
                v2 = A[:, 8192:8192 + 4 * 1028].rearrange("p (s h n) -> p s h n", s=4, h=4)
                tiles_of(ST[p + "ml_v"], lambda c, j, i: af(v2[:, c, 2 * j:2 * j + 2, 0:256],
                                                            bank[c][:, :].rearrange("p (h n) -> p h n", h=2), ACT.Copy))
                t.wait("pe_for_act")
                t.step(af(ROWS_X, bank[4][:, :], ACT.Identity, bias=pc(p + "gate_b")))
                t.step(af(ROWS_L, ROWS_X, ACT.Abs))
                t.step(af(ROWS_L, ROWS_L, ACT.Exp, scale=-1.0))
                t.out(af(ROWS_L, ROWS_L, ACT.Ln, bias=1.0), "act_for_dve")
                t.wait("dve_for_act")
                t.out(af(ROWS_EM, ROWS_EM, ACT.Exp), "act_for_dve")
                for h in range(4):
                    for d in range(2):
                        at = G[:, d * 2048:(d + 1) * 2048].rearrange("p (s q) -> p s q", s=4)
                        for s in range(4):
                            t.wait("dve_for_act")
                            t.out(af(at[:, s, 0:nq], at[:, s, 0:nq], ACT.Exp), "act_for_dve")
                t.wait("dve_for_act")
                t.out(af(G[:, :], A[:, Y_ML:Y_ML + 4096], ACT.Square), "act_for_dve")
                t.wait("dve_for_act")
                t.out(af(stat[:, 16:32], stat[:, 0:16], ACT.Sqrt), "act_for_dve")
                o_gate = tiles(A, 4096, KT, 2 * T)
                tiles_of(ST[p + "ml_o"], lambda c, j, i: af(o_gate[:, 4 * j + c, 0:nq], bank[c][:, 0:nq], ACT.Sigmoid))
                merge(p + "ml", nq)
                act.wait_ge(S["dve_out"], ST[p + "da_q"].dve0)
                tiles_of(ST[p + "da_q"], lambda c, j, i: af(qT[:, 4 * j + c, 0:nq], bank[c][:, 0:nq], ACT.Copy))
                tiles_of(ST[p + "da_k"], lambda c, j, i: af(kT[:, 4 * j + c], bank[c][:, :], ACT.Copy))
                v3 = tiles(A, 8192, 4, D)
                tiles_of(ST[p + "da_v"], lambda c, j, i: af(v3[:, c, j * 512:(j + 1) * 512], bank[c][:, :], ACT.Copy))
                t.wait("dve_for_act")
                for n in range(8 * qtiles):
                    w = 512 if n % qtiles < 2 else 256
                    t.wait("weights_out")
                    for m in range(2):
                        pr = A[:, 16384 + (n % 2) * 1024 + m * 512:16384 + (n % 2) * 1024 + m * 512 + w]
                        ins = af(pr, bank[4 * m + n % 2][:, 0:w], ACT.Exp, scale=0.125, bias=stat[:, 4 * (n % 2) + m:4 * (n % 2) + m + 1],
                                 accum_out=stat[:, 4 * (n % 2) + 2 + m:4 * (n % 2) + 3 + m])
                        if m == 0:
                            t.step(ins)
                    t.out(ins, "probs_in")
                t.wait("dve_for_act")
                t.out(af(G_SQ(la), A[:, 12288:16384], ACT.Square), "act_for_dve")
                t.wait("dve_for_act")
                t.out(af(stat[:, 64:96], stat[:, 32:64], ACT.Sqrt), "act_for_dve")
                merge(p + "da", nq)
                act.wait_ge(S["dve_out"], ST[p + "fn"].dve0)
                z = tiles(A, 4096, 4, D)
                tiles_of(ST[p + "fn"], lambda c, j, i: af(z[:, c, j * 512:(j + 1) * 512], bank[c][:, :], ACT.Copy))
                zf = A[:, 8192:16384].rearrange("p (k f s t) -> p k f s t", k=KT, f=2, s=2)
                n = 0
                for k in range(KT):
                    for s in range(nq // T):
                        t.wait("pe_for_act")
                        t.out(af(zf[:, k, :, s], bank[4 + n % 4][:, :].rearrange("p (f t) -> p f t", f=2), ACT.Copy), "act_for_pe")
                        n += 1
                yT = tiles(A, 0, KT, 2 * T)
                for k in range(KT):
                    t.wait("pe_for_act")
                    t.out(af(yT[:, k, 0:nq], bank[4 + k % 4][:, 0:nq], ACT.Copy), "act_for_pe")
                merge(p + "fn", nq)
                norm(X2, nq)
                ffn(p + "ffn", nq)
            norm(X2, T)
            t.wait("dve_for_act")
            act.dma_start(out, H1).then_inc(S["out_done"], 16)
            act.wait_ge(S["out_done"], 16)

        @block.vector
        def _(dve):
            t = Tally(dve, S, "dve_steps")
            tt, ts, stt = nc.vector.tensor_tensor, nc.vector.tensor_scalar, nc.vector.scalar_tensor_tensor
            mul, add, sub = ALU.mult, ALU.add, ALU.subtract

            def tiles_of(st, body, cs=(0, 1, 2, 3)):
                def one(j, i):
                    for n, c in enumerate(cs):
                        dve.wait_ge(S["tile_done"], st.done0 + st.done * j + c + 1 + i * (SLOTS * st.done))
                        ins = body(n, j, i)
                        ins.then_inc(S["dve_out"], 1)
                        dve.wait_ge(S["dve_out"], st.dve0 + st.dve * j + n + 1 + i * (SLOTS * st.dve))
                over_slabs(dve, st.slabs, one, 0)

            def rstd(width):
                t.wait("sums_ready")
                t.out(ts(A[:, 4096:4096 + width], bank[4][:, 0:width], 1.0 / D, EPS, mul, add), "means_ready")
                t.wait("roots_ready")
                t.step(nc.vector.reciprocal(A[:, 4096:4096 + width], A[:, 4096 + width:4096 + 2 * width]))
                return A[:, 4096:4096 + width]

            def norm(x, h, width, gain):
                r = rstd(width)
                for k in range(KT):
                    ins = stt(h[:, k], x[:, k, 0:width], pc(gain, k), r, mul, mul)
                    if k < KT - 1:
                        t.step(ins)
                t.out(ins, "h_ready")

            def norm_mod(x, h, width, which):
                r = rstd(width)
                g4 = gs.rearrange("p (w k s) -> p w k s", w=2, k=KT)
                a3 = ada.rearrange("p (k s) -> p k s", s=2)
                for k in range(KT):
                    for s in range(width // T):
                        cols = slice(s * T, (s + 1) * T)
                        t.step(stt(h[:, k, cols], x[:, k, cols], g4[:, which, k, s:s + 1], r[:, cols], mul, mul))
                        ins = ts(h[:, k, cols], h[:, k, cols], a3[:, 24 * which + k, s:s + 1], None, add)
                        if k < KT - 1 or s < width // T - 1:
                            t.step(ins)
                t.out(ins, "h_ready")

            silu_count = [0]

            def ffn(name, x, width, gate=None):
                st = ST[name + "_up"]
                base = silu_count[0]
                tmp = tiles(A, FT * 2 * T, 2, width)

                def one(j, i):
                    for c in range(2):
                        dve.wait_ge(S["tile_done"], st.done0 + 4 * j + 2 + c + 1 + i * (4 * SLOTS))
                        dve.wait_ge(S["silu_ready"], base + 2 * j + c + 1 + i * (2 * SLOTS))
                        dst = A[:, bass.ds((2 * j + c) * width + i * (2 * SLOTS * width), width)]
                        tt(dst, tmp[:, c], bank[2 + c][:, 0:width], mul).then_inc(S["dve_out"], 1)
                over_slabs(dve, st.slabs, one, 0)
                silu_count[0] += 2 * st.slabs
                st = ST[name + "_down"]
                dve.wait_ge(S["dve_out"], st.dve0)
                for j in range(KT):
                    dve.wait_ge(S["tile_done"], st.done0 + j + 1)
                    src = bank[j % SLOTS]
                    if gate is None:
                        ins = stt(x[:, j, 0:width], src[:, 0:width], 0.5, x[:, j, 0:width], mul, add)
                    else:
                        for s in range(width // T):
                            cols = slice(s * T, (s + 1) * T)
                            ins = stt(x[:, j, cols], src[:, cols], gate(j, s), x[:, j, cols], mul, add)
                            if s < width // T - 1:
                                t.step(ins)
                    ins.then_inc(S["dve_out"], 1)
                    dve.wait_ge(S["dve_out"], st.dve0 + j + 1)

            def merge(name, g, width, first, gates_at=16384):
                gt = tiles(A, gates_at, 4, 2 * T)
                for half in range(2):
                    st = ST[f"{name}_proj{half}"]
                    dve.wait_ge(S["act_out"], st.act0)
                    for c in range(4):
                        dve.wait_ge(S["tile_done"], st.done0 + c + 1)
                        dst = g[:, 4 * half + c, 0:width]
                        if first:
                            tt(dst, gt[:, c, 0:width], bank[c][:, 0:width], mul).then_inc(S["dve_out"], 1)
                        else:
                            t.step(tt(gt[:, c, 0:width], gt[:, c, 0:width], bank[c][:, 0:width], mul))
                            tt(dst, dst, gt[:, c, 0:width], add).then_inc(S["dve_out"], 1)
                        dve.wait_ge(S["dve_out"], st.dve0 + c + 1)

            def say(name):
                t.out(nc.vector.memset(stat[0:1, 139:140], 0.0), name)

            dve.wait_ge(S["loads"], 64)
            norm(X1, H1, T, "ffn1_norm")
            ffn("ffn1", X1, T)
            say("x_ready")
            norm(X1, H1, T, "mix_norm")
            shift = X[:, HALF:HALF + 4 * 257].rearrange("p (b n) -> p b n", b=4)
            t.out(nc.vector.memset(shift[:, :, 0:1], 0.0), "dve_for_act")
            n = 0
            dif = X[:, HALF + 1040:HALF + 1296]
            for name, base in (("r", sR), ("k", sK), ("v", sV), ("lora_in", sBH)):
                st = ST["rwkv_" + name]
                for q in range(st.slabs * st.act):
                    dve.wait_ge(S["act_out"], st.act0 + q + 1)
                    cur, prev = shift[:, n % 4, 1:257], shift[:, n % 4, 0:256]
                    rows = slice(0, P) if n < 26 else slice(0, 32)
                    t.step(tt(dif[rows], prev[rows], cur[rows], sub))
                    t.out(stt(slot3(base)[rows, q], dif[rows], pc("mu", n)[rows], cur[rows], mul, add), "shift_done")
                    n += 1
            dve.wait_ge(S["act_out"], ST["rwkv_lora_out"].act_end)
            L, R3, A3, B3, K3 = slot(sL), slot3(sR), slot3(sA), slot3(sB), slot3(sK)
            t.out(tt(A3, K3, bc(pc("k_k", 0, 8), 2, T), mul), "dve_for_act")
            t.step(ts(L, L, -math.exp(-0.5), None, mul))
            t.wait("act_for_dve")
            t.step(ts(slot(sBH), slot(sBH), 1e-12, None, ALU.max))
            t.step(nc.vector.reciprocal(slot(sBH), slot(sBH)))
            t.step(tt(slot(sA), slot(sA), slot(sBH), mul))
            t.step(tt(slot(sB), slot(sA), slot(sAA), mul))
            t.step(ts(slot(sAA), slot(sAA), -1.0, None, add))
            t.step(tt(slot3(sAA), slot3(sAA), bc(pc("k_a", 0, 8), 2, T), mul))
            t.step(stt(slot(sK), slot(sAA), 1.0, slot(sK), add, mul))
            t.step(tt(slot(sKH), slot(sR), slot(sK), mul))
            t.out(tt(slot3(sKH), slot3(sKH), bc(pc("r_k", 0, 8), 2, T), mul), "dve_for_pe")
            t.wait("pe_for_dve")
            for b in range(4):
                c = slice(b * 512, (b + 1) * 512)
                t.step(tt(slot(sAA)[:, c], slot(sV)[:, c], bank[4 + b][:, :], mul))
            t.step(tt(slot3(sAA), slot3(sAA), bc(pc("ln_b", 0, 8), 2, T), add))
            lm = G[:, HALF:2 * HALF]
            t.step(nc.vector.tensor_copy(lm, L))
            for k in range(KT):
                t.step(nc.vector.tensor_tensor_scan(slot3(sL)[:, k], C[:, C1["reset"]:C1["reset"] + T],
                                                    lm[:, k * T:(k + 1) * T], 0.0, mul, add))
            t.out(tt(lm, L, lm, sub), "dve_for_act")
            t.wait("act_for_dve")
            t.step(tt(slot(sR), slot(sR), slot(sBH), mul))
            e_last = slot(sBH).rearrange("p (k c t) -> p k c t", k=KT, t=CHUNK)[:, :, :, CHUNK - 1]
            d3 = dec.rearrange("p (k c) -> p k c", k=KT)
            t.out(nc.vector.tensor_copy(d3, e_last), "dve_for_act")
            t.wait("act_for_dve")
            t.step(tt(slot(sK), slot(sK), slot(sKH), mul))
            t.out(tt(slot(sB), slot(sB), slot(sKH), mul), "dve_for_act")

            def by_chunk(k):
                return slot(k).rearrange("p (k t) -> p k t", t=CHUNK)

            dcol = bc(dec, 2, CHUNK)
            t.step(tt(by_chunk(sBH), by_chunk(sB), dcol, mul))
            t.step(tt(by_chunk(sKH), by_chunk(sK), dcol, mul))
            t.wait("act_for_dve")
            t.step(stt(slot(sA), slot(sA), -1.0, slot(sL), mul, mul))
            tok_v = X[:, HALF + 896 + 384:HALF + 1408]
            gram = H[:, HALF:HALF + 1024].rearrange("p (g a c) -> p g a c", g=2, a=4)
            gramf = H[:, HALF:HALF + 1024].rearrange("p (g a) -> p g a", g=2)
            ark = H[:, HALF + 1024:HALF + 1280].rearrange("p (g c) -> p g c", g=2)
            mtf = H[:, HALF + 1280:HALF + 1536]
            mt = mtf.rearrange("p (g c) -> p g c", g=2)
            q8 = H[:, HALF + 1536:HALF + 1792]
            p2 = G[:, HALF:HALF + 512]
            p4 = G[:, HALF + 512:HALF + 1024]
            wn = G[:, HALF + 1024:HALF + 1408]
            vb = C[:, C1_N:C1_N + 1024].rearrange("p (g h n) -> p g h n", g=2, h=8)
            ub = C[:, C1_N + 1024:C1_N + 2048].rearrange("p (g n) -> p g n", g=2)
            state = C[:, C1_N + 2048:C1_N + 2560]
            om = G[:, HALF + 1408:HALF + 1920]
            head = C[:, C1["head"]:C1["head"] + 512]
            t.step(nc.vector.memset(state, 0.0))
            t.step(nc.vector.memset(stat[0:1, 138:139], 0.0))
            nc.vector.memset(stat[0:1, 139:140], 0.0).then_inc(S["chunk_free"], 1)
            dve.wait_ge(S["chunk_free"], 1)
            say("rwkv_in_ready")
            copy = nc.vector.tensor_copy
            with dve.Fori(0, NCH) as i:
                t.loop(i, {"gram_psum": 1, "gram_ready": 1, "tok_ready": 1, "pow_psum": 7, "pow_ready": 7, "scan_psum": 1,
                           "u_ready": 1, "o_psum": 1, "s_ready": 1, "chunk_free": 1, "dve_steps": 14})
                t.wait("gram_psum")
                for g in range(2):
                    t.step(tt(gramf[:, g], bank[g][:, :], C[:, C1["gram"]:C1["gram"] + 512], mul))
                    t.step(tt(ark[:, g], bank[2 + g][:, 0:128], C[:, C1["ark"]:C1["ark"] + 128], mul))
                t.out(tt(mt, gram[:, :, 1], bc(ident, 1, 2), add), "gram_ready")
                t.wait("tok_ready")
                for g in range(2):
                    t.step(tt(vb[:, g], bc(tok_v[:, 64 * g:64 * g + 64], 1, 8), head.rearrange("p (h n) -> p h n", h=8), mul))
                t.wait("pow_psum")
                t.out(copy(p2, bank[5][:, :]), "pow_ready")
                t.wait("pow_psum")
                t.out(tt(mtf, mtf, bank[6][:, 0:256], add), "pow_ready")
                t.wait("pow_psum")
                t.out(copy(p4, bank[7][:, :]), "pow_ready")
                t.wait("pow_psum")
                t.out(tt(mtf, mtf, bank[6][:, 0:256], add), "pow_ready")
                t.wait("pow_psum")
                t.out(copy(q8, bank[5][:, 0:256]), "pow_ready")
                t.wait("pow_psum")
                t.out(tt(mtf, mtf, bank[6][:, 0:256], add), "pow_ready")
                t.wait("pow_psum")
                t.out(copy(wn, bank[7][:, 0:384]), "pow_ready")
                t.wait("scan_psum")
                t.step(tt(ub[:, 0], bank[0][:, :], head, mul))
                t.out(tt(ub[:, 1], bank[1][:, :], head, mul), "u_ready")
                s3 = state.rearrange("p (h n) -> p h n", h=8)
                t.wait("o_psum")
                t.step(tt(s3, s3, dec.rearrange("p (k c) -> p k c", k=KT)[:, :, bass.ds(i, 1)].to_broadcast([P, 8, 64]), mul))
                t.step(tt(state, state, bank[4][:, :], add))
                for g in range(2):
                    t.step(tt(om, bank[2 + g][:, :], head, mul))
                    t.step(nc.vector.tensor_reduce(slot(sL)[:, bass.ds(i * P + g * 64, 64)], om.rearrange("p (h n) -> p n h", h=8),
                                                   axis=AX.X, op=add))
                t.step(copy(stat[0:1, 138:139], stat[0:1, 139:140]))
                t.out(copy(stat[0:1, 138:139], stat[0:1, 139:140]), "s_ready")
                t.out(copy(stat[0:1, 138:139], stat[0:1, 139:140]), "chunk_free")
            t.skip("chunk_free", 1) if False else None
            t.end(NCH)
            o3 = slot(sL).rearrange("p (u n) -> p u n", n=64)
            sq = slot(sBH)
            sq3 = sq.rearrange("p (u n) -> p u n", n=64)
            mean, var, root = stat[:, 0:32], stat[:, 64:96], stat[:, 32:64]
            t.step(nc.vector.tensor_reduce(mean, o3, axis=AX.X, op=add))
            t.step(ts(mean, mean, 1.0 / 64, None, mul))
            t.step(tt(o3, o3, bc(mean, 2, 64), sub))
            t.step(tt(sq, slot(sL), slot(sL), mul))
            t.step(nc.vector.tensor_reduce(var, sq3, axis=AX.X, op=add))
            t.out(ts(var, var, 1.0 / 64, GN_EPS, mul, add), "dve_for_act")
            t.wait("act_for_dve")
            t.step(nc.vector.reciprocal(root, root))
            t.out(tt(o3, o3, bc(root, 2, 64), mul), "dve_for_pe")
            t.wait("pe_for_dve")
            for b in range(4):
                for c in range(4):
                    t.step(tt(slot3(sR)[:, :, (4 * b + c) * CHUNK:(4 * b + c + 1) * CHUNK],
                              bank[4 + b][:, c * P:(c + 1) * P].rearrange("p (k t) -> p k t", k=KT),
                              bc(pc("ln_w", 0, 8), 2, CHUNK), mul))
            t.step(tt(slot(sR), slot(sR), slot(sAA), add))
            t.out(tt(slot(sR), slot(sR), slot(sG), mul), "dve_for_pe")
            merge("rwkv", G1, T, True, gates_at=sA * HALF)

            st = ST["dil_v"]
            v1 = tiles(A, 6144, 2, 768)
            for j in range(2):
                for q in range(2):
                    dve.wait_ge(S["tile_done"], st.done0 + 2 * j + q + 1)
                    copy(v1[:, q, j * 384:(j + 1) * 384], bank[q][:, 0:384]).then_inc(S["dve_out"], 1)
            dve.wait_ge(S["dve_out"], st.dve_end)
            for half in range(2):
                t.wait("pe_for_dve")
                for b in range(3):
                    dst = A[:, 15360 + b * 512:15360 + (b + 1) * 512]
                    if half == 0:
                        ins = ts(dst, bank[4 + b][:, :], 1.0, 64 * EPS, mul, add)
                    else:
                        ins = ts(dst, bank[4 + b][:, :], 1.0 / 64, EPS, mul, add)
                    if b < 2:
                        t.step(ins)
                t.out(ins, "dve_for_act")
                t.wait("act_for_dve")
                rs = A[:, 15360:16896]
                t.step(nc.vector.reciprocal(rs, rs))
                qkf = A[:, 3072 + half * 1536:3072 + (half + 1) * 1536]
                t.out(stt(qkf, qkf, pc("q_norm" if half == 0 else "k_norm"), rs, mul, mul), "dve_for_pe")
            y1 = tiles(A, 13824, 2, 768)

            def dil_in(h):
                pr = A[:, 10752 + (h % 2) * 512:10752 + (h % 2) * 512 + 512]
                t.wait("scores")
                if h >= 2:
                    pass
                t.out(tt(pr, bank[h % 2][:, :], C[:, C1["dil"] + (h // 4) * 512:C1["dil"] + (h // 4) * 512 + 512], add), "probs_in")
                t.step(nc.vector.tensor_reduce(stat[:, 72 + 2 * h:74 + 2 * h], pr.rearrange("p (q k) -> p q k", q=2), axis=AX.X, op=ALU.max))
                t.out(ts(stat[:, 24 + 2 * h:26 + 2 * h], stat[:, 72 + 2 * h:74 + 2 * h], -1.0, None, mul), "weights_out")

            def dil_out(h):
                t.wait("pt_psum")
                t.out(copy(A[:, 11776 + (h % 2) * 512:11776 + (h % 2) * 512 + 512], bank[4 + h % 2][:, :]), "pt_ready")
                t.wait("pv_psum")
                t.out(copy(y1[:, :, h * 64:(h + 1) * 64], bank[6 + h % 2][:, 0:128].rearrange("p (q n) -> p q n", q=2)), "pv_out")

            for h in range(12):
                dil_in(h)
                if h:
                    dil_out(h - 1)
            dil_out(11)
            t.wait("act_for_dve")
            lse, mx = stat[:, 0:24], stat[:, 96:104]
            t.step(tt(lse, lse, stat[:, 72:96], add))
            t.step(nc.vector.tensor_reduce(mx, lse.rearrange("p (g u) -> p u g", g=3), axis=AX.X, op=ALU.max))
            t.out(tt(lse.rearrange("p (g u) -> p g u", g=3), lse.rearrange("p (g u) -> p g u", g=3), bc(mx, 1, 3), sub), "dve_for_act")
            t.wait("act_for_dve")
            t.step(nc.vector.tensor_reduce(mx, lse.rearrange("p (g u) -> p u g", g=3), axis=AX.X, op=add))
            t.step(tt(stat[:, 48:72].rearrange("p (g u) -> p g u", g=3), stat[:, 48:72].rearrange("p (g u) -> p g u", g=3), bc(mx, 1, 3), mul))
            t.step(nc.vector.reciprocal(stat[:, 48:72], stat[:, 48:72]))
            t.step(tt(stat[:, 48:72], stat[:, 48:72], lse, mul))
            for q in range(2):
                yq = y1[:, q].rearrange("p (h n) -> p h n", h=12)
                wq = bc(stat[:, 48:72].rearrange("p (h q) -> p h q", q=2)[:, :, q], 2, 64)
                ins = tt(yq, yq, wq, mul)
                if q == 0:
                    t.step(ins)
            t.out(ins, "dve_for_pe")
            t.wait("pe_for_dve")
            yT = tiles(A, 0, 6, T)
            for q in range(2):
                for b in range(2):
                    ins = copy(yT[:, 3 * b:3 * b + 3, q * P:(q + 1) * P], bank[4 + 2 * q + b][:, 0:384].rearrange("p (k t) -> p k t", k=3))
                    if not (q == 1 and b == 1):
                        t.step(ins)
            t.out(ins, "dve_for_pe")
            merge("dil", G1, T, False)
            say("dve_for_pe")
            tiles_of(ST["mix_out"], lambda c, j, i: tt(X1[:, 4 * j + c], X1[:, 4 * j + c], bank[c][:, 0:T], add))
            say("x_ready")
            norm(X1, H1, T, "ffn2_norm")
            ffn("ffn2", X1, T)
            t.out(copy(G1, X1), "block2_free")
            t.step(copy(X2[:, :, 0:T], G1))
            dve.wait_ge(S["consts2"], 32)
            t.step(copy(X2[:, :, T:], H2[:, :, T:]))

            for la in range(2):
                nq = 2 * T if la == 0 else T
                qtiles = nq // P
                p = f"l{la}_"
                a3 = ada.rearrange("p (k s) -> p k s", s=2)
                tiles_of(ST[p + "ada"], lambda c, j, i: ts(ada[:, bass.ds(8 * j + 2 * c + i * (8 * SLOTS), 2)], bank[c][:, 0:2],
                                                          par[:, bass.ds(PCOL[p + "b_ada"][0] + 4 * j + c + i * (4 * SLOTS), 1)], None, add))
                g4 = gs.rearrange("p (w k s) -> p w k s", w=2, k=KT)
                for w in range(2):
                    t.step(stt(g4[:, w], a3[:, 24 * w + 8:24 * w + 16], 1.0, bc(pc(p + "norm_g", 8 * w, 8), 2, 2), add, mul))
                lq = pc(p + "lam", 0, 4).rearrange("p (a b) -> p a b", b=2)
                t.out(tt(lam_in[0:64, :], lq[0:64, :, 0], lq[0:64, :, 1], mul), "dve_for_pe")
                t.wait("act_for_dve")
                t.step(tt(lam[:, 2:3], lam[:, 1:2], lam[:, 0:1], sub))
                t.step(ts(lam[:, 2:3], lam[:, 2:3], -LAM_INIT[la], None, add))
                say("x_ready")
                norm_mod(X2, H2, 2 * T, 0)
                say("dve_for_act")
                gw = tiles(G, 0, KT, P)
                t.step(nc.vector.memset(G[:, 0:KT * P], 0.0))
                gsrc = pc(p + "gate_w", 0, 128).rearrange("p (k n) -> p k n", k=KT)
                for n in range(4):
                    t.step(copy(gw[:, :, 32 * n:32 * n + 4], gsrc[:, :, 4 * n:4 * n + 4]))
                v2 = A[:, 8192:8192 + 4 * 1028].rearrange("p (s n) -> p s n", n=257)
                t.step(nc.vector.memset(A[:, ROWS0:ROWS0 + 7 * 512], 0.0))
                t.step(nc.vector.memset(ROWS_1, 1.0))
                t.step(nc.vector.memset(A[:, 8192:8192 + 16 * 257].rearrange("p (u n) -> p u n", n=257)[:, :, 256:257], 1.0))
                say("dve_for_pe")
                t.wait("act_for_dve")
                t.step(stt(ROWS_L, ROWS_X, 0.0, ROWS_L, ALU.min, sub))
                scan = nc.vector.tensor_tensor_scan
                for d in range(2):
                    fr, ir = slice(64 * d + 32, 64 * d + 36), slice(64 * d, 64 * d + 4)

                    def seq(ap, s, d=d):
                        lo = T * s
                        cols = ap[:, lo:lo + T]
                        return cols if d == 0 else cols[:, ::-1]

                    end = (2 * T - 1) if d == 0 else T
                    t.step(scan(seq(ROWS_B[ir], 1), seq(ROWS_1[fr], 1), seq(ROWS_L[fr], 1), 0.0, mul, add))
                    t.step(copy(ROWS_EM[fr, 0:1], ROWS_B[ir, end:end + 1]))
                    t.step(scan(seq(ROWS_B[ir], 0), seq(ROWS_1[fr], 0), seq(ROWS_L[fr], 0), ROWS_EM[fr, 0:1], mul, add))
                    t.step(tt(ROWS_GI[ir], ROWS_X[ir], ROWS_B[ir], sub))
                    t.step(scan(seq(ROWS_NCM[ir], 1), seq(ROWS_GI[ir], 1), seq(ROWS_GI[ir], 1), 0.0, ALU.max, ALU.max))
                    t.step(scan(seq(ROWS_NCM[ir], 0), seq(ROWS_GI[ir], 0), seq(ROWS_GI[ir], 0), ROWS_NCM[ir, end:end + 1], ALU.max, ALU.max))
                    t.step(ts(ROWS_NCM[ir], ROWS_NCM[ir], -1.0, None, mul))
                    t.step(tt(ROWS_EM[ir], ROWS_NCM[ir], ROWS_B[ir], sub))
                say("dve_for_act")
                t.wait("act_for_dve")
                say("dve_for_pe")
                t.wait("pe_for_dve")
                for n in range(2):
                    for d in range(2):
                        ins = copy(ML_COLS[:, n, :, d], bank[5 + n][:, :].rearrange("p (c q) -> p c q", c=4)[:, :, 64 * d:64 * d + 4])
                        if not (n == 1 and d == 1):
                            t.step(ins)
                t.out(ins, "dve_for_pe")
                y2 = tiles(A, Y_ML, 4, D)
                if nq < 2 * T:
                    t.step(nc.vector.memset(A[:, Y_ML + 2048:Y_ML + 4096], 0.0))

                def num_out(h, d):
                    for q in range(qtiles):
                        t.wait("pv_psum")
                        b = bank[2 + q % 2]
                        den = stat[:, 100:101]
                        t.step(ts(den, b[:, 256:257], -1.0, None, mul))
                        t.step(stt(den, b[:, 256:257], ML_COLS[:, 1, q, d, h:h + 1], den, ALU.max, ALU.max))
                        t.step(nc.vector.reciprocal(den, den))
                        dst = y2[:, q, h * 256:(h + 1) * 256]
                        if d == 0:
                            t.out(ts(dst, b[:, 0:256], den, None, mul), "pv_out")
                        else:
                            t.out(stt(dst, b[:, 0:256], den, dst, mul, add), "pv_out")

                for h in range(4):
                    t.wait("scores")
                    for d in range(2):
                        at = G[:, d * 2048:(d + 1) * 2048].rearrange("p (s q) -> p s q", s=4)
                        for s in range(4):
                            mask = C[:, C2["ml"] + (4 * d + s) * 512:C2["ml"] + (4 * d + s) * 512 + nq]
                            t.out(stt(at[:, s, 0:nq], bank[d][:, 0:nq], ML_COLS[:, 0, s, d, h:h + 1], mask, add, ALU.min), "dve_for_act")
                            t.wait("act_for_dve")
                            ins = tt(at[:, s, 0:nq], at[:, s, 0:nq], bank[4 + s][:, 0:nq], mul)
                            if s < 3:
                                t.step(ins)
                        t.out(ins, "probs")
                        num_out(h, d)
                    if h < 3:
                        say("dve_for_pe")
                say("dve_for_act")
                t.wait("act_for_dve")
                ms, rt = stat[:, 0:16], stat[:, 16:32]
                t.step(nc.vector.tensor_reduce(ms, G[:, :].rearrange("p (u n) -> p u n", n=256), axis=AX.X, op=add))
                t.out(ts(ms, ms, 1.0 / 256, EPS, mul, add), "dve_for_act")
                t.wait("act_for_dve")
                t.step(nc.vector.reciprocal(rt, rt))
                yv = A[:, Y_ML:Y_ML + 4096].rearrange("p (u n) -> p u n", n=256)
                t.out(tt(yv, yv, bc(rt, 2, 256), mul), "dve_for_pe")
                bT = tiles(A, 0, KT, 2 * T)

                def outputs_back(gain):
                    for k in range(KT):
                        t.wait("pe_for_dve")
                        t.out(ts(bT[:, k, 0:nq], bank[4 + k % 4][:, 0:nq], gain(k), None, mul), "dve_for_pe")

                outputs_back(lambda k: pc(p + "ml_g", k))
                dve.wait_ge(S["act_out"], ST[p + "ml_o"].act_end)
                o_gate = tiles(A, 4096, KT, 2 * T)
                t.out(tt(bT[:, :, 0:nq], bT[:, :, 0:nq], o_gate[:, :, 0:nq], mul), "dve_for_pe")
                merge(p + "ml", G2, nq, True)
                qT, kT = tiles(A, 0, KT, 2 * T), tiles(A, 4096, KT, 2 * T)
                dve.wait_ge(S["act_out"], ST[p + "da_v"].act_end)
                for n in range(8):
                    x2 = (qT, kT)[n // 4][:, 2 * (n % 4):2 * (n % 4) + 2, 0:T]
                    t.wait("pe_for_dve")
                    tmp = tiles(A, 16384, 2, T)
                    t.step(tt(tmp, bank[4 + n % 2][:, :].rearrange("p (a t) -> p a t", a=2), bc(C[:, C2["sin"]:C2["sin"] + T], 1, 2), mul))
                    t.step(tt(x2, x2, bc(C[:, C2["cos"]:C2["cos"] + T], 1, 2), mul))
                    t.out(tt(x2, x2, tmp, add), "dve_for_pe")
                say("dve_for_act")
                units = [(h, q) for h in range(8) for q in range(qtiles)]
                y3 = tiles(A, 12288, 4, D)
                if nq < 2 * T:
                    t.step(nc.vector.memset(A[:, 12288 + 2048:12288 + 4096], 0.0))

                def da_in(n):
                    w = 512 if units[n][1] < 2 else 256
                    st_ = stat[:, 4 * (n % 2):4 * (n % 2) + 4]
                    t.wait("scores")
                    for m in range(2):
                        t.step(nc.vector.tensor_reduce(st_[:, m:m + 1], bank[4 * m + n % 2][:, 0:w], axis=AX.X, op=ALU.max))
                    t.out(ts(st_[:, 0:2], st_[:, 0:2], -0.125, None, mul), "weights_out")

                def da_mid(n):
                    w = 512 if units[n][1] < 2 else 256
                    st_ = stat[:, 4 * (n % 2):4 * (n % 2) + 4]
                    p0 = A[:, 16384 + (n % 2) * 1024:16384 + (n % 2) * 1024 + w]
                    p1 = A[:, 16384 + (n % 2) * 1024 + 512:16384 + (n % 2) * 1024 + 512 + w]
                    t.wait("probs_in")
                    t.step(nc.vector.reciprocal(st_[:, 2:4], st_[:, 2:4]))
                    t.step(tt(st_[:, 3:4], st_[:, 3:4], lam[:, 2:3], mul))
                    t.step(ts(p1, p1, st_[:, 3:4], None, mul))
                    t.out(stt(p0, p0, st_[:, 2:3], p1, mul, add), "probs")

                def da_out(n):
                    h, q = units[n]
                    w = 512 if q < 2 else 256
                    t.wait("pt_psum")
                    t.out(copy(A[:, 18432 + (n % 2) * 512:18432 + (n % 2) * 512 + w], bank[2 + n % 2][:, 0:w]), "pt_ready")
                    t.wait("pv_psum")
                    t.out(copy(y3[:, q, h * P:(h + 1) * P], bank[6 + n % 2][:, 0:P]), "pv_out")

                da_in(0)
                for n in range(len(units)):
                    da_mid(n)
                    if n + 1 < len(units):
                        da_in(n + 1)
                    da_out(n)
                say("dve_for_act")
                t.wait("act_for_dve")
                ms, rt = stat[:, 32:64], stat[:, 64:96]
                t.step(nc.vector.tensor_reduce(ms, A[:, 0:4096].rearrange("p (u n) -> p u n", n=P), axis=AX.X, op=add))
                t.out(ts(ms, ms, 1.0 / P, EPS, mul, add), "dve_for_act")
                t.wait("act_for_dve")
                t.step(nc.vector.reciprocal(rt, rt))
                t.step(ts(rt, rt, 1.0 - LAM_INIT[la], None, mul))
                yv = A[:, 12288:16384].rearrange("p (u n) -> p u n", n=P)
                t.out(tt(yv, yv, bc(rt, 2, P), mul), "dve_for_pe")
                outputs_back(lambda k: pc(p + "da_g", k))
                say("dve_for_pe")
                merge(p + "da", G2, nq, False)
                say("dve_for_pe")
                merge(p + "fn", G2, nq, False)
                say("dve_for_pe")
                for j in range(2):
                    st = ST[p + "out"]
                    for c in range(4):
                        dve.wait_ge(S["tile_done"], st.done0 + 4 * j + c + 1)
                        k = 4 * j + c
                        for s in range(nq // T):
                            cols = slice(s * T, (s + 1) * T)
                            ins = stt(X2[:, k, cols], bank[c][:, cols], a3[:, 16 + k, s:s + 1], X2[:, k, cols], mul, add)
                            if s < nq // T - 1:
                                t.step(ins)
                        ins.then_inc(S["dve_out"], 1)
                        dve.wait_ge(S["dve_out"], st.dve0 + 4 * j + c + 1)
                say("x_ready")
                norm_mod(X2, H2, nq, 1)
                ffn(p + "ffn", X2, nq, gate=lambda k, s: a3[:, 40 + k, s:s + 1])
                if la == 1:
                    say("x_ready")
            norm(X2, H1, T, "final_g")
            say("dve_for_act")



def constants():
    import numpy as np
    f = np.float32
    common = np.zeros((P, C_COMMON), f)
    common[:, 0:128] = np.eye(P)
    common[:, 128:256] = 1.0
    idx = np.arange(P)
    common[:, 256:384] = (idx[:, None] // 64 == idx[None, :] // 64)
    c1 = np.zeros((P, C1_N), f)
    h, tk = idx // CHUNK, idx % CHUNK
    same = h[:, None] == h[None, :]
    r, c = tk[:, None], tk[None, :]
    c1[:, 0:128] = same & (r <= c)
    c1[:, 128:256] = same & (r < c)
    c1[:, 256:384] = same & (c < r)
    c1[:, 384:512] = same & (c < r)
    c1[:, 512:640] = same & (r <= c)
    c1[:, 640:1152] = (h[:, None] == (np.arange(512) // 64)[None, :])
    c1[:, 1152:1408] = (np.arange(T) % CHUNK != 0)[None, :]
    for g, (win, dil) in enumerate(((128, 1), (512, 4), (2048, 16))):
        span = win // dil
        for q in range(2):
            d = (q * P + idx)[:, None] - np.arange(T)[None, :]
            ok = (d >= 0) & (d % dil == 0) & (d // dil <= span)
            c1[:, 1408 + g * 512 + q * T:1408 + g * 512 + (q + 1) * T] = np.where(ok, 0.0, -1e30)
    c2 = np.zeros((P, C2_N), f)
    tok = np.arange(2 * T)
    for d in range(2):
        for s in range(4):
            key = s * P + idx
            key_ctx = (key >= T)[:, None]
            q_ctx = (tok >= T)[None, :]
            order = (key[:, None] <= tok[None, :]) if d == 0 else (key[:, None] >= tok[None, :])
            ok = np.where(key_ctx == q_ctx, order, key_ctx & ~q_ctx)
            c2[:, (4 * d + s) * 512:(4 * d + s + 1) * 512] = np.where(ok, 0.0, -1e30)
    n = np.arange(T)
    ang = 2 * np.pi * ((n[:, None] * n[None, :]) % T) / T
    cos, sin = np.cos(ang) / 16.0, np.sin(ang) / 16.0
    for k in range(2):
        c2[:, 4096 + k * 512:4096 + k * 512 + 256] = cos[k * P:(k + 1) * P]
        c2[:, 4096 + k * 512 + 256:4096 + (k + 1) * 512] = sin[k * P:(k + 1) * P]
        c2[:, 5120 + k * 256:5120 + (k + 1) * 256] = cos[k * P:(k + 1) * P]
        c2[:, 5632 + k * 256:5632 + (k + 1) * 256] = -sin[k * P:(k + 1) * P]
    nf = 16
    inv = (f(10000.0) ** (-np.arange(nf, dtype=f) / f(nf))).astype(f)
    rr = np.repeat(np.arange(T // 64, dtype=f), 64)
    cc = np.tile(np.arange(64, dtype=f), T // 64)
    a = np.concatenate([rr[:, None] * inv, cc[:, None] * inv], axis=-1)
    c2[:, 6144:6400] = np.cos(a).T[idx % 32]
    c2[:, 6400:6656] = np.sin(a).T[idx % 32]
    for m in range(P):
        if m % 64 < 32:
            c2[m + 32, 6656 + m] = -1.0
        else:
            c2[m - 32, 6656 + m] = 1.0
    return common, c1, c2


def layout(inputs):
    import numpy as np
    f = np.float32
    wide, down = [], []

    def cols(w, n0, n1, kt=None):
        k = w.shape[0] // P
        n = (n1 - n0) // P
        return w[:, n0:n1].reshape(k, P, n, P).transpose(1, 2, 0, 3)

    def put(a):
        a = a.reshape(P, -1)
        if a.shape[1] < SLAB:
            a = np.concatenate([a, np.zeros((P, SLAB - a.shape[1]), f)], axis=1)
        wide.append(a)

    def stationary(w):
        for n0 in range(0, w.shape[1], 512):
            put(cols(w, n0, n0 + 512))

    def moving(w, width):
        for n0 in range(0, w.shape[1], width):
            put(w[:, n0:n0 + width].reshape(KT, P, width).transpose(1, 0, 2))

    def ffn(w_in, w_out):
        for j in range(FT // 2):
            put(np.concatenate([cols(w_in, 256 * j, 256 * (j + 1)), cols(w_in, FF + 256 * j, FF + 256 * (j + 1))], axis=1))
        for n in range(KT):
            down.append(cols(w_out, n * P, (n + 1) * P).reshape(P, DOWN))

    def merge(gate, proj):
        for half in range(2):
            put(cols(gate, 512 * half, 512 * (half + 1)))
            put(cols(proj, 512 * half, 512 * (half + 1)))

    g = {k: np.asarray(v) for k, v in inputs.items()}
    ffn(g["ffn1_w_in"][0], g["ffn1_w_out"][0])
    w = g["w_in"][0]
    for n in range(3):
        stationary(w[:, n * D:(n + 1) * D])
    put(cols(np.concatenate([w[:, 3072:3360], np.zeros((D, 96), f)], axis=1), 0, 384))
    wa2 = np.concatenate([g["rwkv_w2"][0], g["rwkv_a2"][0]], axis=0)
    g2 = g["rwkv_g2"][0]
    put(np.concatenate([wa2, g2[0:P], np.concatenate([g2[P:], np.zeros((96, D), f)], axis=0)], axis=1))
    gate0 = 3360 + 3 * 768
    merge(w[:, gate0:gate0 + D], g["w_proj_rwkv"][0])
    stationary(w[:, 3360:3360 + 1536])
    moving(w[:, 3360 + 1536:gate0], 384)
    merge(w[:, gate0 + D:gate0 + 2 * D], g["w_proj_attn"][0])
    stationary(g["w_out"][0])
    ffn(g["ffn2_w_in"][0], g["ffn2_w_out"][0])
    for la in range(2):
        w = g["w_in_2"][la]
        stationary(g["w_ada_2"][la])
        o = 4112
        stationary(w[:, 0:D])
        stationary(w[:, D:2 * D])
        moving(w[:, 2 * D:3 * D], 512)
        stationary(w[:, 3 * D:4 * D])
        gates = w[:, o + 4 * D:o + 7 * D]
        merge(gates[:, 0:D], g["w_br_ml_2"][la])
        stationary(w[:, o:o + D])
        stationary(w[:, o + D:o + 2 * D])
        moving(w[:, o + 2 * D:o + 3 * D], 512)
        merge(gates[:, D:2 * D], g["w_br_da_2"][la])
        moving(w[:, o + 3 * D:o + 4 * D], 512)
        merge(gates[:, 2 * D:3 * D], g["w_br_fn_2"][la])
        stationary(g["w_out_2"][la])
        ffn(g["w_ffn_in_2"][la], g["w_ffn_out_2"][la])

    par = np.zeros((P, NPAR), f)

    def column(name, v):
        n0, n = PCOL[name]
        v = v.reshape(-1)
        if v.size % P:
            v = np.concatenate([v, np.zeros(P - v.size % P, f)])
        par[:, n0:n0 + n] = v.reshape(-1, P).T

    for name, key in (("ffn1_norm", "ffn1_norm"), ("mix_norm", "mix_norm"), ("b_gate", "b_gate"), ("mu", "rwkv_mu"), ("w0", "rwkv_w0"),
                      ("a0", "rwkv_a0"), ("k_k", "rwkv_k_k"), ("k_a", "rwkv_k_a"), ("r_k", "rwkv_r_k"), ("ln_w", "rwkv_ln_w"),
                      ("ln_b", "rwkv_ln_b"), ("ffn2_norm", "ffn2_norm"), ("final_g", "final_g_2")):
        column(name, g[key])
    column("q_norm", np.concatenate([g["attn_q_norm"][0]] * 2))
    column("k_norm", np.concatenate([g["attn_k_norm"][0]] * 2))
    n0 = PCOL["c"][0]
    par[:, n0:n0 + 16:2] = g["c_2"][0].reshape(KT, P).T
    par[:, n0 + 1:n0 + 16:2] = g["c_ctx_2"].reshape(KT, P).T
    for la in range(2):
        column(f"l{la}_b_ada", g["b_ada_2"][la])
        column(f"l{la}_norm_g", g["norm_g_2"][la])
        column(f"l{la}_ml_g", g["ml_head_g_2"][la])
        column(f"l{la}_da_g", g["da_head_g_2"][la])
        n0 = PCOL[f"l{la}_gate_b"][0]
        for n in range(4):
            par[32 * n:32 * n + 4, n0] = g["ml_gate_b_2"][la][4 * n:4 * n + 4]
        n0 = PCOL[f"l{la}_lam"][0]
        par[0:64, n0:n0 + 4] = g["da_lam_2"][la].T
        n0 = PCOL[f"l{la}_gate_w"][0]
        par[:, n0:n0 + 128] = g["w_in_2"][la][:, 4096:4112].reshape(KT, P, 16).transpose(1, 0, 2).reshape(P, 128)
    assert len(wide) == N_WIDE and len(down) == N_DOWN, (len(wide), N_WIDE, len(down), N_DOWN)
    xT = g["x"][0].T.reshape(KT, P, T).transpose(1, 0, 2)
    cT = g["ctx_2"][0].T.reshape(KT, P, T).transpose(1, 0, 2)
    return xT, cT, np.stack(wide), np.stack(down), par


def kernel(**inputs):
    import numpy as _np
    import concourse.bacc as _bacc
    from concourse import mybir as _mybir
    from concourse.bass_utils import run_bass_kernel_spmd as _run

    nc = _bacc.Bacc("TRN2", target_bir_lowering=False, num_devices=1)
    names = ["x_T", "ctx_T", "wide_slabs", "down_slabs", "params", "common_consts", "first_consts", "second_consts"]
    data = list(layout(inputs)) + list(constants())
    arrays, args = {}, []
    for name, a in zip(names, data):
        a = _np.ascontiguousarray(a)
        arrays[name + "_dram"] = a
        args.append(nc.dram_tensor(name + "_dram", a.shape, _mybir.dt.from_np(a.dtype), kind="ExternalInput").ap())
    args.append(nc.dram_tensor("out_dram", (P, KT, T), _mybir.dt.float32, kind="ExternalOutput").ap())
    program(nc, *args)
    r = _run(nc, [arrays], core_ids=[0])
    y = r.results[0]["out_dram"]
    return y.transpose(2, 1, 0).reshape(1, T, D)
```

```python
import math
from contextlib import ExitStack

import concourse.bass as bass
from concourse import mybir

F32 = mybir.dt.float32
ALU = mybir.AluOpType
ACT = mybir.ActivationFunctionType
AX = mybir.AxisListType

P = 128
D = 1024
KT = D // P
T = 256
FF = 2816
FT = FF // P
SLOTS = 3
SLAB = 32 * P
DOWN = FT * P
CHUNK = 16
NCH = T // CHUNK
LAM_INIT = [0.8 - 0.6 * math.exp(-0.3 * layer) for layer in range(2)]
EPS = 1e-6
GN_EPS = 64e-5



def stage_list():
    out = []

    def add(name, slabs, done, act, dve, down=False):
        out.append((name, slabs, DOWN if down else SLAB, done, act, dve))

    def ffn(name):
        add(name + "_up", FT // 2, 4, 0, 2)
        add(name + "_down", KT, 1, 0, 1, down=True)

    def merge(name):
        for half in range(2):
            add(f"{name}_gate{half}", 1, 4, 4, 0)
            add(f"{name}_proj{half}", 1, 4, 0, 4)

    def gates(name):
        for half in range(2):
            add(f"{name}_gate{half}", 1, 4, 4, 0)

    def projections(name):
        for half in range(2):
            add(f"{name}_proj{half}", 1, 4, 0, 4)

    ffn("ffn1")
    for n in ("r", "k", "v"):
        add("rwkv_" + n, 2, 4, 4, 0)
    add("rwkv_lora_in", 1, 3, 3, 0)
    add("rwkv_lora_out", 1, 24, 24, 0)
    gates("rwkv")
    add("ada", 24, 1, 0, 0)
    add("dil_qk", 3, 4, 4, 0)
    add("dil_v", 2, 2, 2, 0)
    projections("rwkv")
    gates("dil")
    projections("dil")
    add("mix_out", 2, 4, 0, 4)
    ffn("ffn2")
    for la in range(2):
        p = f"l{la}_"
        for n in ("q", "k", "v"):
            add(p + "ml_" + n, 2, 4, 4, 0)
        add(p + "ml_o", 2, 4, 4, 0)
        merge(p + "ml")
        for n in ("q", "k", "v"):
            add(p + "da_" + n, 2, 4, 4, 0)
        merge(p + "da")
        add(p + "fn", 2, 4 if la == 0 else 2, 4 if la == 0 else 2, 0)
        merge(p + "fn")
        add(p + "out", 2, 4, 0, 4)
        ffn(p + "ffn")
    return out


class Stage:

    def __init__(self, name, slabs, words, done, act, dve, slab0, wide0, down0, done0, act0, dve0):
        self.name, self.slabs, self.words, self.done, self.act, self.dve = name, slabs, words, done, act, dve
        self.slab0, self.wide0, self.down0 = slab0, wide0, down0
        self.done0, self.act0, self.dve0 = done0, act0, dve0
        self.done_end = done0 + slabs * done
        self.act_end = act0 + slabs * act
        self.dve_end = dve0 + slabs * dve

    def slot(self, j):
        return (self.slab0 + j) % SLOTS

    def landed(self, j, i):
        return ((self.slab0 + j) // SLOTS + 1 + i) * 16


def make_stages():
    st, order = {}, []
    slab = wide = down = done = act = dve = 0
    for name, n, words, d, a, v in stage_list():
        s = Stage(name, n, words, d, a, v, slab, wide, down, done, act, dve)
        st[name] = s
        order.append(s)
        slab += n
        wide += n if words == SLAB else 0
        down += n if words == DOWN else 0
        done, act, dve = s.done_end, s.act_end, s.dve_end
    return st, order


ST, ORDER = make_stages()
N_WIDE = sum(s.slabs for s in ORDER if s.words == SLAB)
N_DOWN = sum(s.slabs for s in ORDER if s.words == DOWN)


def over_slabs(eng, n, body, peel):
    for j in range(min(peel, n)):
        body(j, 0)
    full = max(n - peel, 0) // SLOTS
    if full > 1:
        with eng.Fori(0, full) as i:
            for j in range(SLOTS):
                body(peel + j, i)
    elif full == 1:
        for j in range(SLOTS):
            body(peel + j, 0)
    for j in range(peel + full * SLOTS, n):
        body(j, 0)


class Tally:

    def __init__(self, eng, sems, own):
        self.eng, self.sems, self.own = eng, sems, own
        self.n, self.i, self.per, self.start = {}, None, {}, {}

    def at(self, name):
        v = self.n.get(name, 0)
        if self.i is None:
            return v
        assert name in self.per, name
        return v + self.i * self.per[name]

    def wait(self, name, k=1):
        self.n[name] = self.n.get(name, 0) + k
        self.eng.wait_ge(self.sems[name], self.at(name))

    def step(self, ins):
        ins.then_inc(self.sems[self.own], 1)
        self.wait(self.own)

    def out(self, ins, name):
        ins.then_inc(self.sems[name], 1)
        self.wait(name)

    def skip(self, name, k=1):
        self.n[name] = self.n.get(name, 0) + k

    def loop(self, i, per):
        self.i, self.per, self.start = i, per, dict(self.n)

    def end(self, iters):
        for name, per in self.per.items():
            assert self.n.get(name, 0) - self.start.get(name, 0) == per, (name, per, self.n.get(name, 0), self.start.get(name, 0))
            self.n[name] = self.start.get(name, 0) + per * iters
        for name in self.n:
            assert name in self.per or self.n[name] == self.start.get(name, 0), name
        self.i = None


PCOL = {}


def param_columns():
    n = 0
    spec = [("ffn1_norm", 8), ("mix_norm", 8), ("b_gate", 16), ("mu", 27), ("w0", 8), ("a0", 8), ("k_k", 8), ("k_a", 8),
            ("r_k", 8), ("ln_w", 8), ("ln_b", 8), ("q_norm", 1), ("k_norm", 1), ("ffn2_norm", 8), ("final_g", 8),
            ("c", 16), ("b_ada", 96)]
    for la in range(2):
        spec += [(f"l{la}_norm_g", 16), (f"l{la}_ml_g", 8), (f"l{la}_da_g", 8),
                 (f"l{la}_gate_b", 1), (f"l{la}_lam", 4), (f"l{la}_gate_w", 128)]
    for name, k in spec:
        PCOL[name] = (n, k)
        n += k
    return n


NPAR = param_columns()
CC = {"ident": 0, "ones": 128, "pair": 256}
C_COMMON = 384
C1 = {"gram": 0, "ark": 512, "head": 640, "reset": 1152, "dil": 1408}
C1_N = 1408 + 1536
C2 = {"ml": 0, "dft_t": 1792, "dft_c": 2816, "cos": 3840, "sin": 4096, "perm": 4352}
C2_N = 4480
CHUNK_WORDS = 2560


def program(nc, x_in, ctx_in, wide_in, down_in, par_in, const_in, const1_in, const2_in, out, dbg=None):
    with ExitStack() as ctx:
        sem_names = [
            "landed0", "landed1", "landed2", "loads", "block2_free", "consts2", "out_done",
            "tile_done", "act_out", "dve_out", "silu_ready",
            "act_steps", "dve_steps",
            "squares_ready", "sums_ready", "means_ready", "roots_ready", "h_ready", "x_ready",
            "shift_done", "lora_ready", "rwkv_in_ready",
            "pe_for_act", "pe_for_dve", "act_for_pe", "act_for_dve", "dve_for_pe", "dve_for_act",
            "chunk_staged", "tok_psum", "tok_ready", "gram_psum", "gram_ready", "pow_psum", "pow_ready",
            "scan_psum", "u_ready", "o_psum", "outputs_taken", "chunk_free",
            "scaled", "cond_ready", "ml_args", "ml_exps", "ml_weights", "ada_rows", "ada_psum", "ada_free",
            "scores", "probs_in", "probs", "pt_psum", "pt_ready", "pv_psum", "pv_out", "weights_out",
        ]
        S = {n: ctx.enter_context(nc.semaphore(n)) for n in sem_names}

        def sb(name, n):
            return ctx.enter_context(nc.sbuf_tensor(name, [P, n], F32))

        ring = sb("weights", SLOTS * SLAB)
        par = sb("params", NPAR)
        com = sb("common", C_COMMON)
        C = sb("masks", max(C2_N, C1_N + CHUNK_WORDS))
        X = sb("x_T", KT * 2 * T)
        H = sb("h_T", KT * 2 * T)
        G = sb("merged_T", KT * 2 * T)
        A = sb("arena", 20480)
        small = sb("small", 400)
        ada_all = sb("modulation", 2 * 96)
        ada_row = sb("modulation_row", 512)
        cond = sb("conditions", 16)
        bank = [ctx.enter_context(nc.psum_tensor(f"bank{b}", [P, 512], F32)) for b in range(8)]

        ident, ones, pair = com[:, 0:128], com[:, 128:256], com[:, 256:384]

        def pc(name, k=0, n=1):
            base = PCOL[name][0]
            return par[:, base + k:base + k + n]

        def tiles(buf, base, n, width):
            return buf[:, base:base + n * width].rearrange("p (k t) -> p k t", k=n)

        def bc(ap, dim, n):
            shape = list(ap.shape)
            shape.insert(dim, n)
            return ap.unsqueeze(dim).to_broadcast(shape)

        X1, H1, G1 = tiles(X, 0, KT, T), tiles(H, 0, KT, T), tiles(G, 0, KT, T)
        X2, H2, G2 = tiles(X, 0, KT, 2 * T), tiles(H, 0, KT, 2 * T), tiles(G, 0, KT, 2 * T)
        HALF = KT * T

        def wtile(st, j, q, n=P):
            base = st.slot(j) * SLAB + q * P
            return ring[:, base:base + n]

        def slot(k):
            return A[:, k * HALF:(k + 1) * HALF]

        def slot3(k):
            return slot(k).rearrange("p (k t) -> p k t", k=KT)

        sR, sA, sB, sK, sBH, sKH, sV, sL, sAA, sG = range(10)
        dec = small[:, 0:128]
        gs = small[:, 224:256]
        lam = small[:, 256:260]
        stat = small[:, 260:400]

        def used_by(slab):
            for st in ORDER:
                if slab < st.slab0 + st.slabs:
                    return st.done0 + (slab - st.slab0 + 1) * st.done
            raise AssertionError

        def ml_keys(d, q):
            if q < 2:
                own = list(range(0, q + 1)) if d == 0 else list(range(q, 2))
                return own + [2, 3]
            return list(range(2, q + 1)) if d == 0 else list(range(q, 4))

        def token_outputs_back(t, transpose, base, qtiles, nf):
            y = tiles(A, base, 4, D)
            t.wait("dve_for_pe")
            for k in range(nf):
                if k >= 4:
                    t.wait("dve_for_pe")
                for q in range(qtiles):
                    last = transpose(bank[4 + k % 4][:, q * P:(q + 1) * P], y[:, q, k * P:(k + 1) * P])
                last.then_inc(S["pe_for_dve"], 1)
            t.wait("dve_for_pe", 4)

        ROWS_X = A[:, 16400:16912]
        ROWS_L = A[:, 16912:17424]
        ROWS_B = A[:, 17424:17936]
        ROWS_GI = A[:, 17936:18448]
        ROWS_NCM = A[:, 18448:18960]
        ROWS_EM = A[:, 18960:19472]
        ROWS_1 = A[:, 19472:19984]
        ML_COLS = A[:, 19984:20048].rearrange("p (n c d h) -> p n c d h", n=2, c=4, d=2)
        small_c = cond[:, :].rearrange("p (k s) -> p k s", k=KT)
        lam_in = small[:, 16:18]
        Y_ML = 12304

        def rows_gi_em(n):
            return (ROWS_GI, ROWS_EM)[n]

        ROWS0 = 16400

        PV_DA = [12 + 8 * 4, 12 + 2 * 8 * 4 + 8 * 2]

        def DA_P(n, m=0):
            base = 16384 + (n % 3) * 1024 + m * 512
            return A[:, base:base + 512]

        def DIL_P(h):
            return A[:, 10752 + (h % 3) * 512:10752 + (h % 3) * 512 + 512].rearrange("p (q k) -> p q k", q=2)

        def DIL_PT(h):
            return A[:, 12288 + (h % 2) * 512:12288 + (h % 2) * 512 + 512]

        DIL_GATES = 18432

        def DA_PT(n):
            return A[:, 19456 + (n % 2) * 512:19456 + (n % 2) * 512 + 512]

        def G_SQ(la):
            return A[:, 0:4096]

        block = ctx.enter_context(nc.Block())

        @block.sync
        def _(sp):
            sp.dma_start(X1, x_in).then_inc(S["loads"], 16)
            sp.dma_start(par[:, :], par_in).then_inc(S["loads"], 16)
            sp.dma_start(com[:, :], const_in).then_inc(S["loads"], 16)
            sp.dma_start(C[:, 0:C1_N], const1_in).then_inc(S["loads"], 16)
            for n, st in enumerate(ORDER):
                if st.name == "mix_out":
                    sp.wait_ge(S["block2_free"], 1)
                    sp.dma_start(C[:, 0:C2_N], const2_in).then_inc(S["consts2"], 16)
                    sp.dma_start(tiles(G, HALF, KT, T), ctx_in).then_inc(S["consts2"], 16)

                def load(j, i, st=st):
                    if st.slab0 + j >= SLOTS:
                        sp.wait_ge(S["tile_done"], used_by(st.slab0 + j - SLOTS) + i * SLOTS * st.done)
                    src = (wide_in, st.wide0) if st.words == SLAB else (down_in, st.down0)
                    base = st.slot(j) * SLAB
                    k = src[1] + j + i * SLOTS
                    view = src[0][bass.ds(k, 1)].rearrange("a p n -> (a p) n")
                    sp.dma_start(ring[:, base:base + st.words], view).then_inc(S[f"landed{st.slot(j)}"], 16)

                over_slabs(sp, st.slabs, load, SLOTS)

        @block.tensor
        def _(pe):
            t = Tally(pe, S, None)
            mm = nc.tensor.matmul

            def matmul(out, lhsT, rhs, start=True, stop=True):
                return mm(out, lhsT, rhs, start=start, stop=stop, skip_group_check=True)

            def transpose(out, in_):
                return nc.tensor.transpose(out, in_, ident[0:in_.shape[0], 0:in_.shape[0]])

            def enter(st):
                if st.act0:
                    pe.wait_ge(S["act_out"], st.act0)
                if st.dve0:
                    pe.wait_ge(S["dve_out"], st.dve0)

            def arrived(st, j, i=0):
                pe.wait_ge(S[f"landed{st.slot(j)}"], st.landed(j, i))

            def project(st, rhs, n, kt=KT, drains=None, part=(0, 4)):
                enter(st)

                def body(j, i):
                    arrived(st, j, i)
                    for c in range(*part):
                        if j >= 1:
                            name, pos = drains[c]
                            per = st.act if name == "act_out" else st.dve
                            base = st.act0 if name == "act_out" else st.dve0
                            pe.wait_ge(S[name], base + per * (j - 1) + pos + 1 + i * (SLOTS * per))
                        for k in range(kt):
                            last = matmul(bank[c][:, 0:n], wtile(st, j, c * kt + k), rhs(k), start=k == 0, stop=k == kt - 1)
                        last.then_inc(S["tile_done"], 1)

                over_slabs(pe, st.slabs, body, 1)

            by_act = [("act_out", c) for c in range(4)]
            by_dve = [("dve_out", c) for c in range(4)]
            by_pairs = [("dve_out", c % 2) for c in range(4)]

            def project_tokens(st, lhs, n_tok, width, groups=4):
                enter(st)
                for j in range(st.slabs):
                    arrived(st, j)
                    for q in range(n_tok):
                        if j >= 1:
                            name = "act_out" if st.act else "dve_out"
                            base, per = (st.act0, st.act) if st.act else (st.dve0, st.dve)
                            pe.wait_ge(S[name], base + per * (j - 1) + q + 1)
                        for k in range(KT):
                            last = matmul(bank[q][:, 0:width], lhs(k, q), wtile(st, j, 0, KT * width)[:, k * width:(k + 1) * width],
                                          start=k == 0, stop=k == KT - 1)
                        last.then_inc(S["tile_done"], 1)

            def norm_sums(width, buf, signals=1):
                sq = tiles(buf, 0, KT, width)
                for k in range(KT):
                    t.wait("squares_ready")
                    last = matmul(bank[4][:, 0:width], ones, sq[:, k], start=k == 0, stop=k == KT - 1)
                last.then_inc(S["sums_ready"], 1)
                t.wait("h_ready", signals)

            def ffn(name, h, width):
                project(ST[name + "_up"], lambda k: h[:, k, 0:width], width, drains=by_pairs)
                st = ST[name + "_down"]
                hid = tiles(A, 0, FT, width)
                enter(st)

                def body(j, i):
                    arrived(st, j, i)
                    b = j % SLOTS
                    if j >= SLOTS:
                        pe.wait_ge(S["dve_out"], st.dve0 + j - SLOTS + 1 + i * SLOTS)
                    for k in range(FT):
                        last = matmul(bank[b][:, 0:width], wtile(st, j, k), hid[:, k], start=k == 0, stop=k == FT - 1)
                    last.then_inc(S["tile_done"], 1)

                over_slabs(pe, st.slabs, body, SLOTS)

            def gate(name, half, part=(0, 4)):
                project(ST[f"{name}_gate{half}"], lambda k: H1[:, k], T, drains=by_act, part=part)

            def branch_projections(name, y, kt=KT):
                t.wait("dve_for_pe")
                for half in range(2):
                    project(ST[f"{name}_proj{half}"], lambda k: y[:, k], T, kt=kt, drains=by_dve)

            def merge(name, h, y, width, kt=KT, output=None):
                for half in range(2):
                    project(ST[f"{name}_gate{half}"], lambda k: h[:, k, 0:width], width, drains=by_act)
                    if half == 0:
                        if output:
                            output()
                        t.wait("dve_for_pe")
                    project(ST[f"{name}_proj{half}"], lambda k: y[:, k, 0:width], width, kt=kt, drains=by_dve)

            pe.wait_ge(S["loads"], 64)
            norm_sums(T, A)
            ffn("ffn1", H1, T)
            norm_sums(T, G)
            for n in ("r", "k", "v"):
                project(ST["rwkv_" + n], lambda k: H1[:, k], T, drains=by_act)
            st = ST["rwkv_lora_in"]
            enter(st)
            arrived(st, 0)
            for c in range(3):
                for k in range(KT):
                    last = matmul(bank[c][:, 0:T], wtile(st, 0, c * KT + k), H1[:, k], start=k == 0, stop=k == KT - 1)
                last.then_inc(S["tile_done"], 1)

            def head_sums(ready, done):
                t.wait(ready)
                for b in range(4):
                    last = matmul(bank[4 + b][:, :], pair, slot(sKH)[:, b * 512:(b + 1) * 512])
                last.then_inc(S[done], 1)

            head_sums("act_for_pe", "pe_for_act")
            st = ST["rwkv_lora_out"]
            enter(st)
            arrived(st, 0)
            t.wait("lora_ready")
            lora = tiles(A, sBH * HALF, 3, T)
            for j in range(KT):
                for c in range(3):
                    q = 3 * j + c
                    if q >= 4:
                        pe.wait_ge(S["act_out"], st.act0 + q - 3)
                    cols = ring[:, st.slot(0) * SLAB:st.slot(0) * SLAB + 3 * D].rearrange("p (a n) -> p a n", a=3)[:, :, j * P:(j + 1) * P]
                    dst = bank[q % 4][:, 0:T]
                    if c == 0:
                        last = matmul(dst, cols[0:64, 0], lora[0:64, 0])
                    elif c == 1:
                        last = matmul(dst, cols[64:128, 0], lora[64:128, 0])
                    else:
                        matmul(dst, cols[:, 1], lora[:, 1], stop=False)
                        last = matmul(dst, cols[0:32, 2], lora[0:32, 2], start=False)
                    last.then_inc(S["tile_done"], 1)
            gate("rwkv", 0)
            head_sums("dve_for_pe", "pe_for_dve")
            gate("rwkv", 1)
            stg = X[:, HALF:HALF + 896].rearrange("p (a c) -> p a c", a=7)
            tok = X[:, HALF + 896:HALF + 1408].rearrange("p (a c) -> p a c", a=4)
            gram = H[:, HALF:HALF + 1024].rearrange("p (g a c) -> p g a c", g=2, a=4)
            ark = H[:, HALF + 1024:HALF + 1280].rearrange("p (g c) -> p g c", g=2)
            mt = H[:, HALF + 1280:HALF + 1536].rearrange("p (g c) -> p g c", g=2)
            q8 = H[:, HALF + 1536:HALF + 1792].rearrange("p (g c) -> p g c", g=2)
            p2 = G[:, HALF:HALF + 512].rearrange("p (g a c) -> p g a c", g=2, a=2)
            p4 = G[:, HALF + 512:HALF + 1024].rearrange("p (g a c) -> p g a c", g=2, a=2)
            wn = G[:, HALF + 1024:HALF + 1408].rearrange("p (a c) -> p a c", a=3)
            vb = C[:, C1_N:C1_N + 1024].rearrange("p (g n) -> p g n", g=2)
            ub = C[:, C1_N + 1024:C1_N + 2048].rearrange("p (g n) -> p g n", g=2)
            state = C[:, C1_N + 2048:C1_N + 2560]
            t.wait("rwkv_in_ready")
            ada_st = ST["ada"]

            def ada_products(j, i, k0):
                if k0 == 0:
                    arrived(ada_st, j, i)
                    t.wait("ada_free")
                for k in (k0, k0 + 1):
                    last = matmul(bank[7][0:2, :], small_c[:, k], ring[:, ada_st.slot(j) * SLAB + k * 512:ada_st.slot(j) * SLAB + (k + 1) * 512],
                                  start=k == 0, stop=k == KT - 1)
                if k0 == KT - 2:
                    last.then_inc(S["tile_done"], 1)

            def ada_columns():
                t.wait("ada_rows")
                for c in range(4):
                    last = matmul(bank[7][:, 2 * c:2 * c + 2], ada_row[0:2, c * P:(c + 1) * P], ident[0:2, 0:2])
                last.then_inc(S["ada_psum"], 1)

            def meanwhile(point, i):
                for first in (0, 5, 10):
                    if point == first + 5:
                        ada_columns()
                for j, first in enumerate((0, 5, 10)):
                    if first <= point < first + 4:
                        ada_products(j, i, 2 * (point - first))

            pe.wait_ge(S["cond_ready"], 1)
            enter(ada_st)
            with pe.Fori(0, NCH // 2) as i:
                t.loop(i, {"chunk_staged": 2, "tok_ready": 2, "gram_ready": 2, "pow_ready": 14, "u_ready": 2,
                           "ada_free": 3, "ada_rows": 3})
                for half in range(2):
                    t.wait("chunk_staged")
                    for n, a in enumerate((1, 4, 5, 6)):
                        last = transpose(bank[6][:, n * P:(n + 1) * P], stg[:, a])
                    last.then_inc(S["tok_psum"], 1)
                    for g in range(2):
                        lo = 64 * g
                        rows = slice(lo, lo + 64)
                        matmul(bank[g][:, 0:256], stg[rows, 2], X[rows, HALF:HALF + 256])
                        last = matmul(bank[g][:, 256:512], stg[rows, 1], X[rows, HALF + 256:HALF + 512])
                    last.then_inc(S["gram_psum"], 1)
                    meanwhile(8 * half + 0, i)
                    t.wait("gram_ready")
                    for g in range(2):
                        matmul(bank[5][:, g * 256:g * 256 + 128], gram[:, g, 2], gram[:, g, 1])
                        last = matmul(bank[5][:, g * 256 + 128:g * 256 + 256], gram[:, g, 1], gram[:, g, 2])
                    last.then_inc(S["pow_psum"], 1)
                    for g in range(2):
                        rows = slice(64 * g, 64 * g + 64)
                        matmul(bank[2 + g][:, 0:P], stg[rows, 3], stg[rows, 0])
                    meanwhile(8 * half + 1, i)
                    t.wait("pow_ready")
                    t.wait("tok_ready")
                    for g in range(2):
                        last = matmul(bank[6][:, g * P:(g + 1) * P], p2[:, g, 1], mt[:, g])
                    last.then_inc(S["pow_psum"], 1)
                    for g in range(2):
                        matmul(bank[5][:, g * 256:g * 256 + 128], p2[:, g, 1], p2[:, g, 0])
                        last = matmul(bank[5][:, g * 256 + 128:g * 256 + 256], p2[:, g, 0], p2[:, g, 1])
                    last.then_inc(S["pow_psum"], 1)
                    meanwhile(8 * half + 2, i)
                    t.wait("pow_ready", 2)
                    for g in range(2):
                        last = matmul(bank[6][:, g * P:(g + 1) * P], p4[:, g, 1], mt[:, g])
                    last.then_inc(S["pow_psum"], 1)
                    for g in range(2):
                        last = matmul(bank[4][:, g * P:(g + 1) * P], p4[:, g, 0], p4[:, g, 1])
                    last.then_inc(S["pow_psum"], 1)
                    meanwhile(8 * half + 3, i)
                    t.wait("pow_ready", 2)
                    for g in range(2):
                        last = matmul(bank[6][:, g * P:(g + 1) * P], q8[:, g], mt[:, g])
                    last.then_inc(S["pow_psum"], 1)
                    meanwhile(8 * half + 4, i)
                    t.wait("pow_ready")
                    for g in range(2):
                        matmul(bank[5][64 * g:64 * g + 64, 0:P], tok[:, 0, 64 * g:64 * g + 64], mt[:, g])
                    for g in range(2):
                        last = matmul(bank[5][:, (1 + g) * P:(2 + g) * P], gram[:, g, 3], mt[:, g])
                    last.then_inc(S["pow_psum"], 1)
                    meanwhile(8 * half + 5, i)
                    t.wait("pow_ready")
                    for g in range(2):
                        rows = slice(64 * g, 64 * g + 64)
                        matmul(bank[g][:, :], wn[rows, 0], state[rows, :], stop=False)
                        last = matmul(bank[g][:, :], wn[:, 1 + g], vb[:, g], start=False)
                    last.then_inc(S["scan_psum"], 1)
                    for g in range(2):
                        rows = slice(64 * g, 64 * g + 64)
                        matmul(bank[2 + g][:, :], stg[rows, 0], state[rows, :], stop=False)
                        matmul(bank[2 + g][:, :], ark[:, g], vb[:, g], start=False, stop=False)
                    meanwhile(8 * half + 6, i)
                    t.wait("u_ready")
                    for g in range(2):
                        rows = slice(64 * g, 64 * g + 64)
                        matmul(bank[4][rows, :], tok[:, 1, rows], ub[:, g], stop=False)
                        matmul(bank[4][rows, :], tok[:, 2, rows], vb[:, g], start=False)
                        last = matmul(bank[2 + g][:, :], gram[:, g, 0], ub[:, g], start=False)
                    last.then_inc(S["o_psum"], 1)
                    meanwhile(8 * half + 7, i)
            t.end(NCH // 2)
            t.wait("outputs_taken")
            qk = tiles(A, 3072, 12, T)
            project(ST["dil_qk"], lambda k: H1[:, k], T, drains=by_act)
            t.wait("dve_for_pe")
            o_tok = slot(sL).rearrange("p (c f) -> p c f", c=NCH)
            for b in range(4):
                for c in range(4):
                    last = transpose(bank[4 + b][:, c * P:(c + 1) * P], o_tok[:, 4 * b + c])
            last.then_inc(S["pe_for_dve"], 1)
            project_tokens(ST["dil_v"], lambda k, q: H1[:, k, q * P:(q + 1) * P], 2, 384)
            branch_projections("rwkv", slot3(sR))

            v1 = tiles(A, 6144, 2, 768)
            for half in range(2):
                if half == 0:
                    t.wait("act_for_pe")
                else:
                    t.wait("dve_for_pe")
                for b in range(3):
                    src = A[:, 7680 + (3 * half + b) * 512:7680 + (3 * half + b + 1) * 512]
                    last = matmul(bank[4 + b][:, :], pair, src)
                last.then_inc(S["pe_for_dve"], 1)
                gate("dil", 0, part=(2 * half, 2 * half + 2))
            t.wait("dve_for_pe")
            y1 = tiles(A, 13824, 2, 768)

            def dil_scores(h):
                if h >= 2:
                    t.wait("probs_in")
                rows = slice(64 * (h % 2), 64 * (h % 2) + 64)
                for q in range(2):
                    last = matmul(bank[h % 2][:, q * T:(q + 1) * T], qk[rows, h // 2, q * P:(q + 1) * P], qk[rows, 6 + h // 2])
                last.then_inc(S["scores"], 1)

            def dil_turn(h):
                t.wait("probs")
                for q in range(2):
                    for k in range(2):
                        last = transpose(bank[4 + h % 2][:, (2 * q + k) * P:(2 * q + k + 1) * P], DIL_P(h)[:, q, k * P:(k + 1) * P])
                last.then_inc(S["pt_psum"], 1)

            def dil_values(h):
                pt = DIL_PT(h).rearrange("p (q k) -> p q k", q=2)
                t.wait("pt_ready")
                if h >= 2:
                    t.wait("pv_out")
                for q in range(2):
                    for k in range(2):
                        last = matmul(bank[6 + h % 2][:, q * 64:(q + 1) * 64], pt[:, q, k * P:(k + 1) * P], v1[:, k, h * 64:(h + 1) * 64],
                                      start=k == 0, stop=k == 1)
                last.then_inc(S["pv_psum"], 1)

            for h in range(15):
                if h < 12:
                    dil_scores(h)
                if 2 <= h < 14:
                    dil_turn(h - 2)
                if h >= 3:
                    dil_values(h - 3)
            t.wait("probs_in", 2)
            t.wait("pv_out", 2)
            gate("dil", 1)
            t.wait("dve_for_pe")
            for q in range(2):
                for b in range(2):
                    for c in range(3):
                        last = transpose(bank[4 + 2 * q + b][:, c * P:(c + 1) * P], y1[:, q, (3 * b + c) * P:(3 * b + c + 1) * P])
            last.then_inc(S["pe_for_dve"], 1)
            branch_projections("dil", tiles(A, 0, 6, T), kt=6)
            pe.wait_ge(S["dve_out"], ST["mix_out"].dve0)
            t.wait("dve_for_pe")
            project(ST["mix_out"], lambda k: G1[:, k], T, drains=by_dve)
            norm_sums(T, A)
            ffn("ffn2", H1, T)

            pe.wait_ge(S["consts2"], 32)
            for la in range(2):
                nq = 2 * T if la == 0 else T
                p = f"l{la}_"
                qtiles = nq // P
                t.wait("dve_for_pe")
                matmul(bank[5][:, 0:2], ones[0:64, :], lam_in[0:64, :]).then_inc(S["pe_for_act"], 1)
                norm_sums(2 * T, G, signals=2 * KT)
                t.wait("dve_for_pe")
                gw = tiles(G, 0, KT, P)
                for k in range(KT):
                    last = matmul(bank[4][:, :], gw[:, k], H2[:, k], start=k == 0, stop=k == KT - 1)
                last.then_inc(S["pe_for_act"], 1)
                project(ST[p + "ml_q"], lambda k: H2[:, k, 0:nq], nq, drains=by_act)
                project(ST[p + "ml_k"], lambda k: H2[:, k], 2 * T, drains=by_act)
                project_tokens(ST[p + "ml_v"], lambda k, q: H2[:, k, q * P:(q + 1) * P], 4, 512)
                t.wait("dve_for_pe")
                for n in range(2):
                    for c in range(4):
                        last = transpose(bank[5 + n][:, c * P:(c + 1) * P], rows_gi_em(n)[:, c * P:(c + 1) * P])
                last.then_inc(S["pe_for_dve"], 1)
                t.wait("dve_for_pe")
                qT, kT = tiles(A, 0, KT, 2 * T), tiles(A, 4096, KT, 2 * T)
                v2 = A[:, 8192:8192 + 4 * 1028].rearrange("p (s n) -> p s n", s=4)

                def ml_shift_row(h, d):
                    r = 64 * d + h
                    matmul(bank[d][:, 0:nq], ident[:, r:r + 1].to_broadcast([P, P]), ROWS_NCM[:, 0:nq]).then_inc(S["scores"], 1)

                def ml_scores(h, s):
                    for kk in range(2):
                        last = matmul(bank[4 + s][:, 0:nq], kT[:, 2 * h + kk, s * P:(s + 1) * P], qT[:, 2 * h + kk, 0:nq],
                                      start=kk == 0, stop=kk == 1)
                    last.then_inc(S["scores"], 1)

                def ml_values(h, d):
                    at = G[:, d * 2048:(d + 1) * 2048].rearrange("p (s q) -> p s q", s=4)
                    for q in range(qtiles):
                        keys = ml_keys(d, q)
                        if (h, d) != (0, 0) or q >= 2:
                            t.wait("pv_out")
                        for n, s in enumerate(keys):
                            last = matmul(bank[2 + q % 2][:, 0:257], at[:, s, q * P:(q + 1) * P], v2[:, s, h * 257:(h + 1) * 257],
                                          start=n == 0, stop=n == len(keys) - 1)
                        last.then_inc(S["pv_psum"], 1)

                pe.wait_ge(S["act_out"], ST[p + "ml_v"].act_end)
                ml_shift_row(0, 0)
                for s in range(4):
                    ml_scores(0, s)
                ml_shift_row(0, 1)
                for h in range(4):
                    t.wait("ml_weights", 4)
                    ml_values(h, 0)
                    if h < 3:
                        ml_shift_row(h + 1, 0)
                    for s in range(4):
                        t.wait("ml_weights")
                        if h < 3:
                            ml_scores(h + 1, s)
                    if h < 3:
                        ml_shift_row(h + 1, 1)
                    ml_values(h, 1)
                t.wait("pv_out", 2)
                project(ST[p + "ml_o"], lambda k: H2[:, k, 0:nq], nq, drains=by_act)
                token_outputs_back(t, transpose, 12304, qtiles, 8)
                merge(p + "ml", H2, tiles(A, 0, KT, 2 * T), nq)
                perm = C[:, C2["perm"]:C2["perm"] + P]

                def rotate(name, src, first):
                    pe.wait_ge(S["act_out"], ST[p + name].act_end)
                    for n in range(4):
                        if not first:
                            t.wait("dve_for_pe")
                        for c in range(2):
                            last = matmul(bank[4 + n][:, c * T:(c + 1) * T], perm, src[:, 2 * n + c, 0:T])
                        last.then_inc(S["pe_for_dve"], 1)

                project(ST[p + "da_q"], lambda k: H2[:, k, 0:nq], nq, drains=by_act)
                rotate("da_q", qT, True)
                project(ST[p + "da_k"], lambda k: H2[:, k], 2 * T, drains=by_act)
                rotate("da_k", kT, False)
                project_tokens(ST[p + "da_v"], lambda k, q: H2[:, k, q * P:(q + 1) * P], 4, 512)
                t.wait("dve_for_pe", 4)
                pe.wait_ge(S["act_out"], ST[p + "da_v"].act_end)
                v3 = tiles(A, 8192, 4, D)
                units = [(h, q) for h in range(8) for q in range(qtiles)]

                def keys_of(q):
                    return (0, 4) if q < 2 else (2, 4)

                def da_scores(n):
                    h, q = units[n]
                    k0, k1 = keys_of(q)
                    if n >= 2:
                        t.wait("probs_in")
                    for m in range(2):
                        rows = slice(64 * m, 64 * m + 64)
                        last = matmul(bank[4 * m + n % 2][:, 0:(k1 - k0) * P], qT[rows, h, q * P:(q + 1) * P], kT[rows, h, k0 * P:k1 * P])
                    last.then_inc(S["scores"], 1)

                def da_turn(n):
                    h, q = units[n]
                    k0, k1 = keys_of(q)
                    t.wait("probs")
                    pr = DA_P(n)
                    for k in range(k1 - k0):
                        last = transpose(bank[2 + n % 2][:, k * P:(k + 1) * P], pr[:, k * P:(k + 1) * P])
                    last.then_inc(S["pt_psum"], 1)

                def da_values(n):
                    h, q = units[n]
                    k0, k1 = keys_of(q)
                    t.wait("pt_ready")
                    if n >= 2:
                        t.wait("pv_out")
                    for k in range(k1 - k0):
                        last = matmul(bank[6 + n % 2][:, 0:P], DA_PT(n)[:, k * P:(k + 1) * P], v3[:, k0 + k, h * P:(h + 1) * P],
                                      start=k == 0, stop=k == k1 - k0 - 1)
                    last.then_inc(S["pv_psum"], 1)

                for n in range(len(units) + 3):
                    if n < len(units):
                        da_scores(n)
                    if 2 <= n < len(units) + 2:
                        da_turn(n - 2)
                    if n >= 3:
                        da_values(n - 3)
                t.wait("probs_in", 2)
                t.wait("pv_out", 2)
                merge(p + "da", H2, tiles(A, 0, KT, 2 * T), nq,
                      output=lambda: token_outputs_back(t, transpose, 12288, qtiles, 8))
                project_tokens(ST[p + "fn"], lambda k, q: H2[:, k, q * P:(q + 1) * P], qtiles, 512)
                pe.wait_ge(S["act_out"], ST[p + "fn"].act_end)
                z = tiles(A, 4096, 4, D)
                dft_t = tiles(C, C2["dft_t"], 2, 512)
                dft_c = C[:, C2["dft_c"]:C2["dft_c"] + 1024].rearrange("p (f k n) -> p f k n", f=2, k=2)
                zf = A[:, 8192:16384].rearrange("p (k f s t) -> p k f s t", k=KT, f=2, s=2)
                n = 0
                for k in range(KT):
                    for s in range(nq // T):
                        if n >= 4:
                            t.wait("act_for_pe")
                        for tt in range(2):
                            last = matmul(bank[4 + n % 4][:, :], z[:, 2 * s + tt, k * P:(k + 1) * P], dft_t[:, tt], start=tt == 0, stop=tt == 1)
                        last.then_inc(S["pe_for_act"], 1)
                        n += 1
                t.wait("act_for_pe", 4)
                for k in range(KT):
                    grp, half = k // 2, k % 2
                    if k >= 4:
                        t.wait("act_for_pe")
                    for f in range(2):
                        for kk in range(2):
                            last = matmul(bank[4 + k % 4][:, 0:nq], dft_c[:, f, kk, half * P:(half + 1) * P],
                                          zf[:, 2 * grp + kk, f].rearrange("p s t -> p (s t)")[:, 0:nq],
                                          start=f == 0 and kk == 0, stop=f == 1 and kk == 1)
                    last.then_inc(S["pe_for_act"], 1)
                t.wait("act_for_pe", 4)
                merge(p + "fn", H2, tiles(A, 0, KT, 2 * T), nq)
                t.wait("dve_for_pe")
                project(ST[p + "out"], lambda k: G2[:, k, 0:nq], nq, drains=by_dve)
                norm_sums(nq, A, signals=KT * nq // T)
                ffn(p + "ffn", H2, nq)
            norm_sums(T, G)

        @block.scalar
        def _(act):
            t = Tally(act, S, "act_steps")
            af = nc.scalar.activation

            def tiles_of(st, body):
                def one(j, i):
                    for c in range(st.act):
                        act.wait_ge(S["tile_done"], st.done0 + st.done * j + c + 1 + i * (SLOTS * st.done))
                        ins = body(c, j, i)
                        ins.then_inc(S["act_out"], 1)
                        act.wait_ge(S["act_out"], st.act0 + st.act * j + c + 1 + i * (SLOTS * st.act))
                over_slabs(act, st.slabs, one, 0)

            def roots():
                t.wait("means_ready")
                w = mean_width[0]
                t.out(af(A[:, 4096 + w:4096 + 2 * w], A[:, 4096:4096 + w], ACT.Sqrt), "roots_ready")

            mean_width = [T]

            def norm(x, width, buf, after=None):
                sq = tiles(buf, 0, KT, width)
                for k in range(KT):
                    if after:
                        act.wait_ge(S["dve_out"], ST[after].dve0 + k + 1)
                    t.out(af(sq[:, k], x[:, k, 0:width], ACT.Square), "squares_ready")
                mean_width[0] = width
                roots()

            def shifts(h, width, which, la):
                a3 = ada_all[:, la * 96:(la + 1) * 96].rearrange("p (k s) -> p k s", s=2)
                for k in range(KT):
                    for s in range(width // T):
                        cols = slice(s * T, (s + 1) * T)
                        t.wait("scaled")
                        ins = af(h[:, k, cols], h[:, k, cols], ACT.Identity, bias=a3[:, 24 * which + k, s:s + 1])
                        ins.then_inc(S["h_ready"], 1)
                t.skip("h_ready", KT * (width // T))
                act.wait_ge(S["h_ready"], t.at("h_ready"))

            silu_count = [0]

            def ffn(name, width):
                st = ST[name + "_up"]
                base = silu_count[0]
                tmp = tiles(A, FT * 2 * T, 2, width)

                def one(j, i):
                    for c in range(2):
                        act.wait_ge(S["tile_done"], st.done0 + 4 * j + c + 1 + i * (4 * SLOTS))
                        if j >= 1:
                            act.wait_ge(S["dve_out"], st.dve0 + 2 * (j - 1) + c + 1 + i * (2 * SLOTS))
                        af(tmp[:, c], bank[c][:, 0:width], ACT.Silu).then_inc(S["silu_ready"], 1)
                over_slabs(act, st.slabs, one, 1)
                silu_count[0] += 2 * st.slabs

            def gate(name, half, gt, bias, part=(0, 4)):
                st = ST[f"{name}_gate{half}"]
                for c in range(*part):
                    act.wait_ge(S["tile_done"], st.done0 + c + 1)
                    af(gt[:, 4 * half + c], bank[c][:, 0:T], ACT.Sigmoid, bias=pc("b_gate", bias + 4 * half + c)).then_inc(S["act_out"], 1)

            def merge(name, width):
                gt = tiles(A, 16384, 4, 2 * T)
                for half in range(2):
                    st = ST[f"{name}_gate{half}"]
                    act.wait_ge(S["dve_out"], st.dve0)
                    tiles_of(st, lambda c, j, i: af(gt[:, c, 0:width], bank[c][:, 0:width], ACT.Sigmoid))

            act.wait_ge(S["loads"], 64)
            norm(X1, T, A)
            ffn("ffn1", T)
            norm(X1, T, G, after="ffn1_down")
            shift = X[:, HALF:HALF + 4 * 257].rearrange("p (b n) -> p b n", b=4)
            t.wait("dve_for_act")
            n = 0
            for name in ("r", "k", "v", "lora_in"):
                st = ST["rwkv_" + name]
                for j in range(st.slabs):
                    for c in range(st.act):
                        act.wait_ge(S["tile_done"], st.done0 + st.done * j + c + 1)
                        if n >= 4:
                            t.wait("shift_done")
                        af(shift[:, n % 4, 1:257], bank[c][:, 0:T], ACT.Copy).then_inc(S["act_out"], 1)
                        n += 1
            t.wait("shift_done", 4)
            lora = tiles(A, sBH * HALF, 3, T)
            t.step(af(lora[0:64, 0], lora[0:64, 0], ACT.Tanh))
            t.step(af(lora[:, 1], lora[:, 1], ACT.Sigmoid))
            t.out(af(lora[0:32, 2], lora[0:32, 2], ACT.Sigmoid), "lora_ready")
            t.wait("dve_for_act")
            t.out(af(slot(sKH), slot(sA), ACT.Square), "act_for_pe")
            t.wait("pe_for_act")
            for b in range(4):
                ins = af(slot(sB)[:, b * 512:(b + 1) * 512], bank[4 + b][:, :], ACT.Sqrt)
                if b < 3:
                    t.step(ins)
            t.out(ins, "act_for_dve")
            st = ST["rwkv_lora_out"]
            for q in range(24):
                j, c = q // 3, q % 3
                act.wait_ge(S["tile_done"], st.done0 + q + 1)
                src = bank[q % 4][:, 0:T]
                if c == 0:
                    ins = af(slot3(sL)[:, j], src, ACT.Sigmoid, bias=pc("w0", j))
                elif c == 1:
                    ins = af(slot3(sAA)[:, j], src, ACT.Sigmoid, bias=pc("a0", j))
                else:
                    ins = af(slot3(sG)[:, j], src, ACT.Copy)
                ins.then_inc(S["act_out"], 1)
            act.wait_ge(S["act_out"], st.act_end)
            gate("rwkv", 0, G1, 0)
            gate("rwkv", 1, G1, 0)
            t.wait("dve_for_act")
            t.out(af(slot(sBH), slot(sL), ACT.Exp), "act_for_dve")
            t.wait("dve_for_act")
            t.out(af(slot(sKH), slot(sL), ACT.Exp, scale=-1.0), "act_for_dve")
            t.wait("dve_for_act")
            t.out(af(slot(sL), G[:, HALF:2 * HALF], ACT.Exp), "act_for_dve")
            stg = X[:, HALF:HALF + 896]
            tok = X[:, HALF + 896:HALF + 1408]
            q7 = A[:, 0:7 * HALF].rearrange("p (a t) -> p a t", a=7 * KT)
            t.out(af(cond[:, :], pc("c", 0, 16), ACT.Silu), "cond_ready")
            t.wait("rwkv_in_ready")
            ada_st = ST["ada"]

            def ada_out_row(j, i):
                act.wait_ge(S["tile_done"], ada_st.done0 + j + 1 + i * SLOTS)
                t.out(af(ada_row[0:2, :], bank[7][0:2, :], ACT.Copy), "ada_rows")

            with act.Fori(0, NCH // 2) as i:
                t.loop(i, {"chunk_free": 2, "chunk_staged": 2, "tok_psum": 2, "tok_ready": 2, "ada_rows": 3})
                for half in range(2):
                    t.wait("chunk_free")
                    t.out(af(stg.rearrange("p (a t) -> p a t", a=7 * KT), q7[:, :, bass.ds(i * (2 * CHUNK) + half * CHUNK, CHUNK)], ACT.Copy), "chunk_staged")
                    t.wait("tok_psum")
                    t.out(af(tok, bank[6][:, :], ACT.Copy), "tok_ready")
                    for j in ((0,), (1, 2))[half]:
                        ada_out_row(j, i)
            t.end(NCH // 2)
            t.wait("dve_for_act")
            t.out(af(stat[:, 32:64], stat[:, 64:96], ACT.Sqrt), "act_for_dve")
            st = ST["dil_qk"]
            qk = tiles(A, 3072, 12, T)
            act.wait_ge(S["dve_out"], st.dve0)
            for j in range(3):
                for c in range(4):
                    act.wait_ge(S["tile_done"], st.done0 + 4 * j + c + 1)
                    af(qk[:, 4 * j + c], bank[c][:, 0:T], ACT.Copy).then_inc(S["act_out"], 1)
            v1 = tiles(A, 6144, 2, 768)
            tiles_of(ST["dil_v"], lambda c, j, i: af(v1[:, c, j * 384:(j + 1) * 384], bank[c][:, 0:384], ACT.Copy))
            t.out(af(A[:, 7680:10752], A[:, 3072:6144], ACT.Square), "act_for_pe")
            for half in range(2):
                t.wait("dve_for_act")
                t.out(af(A[:, 15360:16896], A[:, 15360:16896], ACT.Sqrt), "act_for_dve")
                gate("dil", 0, tiles(A, DIL_GATES, KT, T), 8, part=(2 * half, 2 * half + 2))
            for n in range(14):
                if n < 12:
                    h = n
                    t.wait("weights_out")
                    for q in range(2):
                        ins = af(DIL_P(h)[:, q], DIL_P(h)[:, q], ACT.Exp, bias=stat[:, 24 + 2 * h + q:25 + 2 * h + q],
                                 accum_out=stat[:, 48 + 2 * h + q:49 + 2 * h + q])
                        if q == 0:
                            t.step(ins)
                    t.out(ins, "probs")
                if n >= 2:
                    h = n - 2
                    t.wait("pt_psum")
                    if h >= 2:
                        act.wait_ge(S["pv_psum"], h - 1)
                    t.out(af(DIL_PT(h), bank[4 + h % 2][:, :], ACT.Copy), "pt_ready")
            t.out(af(stat[:, 0:24], stat[:, 48:72], ACT.Ln), "act_for_dve")
            t.wait("dve_for_act")
            t.out(af(stat[:, 0:24], stat[:, 0:24], ACT.Exp), "act_for_dve")
            gate("dil", 1, tiles(A, DIL_GATES, KT, T), 8)
            norm(X1, T, A, after="mix_out")
            ffn("ffn2", T)

            t.skip("h_ready", 3)
            for la in range(2):
                nq = 2 * T if la == 0 else T
                qtiles = nq // P
                p = f"l{la}_"
                t.wait("pe_for_act")
                t.out(af(lam[:, 0:2], bank[5][:, 0:2], ACT.Exp), "act_for_dve")
                if la == 0:
                    t.wait("x_ready")
                    norm(X2, 2 * T, G)
                else:
                    norm(X2, 2 * T, G, after="l0_ffn_down")
                shifts(H2, 2 * T, 0, la)
                qT, kT = tiles(A, 0, KT, 2 * T), tiles(A, 4096, KT, 2 * T)
                t.wait("pe_for_act")
                t.step(af(ROWS_X, bank[4][:, :], ACT.Identity, bias=pc(p + "gate_b")))
                t.step(af(ROWS_L, ROWS_X, ACT.Abs))
                t.step(af(ROWS_L, ROWS_L, ACT.Exp, scale=-1.0))
                t.out(af(ROWS_L, ROWS_L, ACT.Ln, bias=1.0), "act_for_dve")
                t.wait("dve_for_act")
                t.out(af(ROWS_EM, ROWS_EM, ACT.Exp), "act_for_dve")
                tiles_of(ST[p + "ml_q"], lambda c, j, i: af(qT[:, 4 * j + c, 0:nq], bank[c][:, 0:nq], ACT.Copy))
                tiles_of(ST[p + "ml_k"], lambda c, j, i: af(kT[:, 4 * j + c], bank[c][:, :], ACT.Copy, scale=1.0 / 16))
                v2 = A[:, 8192:8192 + 4 * 1028].rearrange("p (s h n) -> p s h n", s=4, h=4)
                tiles_of(ST[p + "ml_v"], lambda c, j, i: af(v2[:, c, 2 * j:2 * j + 2, 0:256],
                                                            bank[c][:, :].rearrange("p (h n) -> p h n", h=2), ACT.Copy))
                for h in range(4):
                    for d in range(2):
                        at = G[:, d * 2048:(d + 1) * 2048].rearrange("p (s q) -> p s q", s=4)
                        for s in range(4):
                            t.wait("ml_args")
                            t.out(af(at[:, s, 0:nq], at[:, s, 0:nq], ACT.Exp), "ml_exps")
                t.wait("dve_for_act")
                t.out(af(G[:, :], A[:, Y_ML:Y_ML + 4096], ACT.Square), "act_for_dve")
                t.wait("dve_for_act")
                t.out(af(stat[:, 16:32], stat[:, 0:16], ACT.Sqrt), "act_for_dve")
                o_gate = tiles(A, 4096, KT, 2 * T)
                tiles_of(ST[p + "ml_o"], lambda c, j, i: af(o_gate[:, 4 * j + c, 0:nq], bank[c][:, 0:nq], ACT.Sigmoid))
                merge(p + "ml", nq)
                act.wait_ge(S["dve_out"], ST[p + "da_q"].dve0)
                tiles_of(ST[p + "da_q"], lambda c, j, i: af(qT[:, 4 * j + c, 0:nq], bank[c][:, 0:nq], ACT.Copy))
                tiles_of(ST[p + "da_k"], lambda c, j, i: af(kT[:, 4 * j + c], bank[c][:, :], ACT.Copy))
                v3 = tiles(A, 8192, 4, D)
                tiles_of(ST[p + "da_v"], lambda c, j, i: af(v3[:, c, j * 512:(j + 1) * 512], bank[c][:, :], ACT.Copy))
                n_units = 8 * qtiles
                for n in range(n_units + 2):
                    if n < n_units:
                        w = 512 if n % qtiles < 2 else 256
                        t.wait("weights_out")
                        sc = stat[:, 4 * (n % 3):4 * (n % 3) + 4]
                        for m in range(2):
                            ins = af(DA_P(n, m)[:, 0:w], bank[4 * m + n % 2][:, 0:w], ACT.Exp, scale=0.125, bias=sc[:, m:m + 1],
                                     accum_out=sc[:, 2 + m:3 + m])
                            if m == 0:
                                t.step(ins)
                        t.out(ins, "probs_in")
                    if n >= 2:
                        k = n - 2
                        w = 512 if k % qtiles < 2 else 256
                        t.wait("pt_psum")
                        if k >= 2:
                            act.wait_ge(S["pv_psum"], PV_DA[la] + k - 1)
                        t.out(af(DA_PT(k)[:, 0:w], bank[2 + k % 2][:, 0:w], ACT.Copy), "pt_ready")
                t.wait("dve_for_act")
                t.out(af(G_SQ(la), A[:, 12288:16384], ACT.Square), "act_for_dve")
                t.wait("dve_for_act")
                t.out(af(stat[:, 64:96], stat[:, 32:64], ACT.Sqrt), "act_for_dve")
                merge(p + "da", nq)
                act.wait_ge(S["dve_out"], ST[p + "fn"].dve0)
                z = tiles(A, 4096, 4, D)
                tiles_of(ST[p + "fn"], lambda c, j, i: af(z[:, c, j * 512:(j + 1) * 512], bank[c][:, :], ACT.Copy))
                zf = A[:, 8192:16384].rearrange("p (k f s t) -> p k f s t", k=KT, f=2, s=2)
                n = 0
                for k in range(KT):
                    for s in range(nq // T):
                        t.wait("pe_for_act")
                        t.out(af(zf[:, k, :, s], bank[4 + n % 4][:, :].rearrange("p (f t) -> p f t", f=2), ACT.Copy), "act_for_pe")
                        n += 1
                yT = tiles(A, 0, KT, 2 * T)
                for k in range(KT):
                    t.wait("pe_for_act")
                    t.out(af(yT[:, k, 0:nq], bank[4 + k % 4][:, 0:nq], ACT.Copy), "act_for_pe")
                merge(p + "fn", nq)
                norm(X2, nq, A, after=p + "out")
                shifts(H2, nq, 1, la)
                ffn(p + "ffn", nq)
            norm(X2, T, G, after="l1_ffn_down")
            t.wait("dve_for_act")
            act.dma_start(out, H1).then_inc(S["out_done"], 16)
            act.wait_ge(S["out_done"], 16)

        @block.vector
        def _(dve):
            t = Tally(dve, S, "dve_steps")
            tt, ts, stt = nc.vector.tensor_tensor, nc.vector.tensor_scalar, nc.vector.scalar_tensor_tensor
            mul, add, sub = ALU.mult, ALU.add, ALU.subtract

            def tiles_of(st, body, cs=(0, 1, 2, 3)):
                def one(j, i):
                    for n, c in enumerate(cs):
                        dve.wait_ge(S["tile_done"], st.done0 + st.done * j + c + 1 + i * (SLOTS * st.done))
                        ins = body(n, j, i)
                        ins.then_inc(S["dve_out"], 1)
                        dve.wait_ge(S["dve_out"], st.dve0 + st.dve * j + n + 1 + i * (SLOTS * st.dve))
                over_slabs(dve, st.slabs, one, 0)

            def rstd(width):
                t.wait("sums_ready")
                t.out(ts(A[:, 4096:4096 + width], bank[4][:, 0:width], 1.0 / D, EPS, mul, add), "means_ready")
                t.wait("roots_ready")
                t.step(nc.vector.reciprocal(A[:, 4096:4096 + width], A[:, 4096 + width:4096 + 2 * width]))
                return A[:, 4096:4096 + width]

            def norm(x, h, width, gain):
                r = rstd(width)
                for k in range(KT):
                    ins = stt(h[:, k], x[:, k, 0:width], pc(gain, k), r, mul, mul)
                    if k < KT - 1:
                        t.step(ins)
                t.out(ins, "h_ready")

            def norm_mod(x, h, width, which, la):
                r = rstd(width)
                g4 = gs.rearrange("p (w k s) -> p w k s", w=2, k=KT)
                a3 = ada_all[:, la * 96:(la + 1) * 96].rearrange("p (k s) -> p k s", s=2)
                for k in range(KT):
                    for s in range(width // T):
                        cols = slice(s * T, (s + 1) * T)
                        t.out(stt(h[:, k, cols], x[:, k, cols], g4[:, which, k, s:s + 1], r[:, cols], mul, mul), "scaled")

            silu_count = [0]

            def ffn(name, x, width, gate=None):
                st = ST[name + "_up"]
                base = silu_count[0]
                tmp = tiles(A, FT * 2 * T, 2, width)

                def one(j, i):
                    for c in range(2):
                        dve.wait_ge(S["tile_done"], st.done0 + 4 * j + 2 + c + 1 + i * (4 * SLOTS))
                        dve.wait_ge(S["silu_ready"], base + 2 * j + c + 1 + i * (2 * SLOTS))
                        dst = A[:, bass.ds((2 * j + c) * width + i * (2 * SLOTS * width), width)]
                        tt(dst, tmp[:, c], bank[2 + c][:, 0:width], mul).then_inc(S["dve_out"], 1)
                over_slabs(dve, st.slabs, one, 0)
                silu_count[0] += 2 * st.slabs
                st = ST[name + "_down"]
                dve.wait_ge(S["dve_out"], st.dve0)
                for j in range(KT):
                    dve.wait_ge(S["tile_done"], st.done0 + j + 1)
                    src = bank[j % SLOTS]
                    if gate is None:
                        ins = stt(x[:, j, 0:width], src[:, 0:width], 0.5, x[:, j, 0:width], mul, add)
                    else:
                        for s in range(width // T):
                            cols = slice(s * T, (s + 1) * T)
                            ins = stt(x[:, j, cols], src[:, cols], gate(j, s), x[:, j, cols], mul, add)
                            if s < width // T - 1:
                                t.step(ins)
                    ins.then_inc(S["dve_out"], 1)
                    dve.wait_ge(S["dve_out"], st.dve0 + j + 1)

            def merge(name, g, width, first, gates=None):
                gates_in = tiles(A, 16384, 4, 2 * T)
                for half in range(2):
                    gt = gates[:, 4 * half:4 * half + 4] if gates is not None else gates_in
                    st = ST[f"{name}_proj{half}"]
                    dve.wait_ge(S["act_out"], st.act0)
                    for c in range(4):
                        dve.wait_ge(S["tile_done"], st.done0 + c + 1)
                        dst = g[:, 4 * half + c, 0:width]
                        if first:
                            tt(dst, gt[:, c, 0:width], bank[c][:, 0:width], mul).then_inc(S["dve_out"], 1)
                        else:
                            t.step(tt(gt[:, c, 0:width], gt[:, c, 0:width], bank[c][:, 0:width], mul))
                            tt(dst, dst, gt[:, c, 0:width], add).then_inc(S["dve_out"], 1)
                        dve.wait_ge(S["dve_out"], st.dve0 + c + 1)

            def say(name):
                t.out(nc.vector.memset(stat[0:1, 139:140], 0.0), name)

            dve.wait_ge(S["loads"], 64)
            norm(X1, H1, T, "ffn1_norm")
            ffn("ffn1", X1, T)
            norm(X1, H1, T, "mix_norm")
            shift = X[:, HALF:HALF + 4 * 257].rearrange("p (b n) -> p b n", b=4)
            t.out(nc.vector.memset(shift[:, :, 0:1], 0.0), "dve_for_act")
            n = 0
            dif = X[:, HALF + 1040:HALF + 1296]
            for name, base in (("r", sR), ("k", sK), ("v", sV), ("lora_in", sBH)):
                st = ST["rwkv_" + name]
                for q in range(st.slabs * st.act):
                    dve.wait_ge(S["act_out"], st.act0 + q + 1)
                    cur, prev = shift[:, n % 4, 1:257], shift[:, n % 4, 0:256]
                    rows = slice(0, P) if n < 26 else slice(0, 32)
                    t.step(tt(dif[rows], prev[rows], cur[rows], sub))
                    t.out(stt(slot3(base)[rows, q], dif[rows], pc("mu", n)[rows], cur[rows], mul, add), "shift_done")
                    n += 1
            L, R3, A3, B3, K3 = slot(sL), slot3(sR), slot3(sA), slot3(sB), slot3(sK)
            t.out(tt(A3, K3, bc(pc("k_k", 0, 8), 2, T), mul), "dve_for_act")
            t.wait("act_for_dve")
            t.step(ts(slot(sB), slot(sB), 1e-12, None, ALU.max))
            t.step(nc.vector.reciprocal(slot(sB), slot(sB)))
            t.step(tt(slot(sA), slot(sA), slot(sB), mul))
            dve.wait_ge(S["act_out"], ST["rwkv_lora_out"].act_end)
            t.step(ts(L, L, -math.exp(-0.5), None, mul))
            t.step(tt(slot(sB), slot(sA), slot(sAA), mul))
            t.step(ts(slot(sAA), slot(sAA), -1.0, None, add))
            t.step(tt(slot3(sAA), slot3(sAA), bc(pc("k_a", 0, 8), 2, T), mul))
            t.step(stt(slot(sK), slot(sAA), 1.0, slot(sK), add, mul))
            t.step(tt(slot(sKH), slot(sR), slot(sK), mul))
            t.out(tt(slot3(sKH), slot3(sKH), bc(pc("r_k", 0, 8), 2, T), mul), "dve_for_pe")
            t.wait("pe_for_dve")
            for b in range(4):
                c = slice(b * 512, (b + 1) * 512)
                t.step(tt(slot(sAA)[:, c], slot(sV)[:, c], bank[4 + b][:, :], mul))
            t.step(tt(slot3(sAA), slot3(sAA), bc(pc("ln_b", 0, 8), 2, T), add))
            lm = G[:, HALF:2 * HALF]
            t.step(nc.vector.tensor_copy(lm, L))
            for k in range(KT):
                t.step(nc.vector.tensor_tensor_scan(slot3(sL)[:, k], C[:, C1["reset"]:C1["reset"] + T],
                                                    lm[:, k * T:(k + 1) * T], 0.0, mul, add))
            t.out(tt(lm, L, lm, sub), "dve_for_act")
            t.wait("act_for_dve")
            t.step(tt(slot(sR), slot(sR), slot(sBH), mul))
            e_last = slot(sBH).rearrange("p (k c t) -> p k c t", k=KT, t=CHUNK)[:, :, :, CHUNK - 1]
            d3 = dec.rearrange("p (k c) -> p k c", k=KT)
            t.out(nc.vector.tensor_copy(d3, e_last), "dve_for_act")
            t.wait("act_for_dve")
            t.step(tt(slot(sK), slot(sK), slot(sKH), mul))
            t.out(tt(slot(sB), slot(sB), slot(sKH), mul), "dve_for_act")

            def by_chunk(k):
                return slot(k).rearrange("p (k t) -> p k t", t=CHUNK)

            dcol = bc(dec, 2, CHUNK)
            t.step(tt(by_chunk(sBH), by_chunk(sB), dcol, mul))
            t.step(tt(by_chunk(sKH), by_chunk(sK), dcol, mul))
            t.wait("act_for_dve")
            t.step(stt(slot(sA), slot(sA), -1.0, slot(sL), mul, mul))
            tok_v = X[:, HALF + 896 + 384:HALF + 1408]
            gram = H[:, HALF:HALF + 1024].rearrange("p (g a c) -> p g a c", g=2, a=4)
            gramf = H[:, HALF:HALF + 1024].rearrange("p (g a) -> p g a", g=2)
            ark = H[:, HALF + 1024:HALF + 1280].rearrange("p (g c) -> p g c", g=2)
            mtf = H[:, HALF + 1280:HALF + 1536]
            mt = mtf.rearrange("p (g c) -> p g c", g=2)
            q8 = H[:, HALF + 1536:HALF + 1792]
            p2 = G[:, HALF:HALF + 512]
            p4 = G[:, HALF + 512:HALF + 1024]
            wn = G[:, HALF + 1024:HALF + 1408]
            vb = C[:, C1_N:C1_N + 1024].rearrange("p (g h n) -> p g h n", g=2, h=8)
            ub = C[:, C1_N + 1024:C1_N + 2048].rearrange("p (g n) -> p g n", g=2)
            state = C[:, C1_N + 2048:C1_N + 2560]
            om = G[:, HALF + 1408:HALF + 1920]
            head = C[:, C1["head"]:C1["head"] + 512]
            t.step(nc.vector.memset(state, 0.0))
            t.step(nc.vector.memset(stat[0:1, 138:139], 0.0))
            say("chunk_free")
            say("rwkv_in_ready")
            copy = nc.vector.tensor_copy

            def ada_add(j, i):
                t.wait("ada_psum")
                dst = ada_all[:, bass.ds(8 * j + i * (8 * SLOTS), 8)].rearrange("p (c s) -> p c s", s=2)
                bias = par[:, bass.ds(PCOL["b_ada"][0] + 4 * j + i * (4 * SLOTS), 4)].unsqueeze(2).to_broadcast([P, 4, 2])
                t.out(tt(dst, bank[7][:, 0:8].rearrange("p (c s) -> p c s", s=2), bias, add), "ada_free")

            say("ada_free")
            with dve.Fori(0, NCH // 2) as i:
                t.loop(i, {"gram_psum": 2, "gram_ready": 2, "tok_ready": 2, "pow_psum": 14, "pow_ready": 14, "scan_psum": 2,
                           "u_ready": 2, "o_psum": 2, "chunk_free": 2, "dve_steps": 26, "ada_psum": 3, "ada_free": 3})
                for half in range(2):
                    t.wait("gram_psum")
                    for g in range(2):
                        t.step(tt(gramf[:, g], bank[g][:, :], C[:, C1["gram"]:C1["gram"] + 512], mul))
                    t.out(tt(mt, gram[:, :, 1], bc(ident, 1, 2), add), "gram_ready")
                    t.wait("pow_psum")
                    t.out(copy(p2, bank[5][:, :]), "pow_ready")
                    t.wait("tok_ready")
                    t.step(tt(vb[:, 0], bc(tok_v[:, 0:64], 1, 8), head.rearrange("p (h n) -> p h n", h=8), mul))
                    t.wait("pow_psum")
                    t.out(tt(mtf, mtf, bank[6][:, 0:256], add), "pow_ready")
                    for g in range(2):
                        t.step(tt(ark[:, g], bank[2 + g][:, 0:P], C[:, C1["ark"]:C1["ark"] + P], mul))
                    t.wait("pow_psum")
                    t.out(copy(p4, bank[5][:, :]), "pow_ready")
                    t.step(tt(vb[:, 1], bc(tok_v[:, 64:128], 1, 8), head.rearrange("p (h n) -> p h n", h=8), mul))
                    if half == 1:
                        ada_add(1, i)
                    t.wait("pow_psum")
                    t.out(tt(mtf, mtf, bank[6][:, 0:256], add), "pow_ready")
                    t.wait("pow_psum")
                    t.out(copy(q8, bank[4][:, 0:256]), "pow_ready")
                    t.wait("pow_psum")
                    t.out(tt(mtf, mtf, bank[6][:, 0:256], add), "pow_ready")
                    t.wait("pow_psum")
                    t.out(copy(wn, bank[5][:, 0:384]), "pow_ready")
                    if half == 0:
                        ada_add(0, i)
                    t.wait("scan_psum")
                    t.step(tt(ub[:, 0], bank[0][:, :], head, mul))
                    t.out(tt(ub[:, 1], bank[1][:, :], head, mul), "u_ready")
                    s3 = state.rearrange("p (h n) -> p h n", h=8)
                    t.wait("o_psum")
                    t.out(copy(stat[0:1, 138:139], stat[0:1, 139:140]), "chunk_free")
                    t.step(tt(s3, s3, dec.rearrange("p (k c) -> p k c", k=KT)[:, :, bass.ds(i * 2 + half, 1)].to_broadcast([P, 8, 64]), mul))
                    t.step(tt(state, state, bank[4][:, :], add))
                    for g in range(2):
                        t.step(tt(om, bank[2 + g][:, :], head, mul))
                        t.step(nc.vector.tensor_reduce(slot(sL)[:, bass.ds(i * (2 * P) + half * P + g * 64, 64)], om.rearrange("p (h n) -> p n h", h=8),
                                                       axis=AX.X, op=add))
                    if half == 1:
                        ada_add(2, i)
            t.end(NCH // 2)
            say("outputs_taken")
            o3 = slot(sL).rearrange("p (u n) -> p u n", n=64)
            sq = slot(sBH)
            sq3 = sq.rearrange("p (u n) -> p u n", n=64)
            mean, var, root = stat[:, 0:32], stat[:, 64:96], stat[:, 32:64]
            t.step(nc.vector.tensor_reduce(mean, o3, axis=AX.X, op=add))
            t.step(ts(mean, mean, 1.0 / 64, None, mul))
            t.step(tt(o3, o3, bc(mean, 2, 64), sub))
            t.step(tt(sq, slot(sL), slot(sL), mul))
            t.step(nc.vector.tensor_reduce(var, sq3, axis=AX.X, op=add))
            t.out(ts(var, var, 1.0 / 64, GN_EPS, mul, add), "dve_for_act")
            t.wait("act_for_dve")
            t.step(nc.vector.reciprocal(root, root))
            t.out(tt(o3, o3, bc(root, 2, 64), mul), "dve_for_pe")
            t.wait("pe_for_dve")
            for b in range(4):
                for c in range(4):
                    t.step(tt(slot3(sR)[:, :, (4 * b + c) * CHUNK:(4 * b + c + 1) * CHUNK],
                              bank[4 + b][:, c * P:(c + 1) * P].rearrange("p (k t) -> p k t", k=KT),
                              bc(pc("ln_w", 0, 8), 2, CHUNK), mul))
            t.step(tt(slot(sR), slot(sR), slot(sAA), add))
            t.out(tt(slot(sR), slot(sR), slot(sG), mul), "dve_for_pe")
            merge("rwkv", G1, T, True, gates=G1)

            for half in range(2):
                t.wait("pe_for_dve")
                for b in range(3):
                    dst = A[:, 15360 + b * 512:15360 + (b + 1) * 512]
                    if half == 0:
                        ins = ts(dst, bank[4 + b][:, :], 1.0, 64 * EPS, mul, add)
                    else:
                        ins = ts(dst, bank[4 + b][:, :], 1.0 / 64, EPS, mul, add)
                    if b < 2:
                        t.step(ins)
                t.out(ins, "dve_for_act")
                t.wait("act_for_dve")
                rs = A[:, 15360:16896]
                t.step(nc.vector.reciprocal(rs, rs))
                qkf = A[:, 3072 + half * 1536:3072 + (half + 1) * 1536]
                t.out(stt(qkf, qkf, pc("q_norm" if half == 0 else "k_norm"), rs, mul, mul), "dve_for_pe")
            y1 = tiles(A, 13824, 2, 768)

            def dil_in(h):
                pr = A[:, 10752 + (h % 3) * 512:10752 + (h % 3) * 512 + 512]
                t.wait("scores")
                if h >= 3:
                    t.wait("pt_ready")
                t.out(tt(pr, bank[h % 2][:, :], C[:, C1["dil"] + (h // 4) * 512:C1["dil"] + (h // 4) * 512 + 512], add), "probs_in")
                t.step(nc.vector.tensor_reduce(stat[:, 72 + 2 * h:74 + 2 * h], pr.rearrange("p (q k) -> p q k", q=2), axis=AX.X, op=ALU.max))
                t.out(ts(stat[:, 24 + 2 * h:26 + 2 * h], stat[:, 72 + 2 * h:74 + 2 * h], -1.0, None, mul), "weights_out")

            for h in range(15):
                if h < 12:
                    dil_in(h)
                if h >= 3:
                    k = h - 3
                    t.wait("pv_psum")
                    t.out(copy(y1[:, :, k * 64:(k + 1) * 64], bank[6 + k % 2][:, 0:128].rearrange("p (q n) -> p q n", q=2)), "pv_out")
            t.wait("act_for_dve")
            lse, mx = stat[:, 0:24], stat[:, 96:104]
            t.step(tt(lse, lse, stat[:, 72:96], add))
            t.step(nc.vector.tensor_reduce(mx, lse.rearrange("p (g u) -> p u g", g=3), axis=AX.X, op=ALU.max))
            t.out(tt(lse.rearrange("p (g u) -> p g u", g=3), lse.rearrange("p (g u) -> p g u", g=3), bc(mx, 1, 3), sub), "dve_for_act")
            t.wait("act_for_dve")
            t.step(nc.vector.tensor_reduce(mx, lse.rearrange("p (g u) -> p u g", g=3), axis=AX.X, op=add))
            t.step(tt(stat[:, 48:72].rearrange("p (g u) -> p g u", g=3), stat[:, 48:72].rearrange("p (g u) -> p g u", g=3), bc(mx, 1, 3), mul))
            t.step(nc.vector.reciprocal(stat[:, 48:72], stat[:, 48:72]))
            t.step(tt(stat[:, 48:72], stat[:, 48:72], lse, mul))
            for q in range(2):
                yq = y1[:, q].rearrange("p (h n) -> p h n", h=12)
                wq = bc(stat[:, 48:72].rearrange("p (h q) -> p h q", q=2)[:, :, q], 2, 64)
                ins = tt(yq, yq, wq, mul)
                if q == 0:
                    t.step(ins)
            t.out(ins, "dve_for_pe")
            t.wait("pe_for_dve")
            yT = tiles(A, 0, 6, T)
            for q in range(2):
                for b in range(2):
                    ins = copy(yT[:, 3 * b:3 * b + 3, q * P:(q + 1) * P], bank[4 + 2 * q + b][:, 0:384].rearrange("p (k t) -> p k t", k=3))
                    if not (q == 1 and b == 1):
                        t.step(ins)
            t.out(ins, "dve_for_pe")
            say("block2_free")
            merge("dil", G1, T, False, gates=tiles(A, DIL_GATES, KT, T))
            say("dve_for_pe")
            tiles_of(ST["mix_out"], lambda c, j, i: tt(X1[:, 4 * j + c], X1[:, 4 * j + c], bank[c][:, 0:T], add))
            norm(X1, H1, T, "ffn2_norm")
            ffn("ffn2", X1, T)
            t.step(copy(G1, X1))
            t.step(copy(X2[:, :, 0:T], G1))
            dve.wait_ge(S["consts2"], 32)
            t.step(copy(X2[:, :, T:], tiles(G, HALF, KT, T)))

            for la in range(2):
                nq = 2 * T if la == 0 else T
                qtiles = nq // P
                p = f"l{la}_"
                a3 = ada_all[:, la * 96:(la + 1) * 96].rearrange("p (k s) -> p k s", s=2)
                g4 = gs.rearrange("p (w k s) -> p w k s", w=2, k=KT)
                for w in range(2):
                    t.step(stt(g4[:, w], a3[:, 24 * w + 8:24 * w + 16], 1.0, bc(pc(p + "norm_g", 8 * w, 8), 2, 2), add, mul))
                lq = pc(p + "lam", 0, 4).rearrange("p (a b) -> p a b", b=2)
                t.out(tt(lam_in[0:64, :], lq[0:64, :, 0], lq[0:64, :, 1], mul), "dve_for_pe")
                t.wait("act_for_dve")
                t.step(tt(lam[:, 2:3], lam[:, 1:2], lam[:, 0:1], sub))
                t.step(ts(lam[:, 2:3], lam[:, 2:3], -LAM_INIT[la], None, add))
                if la == 0:
                    say("x_ready")
                norm_mod(X2, H2, 2 * T, 0, la)
                gw = tiles(G, 0, KT, P)
                t.step(nc.vector.memset(G[:, 0:KT * P], 0.0))
                gsrc = pc(p + "gate_w", 0, 128).rearrange("p (k n) -> p k n", k=KT)
                for n in range(4):
                    t.step(copy(gw[:, :, 32 * n:32 * n + 4], gsrc[:, :, 4 * n:4 * n + 4]))
                v2 = A[:, 8192:8192 + 4 * 1028].rearrange("p (s n) -> p s n", n=257)
                t.step(nc.vector.memset(A[:, ROWS0:ROWS0 + 7 * 512], 0.0))
                t.step(nc.vector.memset(ROWS_1, 1.0))
                t.step(nc.vector.memset(A[:, 8192:8192 + 16 * 257].rearrange("p (u n) -> p u n", n=257)[:, :, 256:257], 1.0))
                say("dve_for_pe")
                t.wait("act_for_dve")
                t.step(stt(ROWS_L, ROWS_X, 0.0, ROWS_L, ALU.min, sub))
                scan = nc.vector.tensor_tensor_scan
                for d in range(2):
                    fr, ir = slice(64 * d + 32, 64 * d + 36), slice(64 * d, 64 * d + 4)

                    def seq(ap, s, d=d):
                        lo = T * s
                        cols = ap[:, lo:lo + T]
                        return cols if d == 0 else cols[:, ::-1]

                    end = (2 * T - 1) if d == 0 else T
                    t.step(scan(seq(ROWS_B[ir], 1), seq(ROWS_1[fr], 1), seq(ROWS_L[fr], 1), 0.0, mul, add))
                    t.step(copy(ROWS_EM[fr, 0:1], ROWS_B[ir, end:end + 1]))
                    t.step(scan(seq(ROWS_B[ir], 0), seq(ROWS_1[fr], 0), seq(ROWS_L[fr], 0), ROWS_EM[fr, 0:1], mul, add))
                    t.step(tt(ROWS_GI[ir], ROWS_X[ir], ROWS_B[ir], sub))
                    t.step(scan(seq(ROWS_NCM[ir], 1), seq(ROWS_GI[ir], 1), seq(ROWS_GI[ir], 1), 0.0, ALU.max, ALU.max))
                    t.step(scan(seq(ROWS_NCM[ir], 0), seq(ROWS_GI[ir], 0), seq(ROWS_GI[ir], 0), ROWS_NCM[ir, end:end + 1], ALU.max, ALU.max))
                    t.step(ts(ROWS_NCM[ir], ROWS_NCM[ir], -1.0, None, mul))
                    t.step(tt(ROWS_EM[ir], ROWS_NCM[ir], ROWS_B[ir], sub))
                say("dve_for_act")
                t.wait("act_for_dve")
                say("dve_for_pe")
                t.wait("pe_for_dve")
                for n in range(2):
                    for d in range(2):
                        ins = copy(ML_COLS[:, n, :, d], bank[5 + n][:, :].rearrange("p (c q) -> p c q", c=4)[:, :, 64 * d:64 * d + 4])
                        if not (n == 1 and d == 1):
                            t.step(ins)
                t.out(ins, "dve_for_pe")
                y2 = tiles(A, Y_ML, 4, D)
                if nq < 2 * T:
                    t.step(nc.vector.memset(A[:, Y_ML + 2048:Y_ML + 4096], 0.0))

                def num_out(h, d, q):
                    t.wait("pv_psum")
                    b = bank[2 + q % 2]
                    den = stat[:, 100:101]
                    t.step(ts(den, b[:, 256:257], -1.0, None, mul))
                    t.step(stt(den, b[:, 256:257], ML_COLS[:, 1, q, d, h:h + 1], den, ALU.max, ALU.max))
                    t.step(nc.vector.reciprocal(den, den))
                    dst = y2[:, q, h * 256:(h + 1) * 256]
                    if d == 0:
                        t.out(ts(dst, b[:, 0:256], den, None, mul), "pv_out")
                    else:
                        t.out(stt(dst, b[:, 0:256], den, dst, mul, add), "pv_out")

                def ml_arg(h, d, s):
                    at = G[:, d * 2048 + s * 512:d * 2048 + s * 512 + nq]
                    m0 = C2["ml"] + 896 * d + 384 - s * P
                    t.out(stt(at, bank[d][:, 0:nq], ML_COLS[:, 0, s, d, h:h + 1], C[:, m0:m0 + nq], add, ALU.min), "ml_args")

                blocks = [(h, d) for h in range(4) for d in range(2)]
                for n, (h, d) in enumerate(blocks):
                    t.wait("scores")
                    ml_arg(h, d, 0)
                    ml_arg(h, d, 1)
                    for s in range(4):
                        if s < 2:
                            ml_arg(h, d, s + 2)
                        t.wait("ml_exps")
                        if d == 0:
                            t.wait("scores")
                        at = G[:, d * 2048 + s * 512:d * 2048 + s * 512 + nq]
                        t.out(tt(at, at, bank[4 + s][:, 0:nq], mul), "ml_weights")
                        if n and s < qtiles:
                            num_out(*blocks[n - 1], s)
                for q in range(qtiles):
                    num_out(3, 1, q)
                say("dve_for_act")
                t.wait("act_for_dve")
                ms, rt = stat[:, 0:16], stat[:, 16:32]
                t.step(nc.vector.tensor_reduce(ms, G[:, :].rearrange("p (u n) -> p u n", n=256), axis=AX.X, op=add))
                t.out(ts(ms, ms, 1.0 / 256, EPS, mul, add), "dve_for_act")
                t.wait("act_for_dve")
                t.step(nc.vector.reciprocal(rt, rt))
                yv = A[:, Y_ML:Y_ML + 4096].rearrange("p (u n) -> p u n", n=256)
                t.out(tt(yv, yv, bc(rt, 2, 256), mul), "dve_for_pe")
                bT = tiles(A, 0, KT, 2 * T)

                def outputs_back(gain):
                    for k in range(KT):
                        t.wait("pe_for_dve")
                        t.out(ts(bT[:, k, 0:nq], bank[4 + k % 4][:, 0:nq], gain(k), None, mul), "dve_for_pe")

                outputs_back(lambda k: pc(p + "ml_g", k))
                dve.wait_ge(S["act_out"], ST[p + "ml_o"].act_end)
                o_gate = tiles(A, 4096, KT, 2 * T)
                t.out(tt(bT[:, :, 0:nq], bT[:, :, 0:nq], o_gate[:, :, 0:nq], mul), "dve_for_pe")
                merge(p + "ml", G2, nq, True)
                qT, kT = tiles(A, 0, KT, 2 * T), tiles(A, 4096, KT, 2 * T)
                for n in range(8):
                    if n % 4 == 0:
                        dve.wait_ge(S["act_out"], ST[p + ("da_q", "da_k")[n // 4]].act_end)
                    x2 = (qT, kT)[n // 4][:, 2 * (n % 4):2 * (n % 4) + 2, 0:T]
                    t.wait("pe_for_dve")
                    tmp = tiles(A, 16384, 2, T)
                    t.step(tt(tmp, bank[4 + n % 4][:, :].rearrange("p (a t) -> p a t", a=2), bc(C[:, C2["sin"]:C2["sin"] + T], 1, 2), mul))
                    t.step(tt(x2, x2, bc(C[:, C2["cos"]:C2["cos"] + T], 1, 2), mul))
                    t.out(tt(x2, x2, tmp, add), "dve_for_pe")
                units = [(h, q) for h in range(8) for q in range(qtiles)]
                y3 = tiles(A, 12288, 4, D)
                if nq < 2 * T:
                    t.step(nc.vector.memset(A[:, 12288 + 2048:12288 + 4096], 0.0))

                def da_in(n):
                    w = 512 if units[n][1] < 2 else 256
                    sc = stat[:, 4 * (n % 3):4 * (n % 3) + 4]
                    t.wait("scores")
                    for m in range(2):
                        t.step(nc.vector.tensor_reduce(sc[:, m:m + 1], bank[4 * m + n % 2][:, 0:w], axis=AX.X, op=ALU.max))
                    t.out(ts(sc[:, 0:2], sc[:, 0:2], -0.125, None, mul), "weights_out")

                def da_mid(n):
                    w = 512 if units[n][1] < 2 else 256
                    sc = stat[:, 4 * (n % 3):4 * (n % 3) + 4]
                    p0, p1 = DA_P(n, 0)[:, 0:w], DA_P(n, 1)[:, 0:w]
                    t.wait("probs_in")
                    t.step(nc.vector.reciprocal(sc[:, 2:4], sc[:, 2:4]))
                    t.step(ts(p1, p1, sc[:, 3:4], lam[:, 2:3], mul, mul))
                    t.out(stt(p0, p0, sc[:, 2:3], p1, mul, add), "probs")

                for n in range(len(units) + 3):
                    if n < len(units):
                        da_in(n)
                    if 1 <= n < len(units) + 1:
                        da_mid(n - 1)
                    if n >= 3:
                        h, q = units[n - 3]
                        t.wait("pv_psum")
                        t.out(copy(y3[:, q, h * P:(h + 1) * P], bank[6 + (n - 3) % 2][:, 0:P]), "pv_out")
                say("dve_for_act")
                t.wait("act_for_dve")
                ms, rt = stat[:, 32:64], stat[:, 64:96]
                t.step(nc.vector.tensor_reduce(ms, A[:, 0:4096].rearrange("p (u n) -> p u n", n=P), axis=AX.X, op=add))
                t.out(ts(ms, ms, 1.0 / P, EPS, mul, add), "dve_for_act")
                t.wait("act_for_dve")
                t.step(nc.vector.reciprocal(rt, rt))
                t.step(ts(rt, rt, 1.0 - LAM_INIT[la], None, mul))
                yv = A[:, 12288:16384].rearrange("p (u n) -> p u n", n=P)
                t.out(tt(yv, yv, bc(rt, 2, P), mul), "dve_for_pe")
                outputs_back(lambda k: pc(p + "da_g", k))
                say("dve_for_pe")
                merge(p + "da", G2, nq, False)
                say("dve_for_pe")
                merge(p + "fn", G2, nq, False)
                say("dve_for_pe")
                for j in range(2):
                    st = ST[p + "out"]
                    for c in range(4):
                        dve.wait_ge(S["tile_done"], st.done0 + 4 * j + c + 1)
                        k = 4 * j + c
                        for s in range(nq // T):
                            cols = slice(s * T, (s + 1) * T)
                            ins = stt(X2[:, k, cols], bank[c][:, cols], a3[:, 16 + k, s:s + 1], X2[:, k, cols], mul, add)
                            if s < nq // T - 1:
                                t.step(ins)
                        ins.then_inc(S["dve_out"], 1)
                        dve.wait_ge(S["dve_out"], st.dve0 + 4 * j + c + 1)
                norm_mod(X2, H2, nq, 1, la)
                ffn(p + "ffn", X2, nq, gate=lambda k, s: a3[:, 40 + k, s:s + 1])
            t.skip("h_ready", 6 * KT + KT)
            norm(X2, H1, T, "final_g")
            say("dve_for_act")



def constants():
    import numpy as np
    f = np.float32
    common = np.zeros((P, C_COMMON), f)
    common[:, 0:128] = np.eye(P)
    common[:, 128:256] = 1.0
    idx = np.arange(P)
    common[:, 256:384] = (idx[:, None] // 64 == idx[None, :] // 64)
    c1 = np.zeros((P, C1_N), f)
    h, tk = idx // CHUNK, idx % CHUNK
    same = h[:, None] == h[None, :]
    r, c = tk[:, None], tk[None, :]
    c1[:, 0:128] = same & (r <= c)
    c1[:, 128:256] = same & (r < c)
    c1[:, 256:384] = same & (c < r)
    c1[:, 384:512] = same & (c < r)
    c1[:, 512:640] = same & (r <= c)
    c1[:, 640:1152] = (h[:, None] == (np.arange(512) // 64)[None, :])
    c1[:, 1152:1408] = (np.arange(T) % CHUNK != 0)[None, :]
    for g, (win, dil) in enumerate(((128, 1), (512, 4), (2048, 16))):
        span = win // dil
        for q in range(2):
            d = (q * P + idx)[:, None] - np.arange(T)[None, :]
            ok = (d >= 0) & (d % dil == 0) & (d // dil <= span)
            c1[:, 1408 + g * 512 + q * T:1408 + g * 512 + (q + 1) * T] = np.where(ok, 0.0, -1e30)
    c2 = np.zeros((P, C2_N), f)
    r0, c0 = idx[:, None], idx[None, :]
    t0, d0 = C2["dft_t"], C2["dft_c"]
    for d in range(2):
        ok = (r0 <= c0) if d == 0 else (r0 >= c0)
        c2[:, d * 896 + 384:d * 896 + 512] = np.where(ok, 0.0, -1e30)
    n = np.arange(T)
    ang = 2 * np.pi * ((n[:, None] * n[None, :]) % T) / T
    cos, sin = np.cos(ang) / 16.0, np.sin(ang) / 16.0
    for k in range(2):
        c2[:, t0 + k * 512:t0 + k * 512 + 256] = cos[k * P:(k + 1) * P]
        c2[:, t0 + k * 512 + 256:t0 + (k + 1) * 512] = sin[k * P:(k + 1) * P]
        c2[:, d0 + k * 256:d0 + (k + 1) * 256] = cos[k * P:(k + 1) * P]
        c2[:, d0 + 512 + k * 256:d0 + 512 + (k + 1) * 256] = -sin[k * P:(k + 1) * P]
    nf = 16
    inv = (f(10000.0) ** (-np.arange(nf, dtype=f) / f(nf))).astype(f)
    rr = np.repeat(np.arange(T // 64, dtype=f), 64)
    cc = np.tile(np.arange(64, dtype=f), T // 64)
    a = np.concatenate([rr[:, None] * inv, cc[:, None] * inv], axis=-1)
    c2[:, C2["cos"]:C2["cos"] + T] = np.cos(a).T[idx % 32]
    c2[:, C2["sin"]:C2["sin"] + T] = np.sin(a).T[idx % 32]
    for m in range(P):
        if m % 64 < 32:
            c2[m + 32, C2["perm"] + m] = -1.0
        else:
            c2[m - 32, C2["perm"] + m] = 1.0
    return common, c1, c2


def layout(inputs):
    import numpy as np
    f = np.float32
    wide, down = [], []

    def cols(w, n0, n1, kt=None):
        k = w.shape[0] // P
        n = (n1 - n0) // P
        return w[:, n0:n1].reshape(k, P, n, P).transpose(1, 2, 0, 3)

    def put(a):
        a = a.reshape(P, -1)
        if a.shape[1] < SLAB:
            a = np.concatenate([a, np.zeros((P, SLAB - a.shape[1]), f)], axis=1)
        wide.append(a)

    def stationary(w):
        for n0 in range(0, w.shape[1], 512):
            put(cols(w, n0, n0 + 512))

    def moving(w, width):
        for n0 in range(0, w.shape[1], width):
            put(w[:, n0:n0 + width].reshape(KT, P, width).transpose(1, 0, 2))

    def ffn(w_in, w_out):
        for j in range(FT // 2):
            put(np.concatenate([cols(w_in, 256 * j, 256 * (j + 1)), cols(w_in, FF + 256 * j, FF + 256 * (j + 1))], axis=1))
        for n in range(KT):
            down.append(cols(w_out, n * P, (n + 1) * P).reshape(P, DOWN))

    def merge(gate, proj):
        for half in range(2):
            put(cols(gate, 512 * half, 512 * (half + 1)))
            put(cols(proj, 512 * half, 512 * (half + 1)))

    def halves(m):
        for half in range(2):
            put(cols(m, 512 * half, 512 * (half + 1)))

    g = {k: np.asarray(v) for k, v in inputs.items()}
    ffn(g["ffn1_w_in"][0], g["ffn1_w_out"][0])
    w = g["w_in"][0]
    for n in range(3):
        stationary(w[:, n * D:(n + 1) * D])
    put(cols(np.concatenate([w[:, 3072:3360], np.zeros((D, 96), f)], axis=1), 0, 384))
    wa2 = np.concatenate([g["rwkv_w2"][0], g["rwkv_a2"][0]], axis=0)
    g2 = g["rwkv_g2"][0]
    put(np.concatenate([wa2, g2[0:P], np.concatenate([g2[P:], np.zeros((96, D), f)], axis=0)], axis=1))
    gate0 = 3360 + 3 * 768
    halves(w[:, gate0:gate0 + D])
    for la in range(2):
        moving(g["w_ada_2"][la], 512)
    stationary(w[:, 3360:3360 + 1536])
    moving(w[:, 3360 + 1536:gate0], 384)
    halves(g["w_proj_rwkv"][0])
    halves(w[:, gate0 + D:gate0 + 2 * D])
    halves(g["w_proj_attn"][0])
    stationary(g["w_out"][0])
    ffn(g["ffn2_w_in"][0], g["ffn2_w_out"][0])
    for la in range(2):
        w = g["w_in_2"][la]
        o = 4112
        stationary(w[:, 0:D])
        stationary(w[:, D:2 * D])
        moving(w[:, 2 * D:3 * D], 512)
        stationary(w[:, 3 * D:4 * D])
        gates = w[:, o + 4 * D:o + 7 * D]
        merge(gates[:, 0:D], g["w_br_ml_2"][la])
        stationary(w[:, o:o + D])
        stationary(w[:, o + D:o + 2 * D])
        moving(w[:, o + 2 * D:o + 3 * D], 512)
        merge(gates[:, D:2 * D], g["w_br_da_2"][la])
        moving(w[:, o + 3 * D:o + 4 * D], 512)
        merge(gates[:, 2 * D:3 * D], g["w_br_fn_2"][la])
        stationary(g["w_out_2"][la])
        ffn(g["w_ffn_in_2"][la], g["w_ffn_out_2"][la])

    par = np.zeros((P, NPAR), f)

    def column(name, v):
        n0, n = PCOL[name]
        v = v.reshape(-1)
        if v.size % P:
            v = np.concatenate([v, np.zeros(P - v.size % P, f)])
        par[:, n0:n0 + n] = v.reshape(-1, P).T

    for name, key in (("ffn1_norm", "ffn1_norm"), ("mix_norm", "mix_norm"), ("b_gate", "b_gate"), ("mu", "rwkv_mu"), ("w0", "rwkv_w0"),
                      ("a0", "rwkv_a0"), ("k_k", "rwkv_k_k"), ("k_a", "rwkv_k_a"), ("r_k", "rwkv_r_k"), ("ln_w", "rwkv_ln_w"),
                      ("ln_b", "rwkv_ln_b"), ("ffn2_norm", "ffn2_norm"), ("final_g", "final_g_2")):
        column(name, g[key])
    column("b_ada", g["b_ada_2"])
    column("q_norm", np.concatenate([g["attn_q_norm"][0]] * 2))
    column("k_norm", np.concatenate([g["attn_k_norm"][0]] * 2))
    n0 = PCOL["c"][0]
    par[:, n0:n0 + 16:2] = g["c_2"][0].reshape(KT, P).T
    par[:, n0 + 1:n0 + 16:2] = g["c_ctx_2"].reshape(KT, P).T
    for la in range(2):
        column(f"l{la}_norm_g", g["norm_g_2"][la])
        column(f"l{la}_ml_g", g["ml_head_g_2"][la])
        column(f"l{la}_da_g", g["da_head_g_2"][la])
        n0 = PCOL[f"l{la}_gate_b"][0]
        for n in range(4):
            par[32 * n:32 * n + 4, n0] = g["ml_gate_b_2"][la][4 * n:4 * n + 4]
        n0 = PCOL[f"l{la}_lam"][0]
        par[0:64, n0:n0 + 4] = g["da_lam_2"][la].T
        n0 = PCOL[f"l{la}_gate_w"][0]
        par[:, n0:n0 + 128] = g["w_in_2"][la][:, 4096:4112].reshape(KT, P, 16).transpose(1, 0, 2).reshape(P, 128)
    assert len(wide) == N_WIDE and len(down) == N_DOWN, (len(wide), N_WIDE, len(down), N_DOWN)
    xT = g["x"][0].T.reshape(KT, P, T).transpose(1, 0, 2)
    cT = g["ctx_2"][0].T.reshape(KT, P, T).transpose(1, 0, 2)
    return xT, cT, np.stack(wide), np.stack(down), par


def kernel(**inputs):
    import numpy as _np
    import concourse.bacc as _bacc
    from concourse import mybir as _mybir
    from concourse.bass_utils import run_bass_kernel_spmd as _run

    nc = _bacc.Bacc("TRN2", target_bir_lowering=False, num_devices=1)
    names = ["x_T", "ctx_T", "wide_slabs", "down_slabs", "params", "common_consts", "first_consts", "second_consts"]
    data = list(layout(inputs)) + list(constants())
    arrays, args = {}, []
    for name, a in zip(names, data):
        a = _np.ascontiguousarray(a)
        arrays[name + "_dram"] = a
        args.append(nc.dram_tensor(name + "_dram", a.shape, _mybir.dt.from_np(a.dtype), kind="ExternalInput").ap())
    args.append(nc.dram_tensor("out_dram", (P, KT, T), _mybir.dt.float32, kind="ExternalOutput").ap())
    program(nc, *args)
    r = _run(nc, [arrays], core_ids=[0])
    y = r.results[0]["out_dram"]
    return y.transpose(2, 1, 0).reshape(1, T, D)
```
